# Optimizing a Trainium2 kernel written in Bass

```python
import math
import jax, jax.numpy as jnp
from jax import lax
import numpy as np

D_MODEL = 1024
BATCH = 1
SEQ = 1024
DEPTH = 1

D_MIX = D_MODEL
RWKV_HEADS = 8
RWKV_HEAD_DIM = 64
D_RWKV = RWKV_HEADS * RWKV_HEAD_DIM
DECAY_RANK = 64
ICLR_RANK = 64
GATE_RANK = 128
D_SHIFT = 3 * D_RWKV + DECAY_RANK + ICLR_RANK + GATE_RANK
S5_GROUP_CH = 16
D_S5 = D_MIX - D_RWKV
S5_GROUPS = D_S5 // S5_GROUP_CH
S5_STATE = 64
D_IN = D_SHIFT + D_S5
N_MEM = 256
XATTN_HEADS = 4
XATTN_HEAD_DIM = D_MODEL // XATTN_HEADS
N_EXPERT_GROUPS = 4
EXPERTS_PER_GROUP = 8
N_EXPERTS = N_EXPERT_GROUPS * EXPERTS_PER_GROUP
EXPERT_TOP_K = 2
D_EXPERT = 512
MOE_BLOCK = 128
RMS_EPS = 1e-6
GN_EPS = 64e-5
L2_EPS = 1e-12

kernel_name = "hybrid_rwkv7_s5_memxattn_hiermoe"

def rmsnorm(x, g):
    xf = x.astype(jnp.float32)
    y = xf * lax.rsqrt(jnp.mean(xf * xf, axis=-1, keepdims=True) + RMS_EPS)
    return (y * g.astype(jnp.float32)).astype(x.dtype)

def token_shift(z, mu):
    prev = jnp.pad(z, ((0, 0), (1, 0), (0, 0)))[:, :-1]
    return z + (prev - z) * mu

def rwkv7_group(p, w0, w_decay_up, a0, w_iclr_up, w_gate_up, k_k, k_a, r_k, ln_w, ln_b):
    bsz, slen = p.shape[0], p.shape[1]
    cuts = [D_RWKV, 2 * D_RWKV, 3 * D_RWKV, 3 * D_RWKV + DECAY_RANK, 3 * D_RWKV + DECAY_RANK + ICLR_RANK]
    r, k, v, dw, da, dg = jnp.split(p, cuts, axis=-1)
    log_w = -jax.nn.softplus(-(w0 + jnp.tanh(dw) @ w_decay_up)) - 0.5
    decay = jnp.exp(-jnp.exp(log_w))
    a = jax.nn.sigmoid(a0 + da @ w_iclr_up)
    g = jax.nn.sigmoid(dg) @ w_gate_up
    hd = lambda t: t.reshape(bsz, slen, RWKV_HEADS, RWKV_HEAD_DIM)
    kk = hd(k * k_k)
    kk = kk / jnp.maximum(jnp.sqrt(jnp.sum(kk * kk, axis=-1, keepdims=True)), L2_EPS)
    k = k * (1.0 + (a - 1.0) * k_a)
    r, k, v, decay, a = hd(r), hd(k), hd(v), hd(decay), hd(a)

    def step(state, inp):
        r_t, w_t, k_t, v_t, kk_t, a_t = inp
        sa = jnp.einsum('bhvk,bhk->bhv', state, -kk_t)
        state = (state * w_t[:, :, None, :]
                 + sa[..., None] * (kk_t * a_t)[:, :, None, :]
                 + v_t[..., None] * k_t[:, :, None, :])
        return state, jnp.einsum('bhvk,bhk->bhv', state, r_t)

    xs = tuple(jnp.moveaxis(t, 1, 0) for t in (r, decay, k, v, kk, a))
    state0 = jnp.zeros((bsz, RWKV_HEADS, RWKV_HEAD_DIM, RWKV_HEAD_DIM), jnp.float32)
    _, y = lax.scan(step, state0, xs)
    y = jnp.moveaxis(y, 0, 1)
    mu = jnp.mean(y, axis=-1, keepdims=True)
    var = jnp.mean(jnp.square(y - mu), axis=-1, keepdims=True)
    y = (y - mu) * lax.rsqrt(var + GN_EPS)
    y = y * ln_w.reshape(RWKV_HEADS, RWKV_HEAD_DIM) + ln_b.reshape(RWKV_HEADS, RWKV_HEAD_DIM)
    y = y + jnp.sum(r * k * r_k, axis=-1, keepdims=True) * v
    return y.reshape(bsz, slen, D_RWKV) * g

def _ssm_combine(e1, e2):
    a1, b1 = e1
    a2, b2 = e2
    return a2 * a1, a2 * b1 + b2

def s5_group(u, lam_re, lam_im, log_dt, b_re, b_im, c_re, c_im, d_skip, w_glu, b_glu):
    bsz, slen = u.shape[0], u.shape[1]
    ug = u.reshape(bsz, slen, S5_GROUPS, S5_GROUP_CH)
    lam = lax.complex(lam_re.astype(jnp.float32), lam_im.astype(jnp.float32))
    dt = jnp.exp(log_dt.astype(jnp.float32))[:, None]
    lam_bar = jnp.exp(lam * dt)
    b = lax.complex(b_re.astype(jnp.float32), b_im.astype(jnp.float32))
    b_bar = ((lam_bar - 1.0) / lam)[..., None] * b
    bu = lax.complex(jnp.einsum('bsgh,gnh->bsgn', ug, jnp.real(b_bar)),
                     jnp.einsum('bsgh,gnh->bsgn', ug, jnp.imag(b_bar)))
    a_elems = jnp.broadcast_to(lam_bar, (1, slen, S5_GROUPS, S5_STATE))
    _, states = lax.associative_scan(_ssm_combine, (a_elems, bu), axis=1)
    y = (jnp.einsum('bsgn,ghn->bsgh', jnp.real(states), c_re)
         - jnp.einsum('bsgn,ghn->bsgh', jnp.imag(states), c_im)
         + d_skip * ug)
    z = jax.nn.gelu(y.reshape(bsz, slen, D_S5))
    return z * jax.nn.sigmoid(z @ w_glu + b_glu)

def memory_cross_attention(h, mem_n, w_q, w_k, w_v, w_o):
    bsz, slen = h.shape[0], h.shape[1]
    q = (h @ w_q).reshape(bsz, slen, XATTN_HEADS, XATTN_HEAD_DIM)
    k = (mem_n @ w_k).reshape(bsz, N_MEM, XATTN_HEADS, XATTN_HEAD_DIM)
    v = (mem_n @ w_v).reshape(bsz, N_MEM, XATTN_HEADS, XATTN_HEAD_DIM)
    s = jnp.einsum('bshd,bmhd->bhsm', q, k).astype(jnp.float32) * (XATTN_HEAD_DIM ** -0.5)
    pr = jax.nn.softmax(s, axis=-1).astype(v.dtype)
    o = jnp.einsum('bhsm,bmhd->bshd', pr, v).reshape(bsz, slen, D_MODEL)
    return o @ w_o

def hierarchical_moe(h, w_rg, b_rg, w_re, b_re, w_gate, w_up, w_down):
    bsz, slen = h.shape[0], h.shape[1]
    hf = h.reshape(-1, D_MODEL)
    n_tok = hf.shape[0]
    logits1 = (hf @ w_rg).astype(jnp.float32) + b_rg
    grp = jnp.argmax(logits1, axis=-1)
    g1 = jnp.take_along_axis(jax.nn.softmax(logits1, axis=-1), grp[:, None], axis=-1)
    logits2 = jnp.einsum('nd,gde->nge', hf, w_re).astype(jnp.float32) + b_re
    logits2 = jnp.take_along_axis(logits2, grp[:, None, None], axis=1)[:, 0]
    top_v, top_i = lax.top_k(logits2, EXPERT_TOP_K)
    gates = g1 * jax.nn.softmax(top_v, axis=-1)
    eid = grp[:, None] * EXPERTS_PER_GROUP + top_i
    n_assign = n_tok * EXPERT_TOP_K
    n_blocks = -(-n_assign // MOE_BLOCK) + N_EXPERTS
    n_slots = n_blocks * MOE_BLOCK
    flat_e = eid.reshape(-1)
    flat_g = gates.reshape(-1)
    flat_tok = jnp.repeat(jnp.arange(n_tok, dtype=jnp.int32), EXPERT_TOP_K)
    order = jnp.argsort(flat_e)
    sorted_e = flat_e[order]
    counts = jnp.bincount(flat_e, length=N_EXPERTS)
    padded = (counts + MOE_BLOCK - 1) // MOE_BLOCK * MOE_BLOCK
    pad_end = jnp.cumsum(padded)
    pad_start = pad_end - padded
    start = jnp.cumsum(counts) - counts
    dest = pad_start[sorted_e] + jnp.arange(n_assign) - start[sorted_e]
    slot_tok = jnp.zeros((n_slots,), jnp.int32).at[dest].set(flat_tok[order])
    slot_gate = jnp.zeros((n_slots,), jnp.float32).at[dest].set(flat_g[order])
    block_start = jnp.arange(n_blocks) * MOE_BLOCK
    block_expert = jnp.minimum(jnp.searchsorted(pad_end, block_start, side='right'), N_EXPERTS - 1)

    def run_block(args):
        tok, gate, e = args
        xb = hf[tok]
        hid = jax.nn.silu(xb @ w_gate[e]) * (xb @ w_up[e])
        return (hid @ w_down[e]) * gate[:, None].astype(xb.dtype)

    y = lax.map(run_block, (slot_tok.reshape(n_blocks, MOE_BLOCK),
                            slot_gate.reshape(n_blocks, MOE_BLOCK), block_expert))
    out = jnp.zeros_like(hf).at[slot_tok].add(y.reshape(n_slots, D_MODEL).astype(hf.dtype))
    return out.reshape(bsz, slen, D_MODEL)

def setup_inputs(seed: int = 0) -> dict:
    key = jax.random.key(seed)
    ks = iter(jax.random.split(key, 48))
    L = DEPTH
    f32 = jnp.float32
    nrm = lambda shape, scale: jax.random.normal(next(ks), shape, f32) * scale
    uni = lambda shape, lo, hi: jax.random.uniform(next(ks), shape, f32, lo, hi)
    gain = lambda shape: 1.0 + nrm(shape, 0.02)
    return {
        "x": nrm((BATCH, SEQ, D_MODEL), 1.0),
        "mem": nrm((BATCH, N_MEM, D_MODEL), 1.0),
        "norm_mix_w": gain((L, D_MODEL)),
        "w_in": nrm((L, D_MODEL, D_IN), D_MODEL ** -0.5),
        "mu_shift": uni((L, D_SHIFT), 0.0, 1.0),
        "w0": uni((L, D_RWKV), -6.0, 1.0),
        "w_decay_up": nrm((L, DECAY_RANK, D_RWKV), 0.5 * DECAY_RANK ** -0.5),
        "a0": uni((L, D_RWKV), -0.5, 0.5),
        "w_iclr_up": nrm((L, ICLR_RANK, D_RWKV), 0.5 * ICLR_RANK ** -0.5),
        "w_gate_up": nrm((L, GATE_RANK, D_RWKV), GATE_RANK ** -0.5),
        "k_k": 0.85 + nrm((L, D_RWKV), 0.02),
        "k_a": gain((L, D_RWKV)),
        "r_k": nrm((L, RWKV_HEADS, RWKV_HEAD_DIM), 0.1),
        "ln_x_w": gain((L, D_RWKV)),
        "ln_x_b": nrm((L, D_RWKV), 0.01),
        "s5_lam_re": -0.5 + nrm((L, S5_GROUPS, S5_STATE), 0.01),
        "s5_lam_im": jnp.pi * jnp.arange(S5_STATE, dtype=f32) + nrm((L, S5_GROUPS, S5_STATE), 0.01),
        "s5_log_dt": uni((L, S5_GROUPS), math.log(1e-3), math.log(1e-1)),
        "s5_b_re": nrm((L, S5_GROUPS, S5_STATE, S5_GROUP_CH), (2 * S5_GROUP_CH) ** -0.5),
        "s5_b_im": nrm((L, S5_GROUPS, S5_STATE, S5_GROUP_CH), (2 * S5_GROUP_CH) ** -0.5),
        "s5_c_re": nrm((L, S5_GROUPS, S5_GROUP_CH, S5_STATE), S5_STATE ** -0.5),
        "s5_c_im": nrm((L, S5_GROUPS, S5_GROUP_CH, S5_STATE), S5_STATE ** -0.5),
        "s5_d": nrm((L, S5_GROUPS, S5_GROUP_CH), 1.0),
        "w_glu": nrm((L, D_S5, D_S5), D_S5 ** -0.5),
        "b_glu": nrm((L, D_S5), 0.01),
        "w_mix_out": nrm((L, D_MIX, D_MODEL), D_MIX ** -0.5),
        "norm_xattn_w": gain((L, D_MODEL)),
        "norm_mem_w": gain((L, D_MODEL)),
        "w_q": nrm((L, D_MODEL, D_MODEL), D_MODEL ** -0.5),
        "w_k": nrm((L, D_MODEL, D_MODEL), D_MODEL ** -0.5),
        "w_v": nrm((L, D_MODEL, D_MODEL), D_MODEL ** -0.5),
        "w_o": nrm((L, D_MODEL, D_MODEL), D_MODEL ** -0.5),
        "norm_moe_w": gain((L, D_MODEL)),
        "w_router_group": nrm((L, D_MODEL, N_EXPERT_GROUPS), D_MODEL ** -0.5),
        "b_router_group": nrm((L, N_EXPERT_GROUPS), 0.01),
        "w_router_expert": nrm((L, N_EXPERT_GROUPS, D_MODEL, EXPERTS_PER_GROUP), D_MODEL ** -0.5),
        "b_router_expert": nrm((L, N_EXPERT_GROUPS, EXPERTS_PER_GROUP), 0.01),
        "w_exp_gate": nrm((L, N_EXPERTS, D_MODEL, D_EXPERT), D_MODEL ** -0.5),
        "w_exp_up": nrm((L, N_EXPERTS, D_MODEL, D_EXPERT), D_MODEL ** -0.5),
        "w_exp_down": nrm((L, N_EXPERTS, D_EXPERT, D_MODEL), D_EXPERT ** -0.5),
        "norm_final_w": gain((D_MODEL,)),
    }

def reference(x, mem, norm_mix_w, w_in, mu_shift, w0, w_decay_up, a0, w_iclr_up, w_gate_up, k_k, k_a,
              r_k, ln_x_w, ln_x_b, s5_lam_re, s5_lam_im, s5_log_dt, s5_b_re, s5_b_im, s5_c_re, s5_c_im,
              s5_d, w_glu, b_glu, w_mix_out, norm_xattn_w, norm_mem_w, w_q, w_k, w_v, w_o, norm_moe_w,
              w_router_group, b_router_group, w_router_expert, b_router_expert, w_exp_gate, w_exp_up,
              w_exp_down, norm_final_w):
    for l in range(DEPTH):
        h = rmsnorm(x, norm_mix_w[l])
        proj = (h @ w_in[l]).astype(jnp.float32)
        p_rwkv = token_shift(proj[..., :D_SHIFT], mu_shift[l])
        u_s5 = proj[..., D_SHIFT:]
        y_rwkv = rwkv7_group(p_rwkv, w0[l], w_decay_up[l], a0[l], w_iclr_up[l], w_gate_up[l],
                             k_k[l], k_a[l], r_k[l], ln_x_w[l], ln_x_b[l])
        y_s5 = s5_group(u_s5, s5_lam_re[l], s5_lam_im[l], s5_log_dt[l], s5_b_re[l], s5_b_im[l],
                        s5_c_re[l], s5_c_im[l], s5_d[l], w_glu[l], b_glu[l])
        y_mix = jnp.concatenate([y_rwkv, y_s5], axis=-1).astype(x.dtype)
        x = x + y_mix @ w_mix_out[l]
        h = rmsnorm(x, norm_xattn_w[l])
        mem_n = rmsnorm(mem, norm_mem_w[l])
        x = x + memory_cross_attention(h, mem_n, w_q[l], w_k[l], w_v[l], w_o[l])
        h = rmsnorm(x, norm_moe_w[l])
        x = x + hierarchical_moe(h, w_router_group[l], b_router_group[l], w_router_expert[l],
                                 b_router_expert[l], w_exp_gate[l], w_exp_up[l], w_exp_down[l])
    return rmsnorm(x, norm_final_w)


_drawn_inputs = setup_inputs


def setup_inputs(seed=0):
    import zlib

    import numpy as np

    out = dict(_drawn_inputs(seed))
    spreads = {}
    factors = {'w_decay_up': 3.045,
     'k_k': 3.262,
     'k_a': 3.659,
     'ln_x_w': 3.57,
     'ln_x_b': 4.103,
     's5_lam_re': 64.0,
     'b_glu': 8.0,
     'norm_xattn_w': 5.289,
     'norm_mem_w': 7.121,
     'b_router_group': 31.528,
     'b_router_expert': 30.16,
     's5_b_im': 2.78,
     'norm_moe_w': 8.0}
    for name, (base, spread) in spreads.items():
        noise = np.random.default_rng([zlib.crc32(name.encode()), seed]).standard_normal(out[name].shape)
        drawn = base * np.exp(spread * noise) if base else spread * noise
        out[name] = __import__('jax').numpy.asarray(drawn.astype(out[name].dtype))
    for name, factor in factors.items():
        out[name] = (out[name] * factor).astype(out[name].dtype)
    return out
```

```python
from contextlib import ExitStack

import concourse.bass as bass
import numpy as np
from concourse import mybir

F32 = mybir.dt.float32
I32 = mybir.dt.int32
U32 = mybir.dt.uint32
ALU = mybir.AluOpType
ACT = mybir.ActivationFunctionType
AX_X = mybir.AxisListType.X
ds = bass.ds

P = 128
D = 1024
T = 1024
KT = D // P
TT = T // P
HEADS, HD = 8, 64
J = HEADS * HD // P
CH = 64
NC = T // CH
N_SHIFT = 14
GROUPS, GC, NS = 32, 16, 64
PAIRS = GROUPS // 2
TAU = P // GC
SC = T // TAU
MEM = 256
XH = 4
NE, NG, EPG = 32, 4, 8
FE = 512
OVER = 2 * T // P - 1
SLOTS = (NE + OVER) * P
EPS = 1e-6
DECAY = float(np.exp(-0.5))
TWO_PI = 2.0 * np.pi

ROWS = {}
_at = 0
for _n, _k in (("norm_mix_w", 8), ("mu_shift", 14), ("w0", 4), ("a0", 4), ("k_k", 4), ("k_a", 4), ("r_k", 4),
               ("norm_xattn_w", 8), ("norm_mem_w", 8), ("norm_moe_w", 8), ("b_glu", 4),
               ("s5_lam_re", 16), ("s5_lam_im", 16)):
    ROWS[_n] = (_at, _k)
    _at += _k
NROWS = _at


def program(nc, I, out):
    ctx = ExitStack()
    with ctx:
        def sb(name, shape, dt=F32):
            return ctx.enter_context(nc.sbuf_tensor(name, shape, dt))

        sems = {}

        def sem(name):
            if name not in sems:
                sems[name] = ctx.enter_context(nc.semaphore(name))
            return sems[name]

        ONCE = {
            "dve_marks": ["rkc_ready", "gn_centred", "gn_var", "gn_done", "ldrow_ready", "s5_angle", "w2_ready", "v1_ready",
                          "kk_ready", "sprev_ready", "l1_ready", "dv_ready", "marks_ready", "slots_ready"],
            "act_marks": ["pcol_ready", "dwda_ready", "gn_sq", "gn_std", "s5_dt", "s5_trig", "exp_l1", "exp_dv"],
            "pe_marks": ["pcol_ps", "dt_ps", "c_ps", "logits_ps", "ranks_ps"],
            "pool_marks": ["consts_a", "consts_b", "reset_ready", "bd_zero", "toe_zero", "router_consts"],
        }

        def once(event):
            return next((name, events.index(event) + 1) for name, events in ONCE.items() if event in events)

        def reach(event):
            return sem(once(event)[0]), 1

        def reached(event):
            return sem(once(event)[0]), once(event)[1]

        arena = sb("arena", [P, 50 * 1024])

        def unit(a, n=1):
            return arena[:, a * 1024:(a + n) * 1024]

        ident = sb("ident", [P, P])
        ones = sb("ones", [P, P])
        blockones = sb("blockones", [P, P])
        pmask = sb("pmask", [P, P])
        strictU = sb("strictU", [P, P])
        lmask = sb("lmask", [P, 6, HD])
        lmask1T = sb("lmask1T", [P, HD])
        eye = sb("eye", [P, HD])
        prow = sb("prow", [P, P])
        pcol = sb("pcol", [P, NROWS])
        omka = sb("omka", [P, J])
        rkc = sb("rkc", [P, J, 2])
        small = sb("small", [P, 64])
        banks = [ctx.enter_context(nc.psum_tensor(f"bank{i}", [P, 512], F32)) for i in range(8)]

        def col(name, k=0):
            return pcol[:, ROWS[name][0] + k:ROWS[name][0] + k + 1]

        def cols(name):
            a, n = ROWS[name]
            return pcol[:, a:a + n]

        hT = unit(0, 8).rearrange("p (k t) -> p k t", k=KT)
        PT = unit(8, 14).rearrange("p (m t) -> p m t", m=N_SHIFT)
        uT = unit(22, 4).rearrange("p (j t) -> p j t", j=4)
        AR = unit(26, 8).rearrange("p (j c x) -> p j c x", j=J, c=NC)
        BK = unit(34, 8).rearrange("p (j c x) -> p j c x", j=J, c=NC)
        X = unit(26, 8).rearrange("p (i d) -> p i d", i=TT)
        wring = [unit(42 + s).rearrange("p (k m) -> p k m", k=KT) for s in range(2)]
        zbuf = [arena[:, (44 * 1024 + s * 1088):(44 * 1024 + s * 1088) + 1025] for s in range(2)]
        shift_d = unit(47)
        xs = [unit(48 + s).rearrange("p (k t) -> p k t", k=KT) for s in range(2)]
        junk = unit(34)

        ss = small[:, 0:8]
        rstd = small[:, 8:16]

        d_u = nc.dram_tensor("d_u", (4 * P, TAU, SC), F32).ap()
        d_z = nc.dram_tensor("d_z", (4 * P, TAU, SC), F32).ap()

        w_in = I["w_in"][0].rearrange("(k p) n -> p k n", p=P)

        sig, csum, gexp, ginv, gprev, kk, avec, tmp = (unit(42 + n) for n in range(8))
        gcol = sb("gcol", [P, NC, J])
        wdi = unit(6)[:, 0:512]
        wgu = unit(6)[:, 512:1024]
        reset = unit(0)
        Vt = unit(12, 4).rearrange("p (i c) -> p i c", i=TT)
        Gt = unit(1, 4).rearrange("p (i c) -> p i c", i=TT)
        rks = sb("rks", [P, TT, HEADS])
        Yt = unit(16, 4).rearrange("p (i c) -> p i c", i=TT)
        ARc = [unit(42 + s)[:, 0:512].rearrange("p (j x) -> p j x", j=J) for s in range(2)]
        BKz = [unit(44 + s).rearrange("p (h x) -> p h x", h=HEADS) for s in range(2)]
        UV = [unit(46)[:, 512 * s:512 * s + 512].rearrange("p (h v) -> p h v", h=HEADS) for s in range(2)]
        V0 = [unit(47)[:, 512 * s:512 * s + 512].rearrange("p (h v) -> p h v", h=HEADS) for s in range(2)]
        PM = unit(48).rearrange("p (h x) -> p h x", h=HEADS)
        BKT = unit(49)[:, 0:512].rearrange("p (j x) -> p j x", j=J)
        Zbd = unit(49)[:, 512:1024].rearrange("p (j x) -> p j x", j=J)
        LTbd = unit(5)[:, 0:512].rearrange("p (j x) -> p j x", j=J)
        TTbd = unit(5)[:, 512:1024].rearrange("p (j x) -> p j x", j=J)
        Xbd = unit(6)[:, 0:512].rearrange("p (j x) -> p j x", j=J)
        TS = unit(6)[:, 512:1024].rearrange("p (a j x) -> p a j x", a=2, j=J)
        Xst = unit(7)[:, 0:256].rearrange("p (j x) -> p j x", j=J)
        Qst = unit(7)[:, 256:512].rearrange("p (j x) -> p j x", j=J)
        Zst = unit(7)[:, 512:768].rearrange("p (j x) -> p j x", j=J)
        Ztmp = unit(7)[:, 768:1024].rearrange("p (j x) -> p j x", j=J)

        gtmp = unit(42, 4)
        lnwb = unit(46)
        gstat = unit(47)[:, 0:192].rearrange("p (a g) -> p a g", a=3)
        ymixT = unit(26, 8).rearrange("p (k t) -> p k t", k=KT)
        Xg = unit(34, 4).rearrange("p (g c) -> p g c", g=GROUPS)
        Toe = unit(38, 4).rearrange("p (g x) -> p g x", g=GROUPS)
        W1 = [unit(20 + 2 * a, 2).rearrange("p (q x) -> p q x", q=PAIRS) for a in range(2)]
        W2 = [arena[:, 5 * 1024 + 2304 * a:5 * 1024 + 2304 * (a + 1)].rearrange("p (q x) -> p q x", q=PAIRS) for a in range(2)]
        V1 = [unit(46 + 2 * a, 2).rearrange("p (q x) -> p q x", q=PAIRS) for a in range(2)]
        Braw = [unit(0)[:, 256 * a:256 * a + 256].rearrange("p (q i) -> p q i", q=PAIRS) for a in range(2)]
        Bbar = [unit(0)[:, 512 + 256 * a:768 + 256 * a].rearrange("p (q i) -> p q i", q=PAIRS) for a in range(2)]
        Cst = [unit(11)[:, 256 * a:256 * a + 256].rearrange("p (q o) -> p q o", q=PAIRS) for a in range(2)]
        Craw = [unit(11)[:, 512 + 256 * a:768 + 256 * a].rearrange("p (r n) -> p r n", r=4) for a in range(2)]
        KK = unit(12, 4)[0:16, :].rearrange("p (g x) -> p g x", g=GROUPS)
        E5 = [unit(24, 2), unit(48, 2)]
        trig = [unit(42, 2), unit(44, 2)]
        Rtab = unit(46, 2)
        rot = [unit(12 + 2 * a, 2) for a in range(2)]
        zst = [unit(1 + 2 * a, 2) for a in range(2)]
        Sprev = [unit(12 + 2 * a, 2) for a in range(2)]
        y5 = unit(16, 4)
        t5 = [unit(9)[:, 512:1024], unit(10)]
        zT = unit(34, 4).rearrange("p (j t) -> p j t", j=4)
        wglu = unit(20, 2).rearrange("p (k m) -> p k m", k=4)
        sglu = unit(24)
        s5d = unit(10)[0:16, 992:1024]
        ldt = unit(10)[0:16, 988:990]
        ldrow = unit(10)[0:16, 856:984]
        names5 = ["dt", "are", "th", "rho", "kr", "rr", "ra", "sn", "cs", "lr", "li", "nr", "den", "cr", "ci", "t1", "t2", "t3", "t4",
                  "r8", "pr", "pi", "pr2", "pi2"]
        a5 = {n: unit(10)[:, 16 * i:16 * i + 16] for i, n in enumerate(names5)}
        pw = [unit(10)[:, 400 + 144 * a:544 + 144 * a].rearrange("p (k q) -> p k q", k=9) for a in range(2)]
        pwr = [unit(9)[:, 512 + 128 * a:640 + 128 * a].rearrange("p (k q) -> p k q", k=8) for a in range(2)]
        Xr = unit(0, 8).rearrange("p (i d) -> p i d", i=TT)
        wmix = unit(8, 8).rearrange("p (k n) -> p k n", k=KT)
        tokring = [unit(16 + s).rearrange("p (k t) -> p k t", k=KT) for s in range(2)]

        hB = unit(18, 8).rearrange("p (k t) -> p k t", k=KT)
        wq = unit(26, 8).rearrange("p (k n) -> p k n", k=KT)
        wvo = unit(8, 8).rearrange("p (k n) -> p k n", k=KT)
        Xm = unit(34, 2).rearrange("p (i d) -> p i d", i=2)
        hM = unit(36, 2).rearrange("p (k m) -> p k m", k=KT)
        kT = unit(38, 2).rearrange("p (k m) -> p k m", k=KT)
        vM = unit(40, 2).rearrange("p (i d) -> p i d", i=2)
        wkr = [unit(42 + s).rearrange("p (k m) -> p k m", k=KT) for s in range(2)]
        qr = [unit(44 + s).rearrange("p (k t) -> p k t", k=KT) for s in range(2)]
        oR = [unit(46 + s).rearrange("p (k t) -> p k t", k=KT) for s in range(2)]
        pr_ = unit(16).rearrange("p (h m) -> p h m", h=XH)
        pT = unit(17).rearrange("p (i h t) -> p i h t", i=2, h=XH)
        junk2 = unit(47)
        smx = [small[:, 16 + 4 * s:20 + 4 * s] for s in range(2)]
        ssum = [small[:, 24 + 4 * s:28 + 4 * s] for s in range(2)]
        wrt = unit(47)[:, 0:288].rearrange("p (k e) -> p k e", k=KT)
        brt = unit(47)[:, 288:324]
        LG = unit(16)[:, 0:288].rearrange("p (i e) -> p i e", i=TT)
        l2 = unit(16)[:, 288:544].rearrange("p (i e) -> p i e", i=TT)
        io32 = unit(16)[:, 544:576]
        io4b, io8b = unit(16)[:, 576:580], unit(16)[:, 580:588]
        io128 = unit(16)[:, 588:620]
        ioM = unit(16)[:, 620:627]
        ioO = unit(16)[:, 628:643]
        e8 = [unit(16)[:, 644 + 64 * i:708 + 64 * i].rearrange("p (i e) -> p i e", i=TT) for i in range(5)]
        O2 = [unit(17)[:, 256 * a:256 * a + 256].rearrange("p (i e) -> p i e", i=TT) for a in range(2)]
        MS = unit(17)[:, 512:768].rearrange("p (i e) -> p i e", i=TT)
        MA = unit(17)[:, 768:1024].rearrange("p (i e) -> p i e", i=TT)
        RK = unit(46)[:, 0:256].rearrange("p (i e) -> p i e", i=TT)
        RT = unit(46)[:, 256:512].rearrange("p (i e) -> p i e", i=TT)
        c32 = [unit(46)[:, 512 + 32 * i:544 + 32 * i] for i in range(5)]
        cmpb = unit(46)[:, 672:672 + 224].rearrange("p (e m) -> p e m", m=7)
        cmpo = unit(45)[:, 0:480].rearrange("p (b e) -> p b e", e=NE)
        v8 = [small[:, 8 * i:8 * i + 8] for i in range(8)]
        s8 = [unit(46)[:, 896 + 8 * i:904 + 8 * i] for i in range(14)]
        gates = sb("gates", [P, 16])
        ints = sb("ints", [P, 48], I32)
        slots_i = ints[:, 0:16]
        tokid = ints[:, 16:24]
        nover_i = ints[:, 24:25]
        eid_i = ints[:, 25:40]
        idx = [ints[:, 40 + s:41 + s] for s in range(2)]
        zint = unit(44)[:, 0:47].bitcast(I32)
        d_slot = nc.dram_tensor("d_slot", (SLOTS, 1), I32).ap()
        d_xn = nc.dram_tensor("d_xn", (T, D), F32).ap()
        d_y = nc.dram_tensor("d_y", (SLOTS, D), F32).ap()
        WG = [unit(a, 4).rearrange("p (k n) -> p k n", k=KT) for a in (26, 8)]
        WU = [unit(a, 4).rearrange("p (k n) -> p k n", k=KT) for a in (30, 12)]
        WD = [unit(a, 4).rearrange("p (k n) -> p k n", k=4) for a in (34, 38)]
        xb = [unit(42 + s) for s in range(2)]
        xbT = [unit(44 + s).rearrange("p (k t) -> p k t", k=KT) for s in range(2)]
        sg = unit(46)[:, 0:512]
        hid = unit(46)[:, 512:1024]
        hidT = unit(47)[:, 0:512].rearrange("p (k t) -> p k t", k=4)
        gainp = unit(47)[:, 512:520]
        ysb = [unit(48 + s) for s in range(2)]
        yg = [[unit(8 + 2 * s + a) for a in range(2)] for s in range(2)]
        wfin = unit(12)
        ost = [unit(13 + s) for s in range(2)]

        block = ctx.enter_context(nc.Block())

        @block.gpsimd
        def _(pool):
            n = [0]

            def step(ins):
                ins.then_inc(sem("pool_chain"), 1)
                n[0] += 1
                pool.wait_ge(sem("pool_chain"), n[0])

            def keep(view, op, base, pattern, cm, fill=0.0):
                step(pool.affine_select(out=view, in_=view, compare_op=op, fill=fill, base=base,
                                        pattern=pattern, channel_multiplier=cm))

            step(pool.memset(ident[:, :], 0.0))
            keep(ident[:, :], ALU.not_equal, 0, [[-1, P]], 1, 1.0)
            step(pool.memset(ones[:, :], 1.0))
            step(pool.memset(blockones[:, :], 0.0))
            step(pool.memset(blockones[0:64, 0:64], 1.0))
            step(pool.memset(blockones[64:128, 64:128], 1.0))
            step(pool.memset(prow[:, :], 0.0))
            step(pool.memset(unit(36), 0.0))
            pool.nop().then_inc(*reach("consts_a"))
            step(pool.memset(pmask[:, :], 1.0))
            step(pool.memset(strictU[:, :], 1.0))
            keep(strictU[:, :], ALU.is_ge, -1, [[1, P]], -1)
            step(pool.memset(eye[:, :], 0.0))
            step(pool.memset(lmask1T[:, :], 0.0))
            step(pool.memset(lmask[:, :, :], 0.0))
            for h in (0, 64):
                keep(eye[h:h + 64, :], ALU.not_equal, 0, [[-1, 64]], 1, 1.0)
                keep(pmask[h:h + 64, 0:64], ALU.is_ge, -1, [[1, 64]], -1)
                keep(pmask[h:h + 64, 64:128], ALU.is_ge, 0, [[1, 64]], -1)
                keep(lmask1T[h:h + 64, 1:64:2], ALU.not_equal, 0, [[-2, 32]], 1, 1.0)
                for lv in range(6):
                    m = 1 << lv
                    v = lmask[h:h + 64, lv, :].rearrange("p (b x) -> p b x", x=2 * m)
                    step(pool.memset(v[:, :, 0:m], 1.0))
                    keep(v, ALU.is_ge, -m, [[-2 * m, 32 // m], [0, 2 * m]], 1)
                    keep(v, ALU.is_ge, 2 * m - 1, [[2 * m, 32 // m], [0, 2 * m]], -1)
            pool.nop().then_inc(*reach("consts_b"))
            pool.wait_ge(sem("z_done"), 4 + 36)
            step(pool.memset(reset, 1.0))
            step(pool.memset(reset.rearrange("p (c x) -> p c x", x=CH)[:, :, 0:1], 0.0))
            pool.sem_inc(*reach("reset_ready"))
            pool.wait_ge(sem("elem_done"), J)
            pool.wait_ge(sem("values_evac"), TT)
            pool.wait_ge(sem("gates_evac"), 2 * TT)
            for v in (unit(5), unit(6)[:, 0:512], unit(7)[:, 512:768], unit(44, 2), unit(47)[0:64, :], unit(49)[:, 512:1024]):
                step(pool.memset(v, 0.0))
            pool.sem_inc(*reach("bd_zero"))
            with pool.Fori(0, NC // 2) as cc:
                for s in range(2):
                    for lv in range(1, 6):
                        pool.wait_ge(sem("Xst_ready"), cc * 10 + (5 * s + lv))
                        pool.sem_inc(sem("pool_waits"), 1)
                        for p in range(2):
                            pool.tensor_copy(Xbd[64 * p:64 * p + 64, :, 64 * p:64 * p + 64],
                                             Xst[64 * p:64 * p + 64, :, :]).then_inc(sem("Xbd_ready"), 1)
            pool.wait_ge(sem("y_free"), 2 + NC)
            step(pool.memset(Toe, 0.0))
            pool.sem_inc(*reach("toe_zero"))
            pool.wait_ge(sem("x_attn"), 4 + 2 * TT)
            for v, pat, base in ((io32, [[1, NE]], 0), (io4b, [[1, NG]], 8), (io8b, [[1, EPG]], 16), (io128, [[P, NE]], 0),
                                 (ioM, [[P, 7]], P), (ioO, [[1, OVER]], 0)):
                step(pool.iota(v, pat, base=base, channel_multiplier=0, allow_small_or_imprecise_dtypes=True))
            step(pool.iota(tokid, [[P, TT]], base=0, channel_multiplier=1))
            step(pool.memset(zint, 0))
            pool.sem_inc(*reach("router_consts"))
            pool.dma_start(d_slot.rearrange("(p b) o -> p (b o)", p=P), zint).then_inc(sem("slot_zero"), 16)
            pool.wait_ge(sem("slot_zero"), 16)
            pool.wait_ge(*reached("slots_ready"))
            for k in range(2 * TT):
                pool.indirect_dma_start(d_slot, bass.IndirectOffsetOnAxis(ap=slots_i[:, k:k + 1], axis=0),
                                        tokid[:, k % TT:k % TT + 1], None).then_inc(sem("slot_written"), 16)
            pool.wait_ge(sem("slot_written"), 16 * 2 * TT)
            pool.wait_ge(sem("xn_stored0"), 16 + 64)
            pool.wait_ge(sem("xn_stored1"), 16 + 64)

            def gather_block(s, n, ns, lead):
                idx_loaded, xb_loaded = (sem("idx_loaded0"), sem("xb_loaded0")) if s == 0 else (sem("idx_loaded1"), sem("xb_loaded1"))
                pool.wait_ge(sem("xT_ps"), n * 2 + 2 * lead)
                pool.dma_start(idx[s], d_slot[ds(n * P, P), :]).then_inc(idx_loaded, 16)
                pool.wait_ge(idx_loaded, ns * 16 + 16)
                pool.sem_inc(sem("pool_waits"), 1)
                pool.indirect_dma_start(xb[s], None, d_xn, bass.IndirectOffsetOnAxis(ap=idx[s], axis=0)).then_inc(xb_loaded, 16)

            with pool.Fori(0, NE // 2) as bb:
                for s in range(2):
                    gather_block(s, bb * 2 + s, bb, 1)
            n_over = pool.value_load(nover_i[0:1, :], min_val=0, max_val=OVER)
            with pool.Fori(0, OVER) as o:
                with pool.If(o < n_over):
                    gather_block(0, o + NE, o + NE // 2, 2)
                pool.nop()
            pool.wait_ge(sem("y_stored0"), n_over * 16 + (16 + 16 * (NE // 2)))
            pool.sem_inc(sem("pool_waits"), 1)
            pool.wait_ge(sem("y_stored1"), 16 + 16 * (NE // 2))
            for i in range(TT):
                if i >= 2:
                    pool.wait_ge(sem("y_added"), 2 * (i - 1))
                for a in range(2):
                    pool.indirect_dma_start(yg[i % 2][a], None, d_y, bass.IndirectOffsetOnAxis(ap=slots_i[:, a * TT + i:a * TT + i + 1], axis=0)
                                            ).then_inc(sem("yg_loaded0") if i % 2 == 0 else sem("yg_loaded1"), 16)

        @block.sync
        def _(sp):
            sp.wait_ge(*reached("consts_a"))
            for name, (a, k) in ROWS.items():
                src = I[name][0]
                if name == "r_k":
                    src = src.rearrange("(j h) c -> j (h c)", j=J)
                elif name.startswith("s5_lam"):
                    src = src.rearrange("(q h) c -> q (h c)", q=PAIRS)
                else:
                    src = src.rearrange("(k p) -> k p", p=P)
                sp.dma_start(prow[a:a + k, :], src).then_inc(sem("params_loaded"), 16)
            sp.dma_start(X, I["x"][0].rearrange("(i p) d -> p i d", p=P)).then_inc(sem("x_loaded"), 16)
            sp.dma_start(d_y[NE * P:SLOTS, :].rearrange("(b p) d -> p b d", p=P),
                         unit(36).rearrange("p (o d) -> p o d", o=1).to_broadcast((P, OVER, D))).then_inc(sem("y_zeroed"), 16)
            with sp.Fori(0, 9) as mm:
                for s in range(2):
                    sp.wait_ge(sem("z_done"), mm * 4 + (2 * s + 2))
                    sp.dma_start(wring[s], w_in[:, :, ds(mm * 256 + s * 128, 128)]).then_inc(
                        sem("win_loaded0") if s == 0 else sem("win_loaded1"), 16)
            sp.wait_ge(sem("z_evac"), 4 + 36)
            sp.wait_ge(sem("z_done"), 4 + 36)
            sp.dma_start(wdi[0:64, :], I["w_decay_up"][0]).then_inc(sem("lora_loaded"), 16)
            sp.dma_start(wdi[64:128, :], I["w_iclr_up"][0]).then_inc(sem("lora_loaded"), 16)
            sp.dma_start(wgu[:, :], I["w_gate_up"][0]).then_inc(sem("lora_loaded"), 16)
            sp.dma_start(d_u.rearrange("(j p) a c -> p j (a c)", p=P), uT).then_inc(sem("u_stored"), 16)
            sp.wait_ge(*reached("bd_zero"))
            sp.wait_ge(sem("values_evac"), TT)
            with sp.Fori(0, NC // 2) as cc:
                for s in range(2):
                    staged = sem("staged0") if s == 0 else sem("staged1")
                    sp.wait_ge(sem("y_free"), cc * 2 + (s + 1))
                    c = cc * 2 + s
                    sp.dma_start(ARc[s], AR[:, :, ds(c, 1), :].rearrange("p j o x -> p j (o x)")).then_inc(staged, 16)
                    for p in range(2):
                        sp.dma_start(BKz[s][64 * p:64 * p + 64, p:HEADS:2, :],
                                     BK[64 * p:64 * p + 64, :, ds(c, 1), :].rearrange("p j o x -> p j (o x)")).then_inc(staged, 16)
                    for v in (UV, V0):
                        sp.dma_start(v[s][64:128, :, :], Vt[64 * s:64 * s + 64, ds(cc, 1), :].rearrange("p o (h v) -> p (o h) v", h=HEADS)
                                     ).then_inc(staged, 16)
            sp.wait_ge(sem("y_free"), 2 + NC)
            sp.wait_ge(sem("u_stored"), 16)
            sp.dma_start(lnwb[:, 0:512], I["ln_x_w"].to_broadcast((P, 512))).then_inc(sem("ln_loaded"), 16)
            sp.dma_start(lnwb[:, 512:1024], I["ln_x_b"].to_broadcast((P, 512))).then_inc(sem("ln_loaded"), 16)
            sp.dma_start(ldt, I["s5_log_dt"][0].rearrange("(q h) -> q h", q=PAIRS)).then_inc(sem("s5_loaded"), 16)
            for a, n in enumerate(("re", "im")):
                sp.dma_start(Braw[a], I["s5_b_" + n][0].rearrange("(q h) n i -> (h n) q i", h=2)).then_inc(sem("s5_loaded"), 16)
                sp.dma_start(Craw[a], I["s5_c_" + n][0].rearrange("(r g) o n -> (g o) r n", r=4)).then_inc(sem("s5_loaded"), 16)
            with nc.allow_non_contiguous_dma(reason="512 skip weights, once"):
                sp.dma_start(s5d, I["s5_d"][0].rearrange("g i -> i g")).then_inc(sem("s5_loaded"), 16)
            for a in range(TAU):
                sp.dma_start(Xg[GC * a:GC * a + GC, :, :], d_u[:, a, :].rearrange("(g i) c -> i g c", i=GC)).then_inc(sem("xg_loaded"), 16)
            sp.wait_ge(*reached("kk_ready"))
            sp.wait_ge(*reached("toe_zero"))
            for a in range(TAU):
                sp.dma_start(Toe[GC * a:GC * a + GC, :, GC * a:P], KK[:, :, 0:P - GC * a]).then_inc(sem("toe_loaded"), 16)
            for a in range(TAU):
                if a == 0:
                    sp.wait_ge(sem("gelu_done"), 8)
                sp.dma_start(d_z[:, a, :].rearrange("(g o) c -> o g c", o=GC),
                             y5[GC * a:GC * a + GC, :].rearrange("p (g c) -> p g c", g=GROUPS)).then_inc(sem("z_stored"), 16)
            sp.dma_start(wglu, I["w_glu"][0].rearrange("(k p) m -> p k m", p=P)).then_inc(sem("wglu_loaded"), 16)
            sp.dma_start(wmix, I["w_mix_out"][0].rearrange("(k p) n -> p k n", p=P)).then_inc(sem("wmix_loaded"), 16)
            sp.dma_start(Xr, I["x"][0].rearrange("(i p) d -> p i d", p=P)).then_inc(sem("xr_loaded"), 16)
            sp.wait_ge(sem("z_stored"), 16 * TAU)
            sp.dma_start(zT, d_z.rearrange("(j p) a c -> p j (a c)", p=P)).then_inc(sem("zT_loaded"), 16)
            sp.wait_ge(sem("ymix_rwkv"), TT)
            sp.wait_ge(sem("ymix_s5"), 8)
            sp.wait_ge(sem("z_stored"), 16 * TAU)
            with sp.Fori(0, TT // 2) as ii:
                for s in range(2):
                    sp.wait_ge(sem("mix_ps"), ii * 4 + (2 * s + 2))
                    sp.dma_start(tokring[s], ymixT[:, :, ds(ii * 256 + s * 128, P)]).then_inc(sem("tok0_loaded") if s == 0 else sem("tok1_loaded"), 16)
            sp.wait_ge(sem("mix_added"), 4 + 2 * TT)
            sp.dma_start(Xm, I["mem"][0].rearrange("(i p) d -> p i d", p=P)).then_inc(sem("xm_loaded"), 16)
            sp.dma_start(wvo, I["w_v"][0].rearrange("(k p) n -> p k n", p=P)).then_inc(sem("wv_loaded"), 16)
            sp.dma_start(wq, I["w_q"][0].rearrange("(k p) n -> p k n", p=P)).then_inc(sem("wq_loaded"), 16)
            wk = I["w_k"][0].rearrange("(k p) n -> p k n", p=P)
            with sp.Fori(0, KT // 2) as mm:
                for s in range(2):
                    sp.wait_ge(sem("k_ps"), mm * 2 + (s + 1))
                    sp.dma_start(wkr[s], wk[:, :, ds(mm * 256 + s * P, P)]).then_inc(sem("wk_loaded0") if s == 0 else sem("wk_loaded1"), 16)
            sp.wait_ge(sem("v_ps"), 4)
            sp.dma_start(wvo, I["w_o"][0].rearrange("(k p) n -> p k n", p=P)).then_inc(sem("wo_loaded"), 16)
            sp.wait_ge(sem("x_attn"), 4 + 2 * TT)
            sp.dma_start(wrt[:, :, 0:NG], I["w_router_group"][0].rearrange("(k p) g -> p k g", p=P)).then_inc(sem("router_loaded"), 16)
            for g in range(NG):
                sp.dma_start(wrt[:, :, NG + EPG * g:NG + EPG * g + EPG], I["w_router_expert"][0, g].rearrange("(k p) e -> p k e", p=P)).then_inc(sem("router_loaded"), 16)
            sp.dma_start(brt[:, 0:NG], I["b_router_group"].to_broadcast((P, NG))).then_inc(sem("router_loaded"), 16)
            sp.dma_start(brt[:, NG:NG + NE], I["b_router_expert"].rearrange("a g e -> a (g e)").to_broadcast((P, NE))).then_inc(sem("router_loaded"), 16)
            sp.dma_start(gainp, I["norm_moe_w"][0].rearrange("(p k) -> p k", p=P)).then_inc(sem("router_loaded"), 16)

            def load_expert(s, e, n, lead):
                g, u, d = (sem("wg0"), sem("wu0"), sem("wd0")) if s == 0 else (sem("wg1"), sem("wu1"), sem("wd1"))
                sp.wait_ge(sem("up_ps"), n + lead)
                sp.dma_start(WG[s], I["w_exp_gate"][0, ds(e, 1)].rearrange("o (p k) n -> p (o k) n", p=P)).then_inc(g, 16)
                sp.dma_start(WU[s], I["w_exp_up"][0, ds(e, 1)].rearrange("o (p k) n -> p (o k) n", p=P)).then_inc(u, 16)
                sp.wait_ge(sem("dn_ps"), n * 2 + 2 * lead)
                sp.dma_start(WD[s], I["w_exp_down"][0, ds(e, 1)].rearrange("o (p k) n -> p (o k) n", p=P)).then_inc(d, 16)

            for i in range(TT):
                sp.wait_ge(sem("xs_ready"), 18 + i + 1)
                sp.dma_start(d_xn[i * P:(i + 1) * P, :], xs[i % 2].rearrange("p k d -> p (k d)")).then_inc(sem("xn_stored0") if i % 2 == 0 else sem("xn_stored1"), 16)
            with sp.Fori(0, NE // 2) as bb:
                for s in range(2):
                    load_expert(s, bb * 2 + s, bb * 2 + s, 1)
            sp.wait_ge(*reached("slots_ready"))
            n_over = sp.value_load(nover_i[0:1, :], min_val=0, max_val=OVER)
            with sp.Fori(0, OVER) as o:
                with sp.If(o < n_over):
                    e = sp.value_load(eid_i[0:1, ds(o, 1)], min_val=0, max_val=NE - 1)
                    load_expert(0, e, o + NE, 2)
                sp.nop()
            sp.wait_ge(sem("dn_ps"), n_over * 2 + (4 + 2 * NE))
            sp.dma_start(wfin, I["norm_final_w"].rearrange("(o d) -> o d", o=1).to_broadcast((P, D))).then_inc(sem("wfin_loaded"), 16)
            for i in range(TT):
                sp.wait_ge(sem("out_ready"), i + 1)
                sp.dma_start(out[0, i * P:(i + 1) * P, :], ost[i % 2]).then_inc(sem("out0") if i % 2 == 0 else sem("out1"), 16)
            sp.wait_ge(sem("out0"), 64)
            sp.wait_ge(sem("out1"), 64)
        def norm_pe(pe, base, tiles):
            with pe.Fori(0, tiles // 2) as i:
                for s in range(2):
                    pe.wait_ge(sem("xs_ready"), i * 2 + (base + s + 1))
                    for q in range(2):
                        pe.wait_ge(sem("hT_ready"), i * 4 + (2 * base + 2 * s + q + 1))
                        for k in range(4):
                            t = pe.transpose(banks[4 + 2 * s + q][:, k * P:(k + 1) * P], xs[s][:, 4 * q + k, :], ident[:, :])
                        t.then_inc(sem("xsT_ps"), 1)

        @block.tensor
        def _(pe):
            pe.sem_inc(sem("z_done"), 4)
            pe.wait_ge(*reached("consts_a"))
            pe.wait_ge(sem("params_loaded"), 16 * len(ROWS))
            pe.transpose(banks[7][:, 0:NROWS], prow[0:NROWS, :], ident[0:NROWS, 0:NROWS]).then_inc(*reach("pcol_ps"))
            norm_pe(pe, 0, TT)
            pe.wait_ge(sem("hT_ready"), 4 + 2 * TT)
            with pe.Fori(0, 9) as mm:
                for s in range(2):
                    pe.wait_ge(sem("win_loaded0") if s == 0 else sem("win_loaded1"), mm * 16 + 16)
                    for h in range(2):
                        pe.wait_ge(sem("z_evac"), mm * 4 + (2 * s + h + 1))
                        for k in range(KT):
                            m = pe.matmul(banks[2 * s + h][:, :], wring[s][:, k, :], hT[:, k, 512 * h:512 * h + 512],
                                          start=(k == 0), stop=(k == KT - 1))
                        m.then_inc(sem("z_done"), 1)
            pe.wait_ge(sem("lora_loaded"), 48)
            pe.wait_ge(*reached("dwda_ready"))
            for j in range(J):
                if j > 0:
                    pe.wait_ge(sem("rates_ready"), 4 * j)
                for h in range(2):
                    pe.matmul(banks[h][:, :], wdi[0:64, j * P:(j + 1) * P], PT[0:64, 12, 512 * h:512 * h + 512],
                              start=True, stop=True)
                    m = pe.matmul(banks[2 + h][:, :], wdi[64:128, j * P:(j + 1) * P],
                                  PT[64:128, 12, 512 * h:512 * h + 512], start=True, stop=True)
                m.then_inc(sem("rates_ps"), 1)
                pe.wait_ge(sem("kk_sq"), j + 1)
                for h in range(2):
                    m = pe.matmul(banks[4 + h][:, :], blockones[:, :], tmp[:, 512 * h:512 * h + 512], start=True, stop=True)
                m.then_inc(sem("kk_sum"), 1)
            pe.wait_ge(*reached("pcol_ready"))
            pe.wait_ge(sem("elem_done"), J)
            pe.wait_ge(*reached("rkc_ready"))
            for i in range(TT):
                b = 4 * (i % 2)
                if i >= 2:
                    pe.wait_ge(sem("gates_evac"), 2 * (i - 1))
                    pe.wait_ge(sem("values_evac"), i - 1)
                for j in range(J):
                    pe.transpose(banks[b][:, j * P:(j + 1) * P], PT[:, 8 + j, i * P:(i + 1) * P], ident[:, :])
                pe.matmul(banks[b + 1][:, :], PT[:, 13, i * P:(i + 1) * P], wgu[:, :], start=True, stop=True)
                for j in range(J):
                    m = pe.matmul(banks[b + 2][:, 2 * j:2 * j + 2], PT[:, j, i * P:(i + 1) * P], rkc[:, j, :], start=True, stop=True)
                m.then_inc(sem("tok_ps"), 1)
            pe.wait_ge(sem("gates_evac"), 2 * TT)
            pe.wait_ge(sem("values_evac"), TT)
            pe.wait_ge(*reached("consts_b"))
            with pe.Fori(0, NC // 2) as cc:
                for s in range(2):
                    pe.wait_ge(sem("staged0") if s == 0 else sem("staged1"), cc * 80 + 80)
                    for h in range(HEADS):
                        m = pe.matmul(banks[h // 4][:, (h % 4) * P:(h % 4 + 1) * P], BKz[s][:, h, :], ARc[s][:, h // 2, :],
                                      start=True, stop=True)
                        if h % 4 == 3:
                            m.then_inc(sem("pm_ps"), 1)
                    for h in range(HEADS):
                        pe_out = banks[2][64 * (h % 2):64 * (h % 2) + 64, (h // 2) * 64:(h // 2) * 64 + 64]
                        m = pe.matmul(pe_out, ARc[s][:, h // 2, 0:64], BKz[s][:, h, 0:64], start=True, stop=True)
                    m.then_inc(sem("L_ps"), 1)
                    for j in range(J):
                        m = pe.matmul(banks[3][:, j * P:j * P + 64], BKz[s][:, 2 * j, :], ident[:, 0:64], start=True, stop=True)
                        m = pe.matmul(banks[3][:, j * P + 64:j * P + 128], BKz[s][:, 2 * j + 1, :], ident[:, 64:128], start=True, stop=True)
                    m.then_inc(sem("bkt_ps"), 1)
                    for lv in range(1, 6):
                        u = 5 * s + lv
                        pe.wait_ge(sem("TS_ready"), cc * 12 + (6 * s + lv))
                        for j in range(J):
                            m = pe.matmul(banks[4][:, j * 64:j * 64 + 64], LTbd[:, j, :], TS[:, 0, j, :], start=True, stop=True)
                        m.then_inc(sem("LxT_ps"), 1)
                        pe.wait_ge(sem("Xst_ready"), cc * 10 + u)
                        for j in range(J):
                            m = pe.matmul(banks[5][:, j * 64:j * 64 + 64], TTbd[:, j, :], Xst[:, j, :], start=True, stop=True)
                        pe.wait_ge(sem("Xbd_ready"), cc * 20 + 2 * u)
                        for j in range(J):
                            m = pe.matmul(banks[5][:, 256 + j * 64:256 + j * 64 + 64], Xbd[:, j, :], TS[:, 1, j, :], start=True, stop=True)
                        m.then_inc(sem("dT_ps"), 1)
                    pe.wait_ge(sem("Z_ready"), cc * 2 + (s + 1))
                    for h in range(HEADS):
                        o = banks[4][64 * (h % 2):64 * (h % 2) + 64, 256 + (h // 2) * 64:256 + (h // 2) * 64 + 64]
                        pe.matmul(o, ARc[s][:, h // 2, 0:64], Zbd[:, h // 2, 64 * (h % 2):64 * (h % 2) + 64], start=True, stop=False)
                        m = pe.matmul(o, PM[:, h, 0:64], V0[s][:, h, :], start=False, stop=True)
                    m.then_inc(sem("Q_ps"), 1)
                    pe.wait_ge(sem("y_free"), cc * 2 + (s + 1))
                    for j in range(J):
                        pe.matmul(banks[7][64 * s:64 * s + 64, j * P:(j + 1) * P], ARc[s][:, j, 64:128], Zbd[:, j, :],
                                  start=(j == 0), stop=False, skip_group_check=True)
                    pe.wait_ge(sem("TS_ready"), cc * 12 + (6 * s + 6))
                    pe.wait_ge(sem("Q_ready"), cc * 2 + (s + 1))
                    for j in range(J):
                        m = pe.matmul(banks[6][:, j * 64:j * 64 + 64], TTbd[:, j, :], Qst[:, j, :], start=True, stop=True)
                    m.then_inc(sem("U_ps"), 1)
                    pe.wait_ge(sem("U_ready"), cc * 4 + (2 * s + 2))
                    for h in range(HEADS):
                        o = banks[6][64 * (h % 2):64 * (h % 2) + 64, 256 + (h // 2) * 64:256 + (h // 2) * 64 + 64]
                        m = pe.matmul(o, BKT[:, h // 2, 64 * (h % 2):64 * (h % 2) + 64], UV[s][:, h, :], start=True, stop=True)
                    m.then_inc(sem("M_ps"), 1)
                    for h in range(HEADS):
                        m = pe.matmul(banks[7][64 * s:64 * s + 64, h * 64:h * 64 + 64], PM[:, h, 64:128], UV[s][:, h, :],
                                      start=False, stop=(h == HEADS - 1), skip_group_check=True)
                    m.then_inc(sem("y_ps"), 1)
            pe.wait_ge(*reached("ldrow_ready"))
            pe.transpose(banks[0][:, 0:16], ldrow, ident[0:16, 0:16]).then_inc(*reach("dt_ps"))
            pe.wait_ge(sem("s5_loaded"), 96)
            for a in range(2):
                for r in range(4):
                    m = pe.transpose(banks[1 + a][0:64, r * P:(r + 1) * P], Craw[a][:, r, :], ident[:, :])
            m.then_inc(*reach("c_ps"))
            pe.wait_ge(*reached("v1_ready"))
            for a in range(2):
                for q4 in range(4):
                    n = 4 * a + q4
                    if n >= 2:
                        pe.wait_ge(sem("w1_evac"), n - 1)
                    for x in range(4):
                        m = pe.transpose(banks[3 + n % 2][:, x * P:(x + 1) * P], V1[a][:, 4 * q4 + x, :], ident[:, :])
                    m.then_inc(sem("w1_ps"), 1)
            pe.wait_ge(*reached("w2_ready"))
            for q4 in range(4):
                for h in range(2):
                    n = 2 * q4 + h
                    if q4 > 0:
                        pe.wait_ge(sem("kk_evac"), n - 1)
                    for x in range(4):
                        q = 4 * q4 + x
                        o = banks[5 + h][0:16, x * P:(x + 1) * P]
                        r = slice(64 * h, 64 * h + 64)
                        pe.matmul(o, Bbar[0][r, q, :], W2[0][r, q, 0:P], start=True, stop=False)
                        m = pe.matmul(o, Bbar[1][r, q, :], W2[1][r, q, 0:P], start=False, stop=True)
                    m.then_inc(sem("kk_ps"), 1)
            pe.wait_ge(sem("xg_loaded"), 16 * TAU)
            pe.wait_ge(sem("w1_evac"), 8)
            pe.wait_ge(sem("c_evac"), 16)
            for q4 in range(4):
                for a in range(2):
                    n = 2 * q4 + a
                    if n >= 4:
                        pe.wait_ge(sem("e_evac"), n - 3)
                    for x in range(4):
                        for h in range(2):
                            q = 4 * q4 + x
                            m = pe.matmul(banks[n % 4][64 * h:64 * h + 64, x * P:(x + 1) * P], W1[a][:, q, 64 * h:64 * h + 64],
                                          Xg[:, 2 * q + h, :], start=True, stop=True)
                    m.then_inc(sem("e_ps"), 1)
            pe.wait_ge(*reached("gn_done"))
            for i in range(TT):
                if i >= 2:
                    pe.wait_ge(sem("ymix_rwkv"), i - 1)
                for j in range(J):
                    m = pe.transpose(banks[4 + i % 2][:, j * P:(j + 1) * P], Yt[:, i, j * P:(j + 1) * P], ident[:, :])
                m.then_inc(sem("ymixT_ps"), 1)
            pe.wait_ge(sem("toe_loaded"), 16 * TAU)
            pe.wait_ge(*reached("sprev_ready"))
            pe.wait_ge(sem("e_evac"), 8)
            for q4 in range(4):
                for h in range(2):
                    n = 2 * q4 + h
                    if n >= 4:
                        pe.wait_ge(sem("gelu_done"), n - 3)
                    for x in range(4):
                        q = 4 * q4 + x
                        o = banks[n % 4][:, x * P:(x + 1) * P]
                        r = slice(64 * h, 64 * h + 64)
                        pe.matmul(o, Toe[:, 2 * q + h, :], Xg[:, 2 * q + h, :], start=True, stop=False)
                        pe.matmul(o, W2[0][r, q, GC:GC + P], Sprev[0].rearrange("p (q c) -> p q c", q=PAIRS)[r, q, :], start=False, stop=False)
                        m = pe.matmul(o, W2[1][r, q, GC:GC + P], Sprev[1].rearrange("p (q c) -> p q c", q=PAIRS)[r, q, :], start=False, stop=True)
                    m.then_inc(sem("y5_ps"), 1)
            pe.wait_ge(sem("wglu_loaded"), 16)
            pe.wait_ge(sem("zT_loaded"), 16)
            pe.wait_ge(sem("gelu_done"), 8)
            for m4 in range(4):
                for h in range(2):
                    n = 2 * m4 + h
                    if n >= 4:
                        pe.wait_ge(sem("glu_evac"), n - 3)
                    for k in range(4):
                        m = pe.matmul(banks[n % 4][:, :], wglu[:, k, m4 * P:(m4 + 1) * P], zT[:, k, 512 * h:512 * h + 512],
                                      start=(k == 0), stop=(k == 3))
                    m.then_inc(sem("glu_ps"), 1)
            pe.sem_inc(sem("mix_ps"), 4)
            pe.wait_ge(sem("wmix_loaded"), 16)
            pe.wait_ge(sem("glu_evac"), 8)
            pe.wait_ge(sem("ymix_rwkv"), TT)
            with pe.Fori(0, TT // 2) as ii:
                for s in range(2):
                    pe.wait_ge(sem("tok0_loaded") if s == 0 else sem("tok1_loaded"), ii * 16 + 16)
                    pe.wait_ge(sem("mix_added"), ii * 4 + (2 * s + 2))
                    for h in range(2):
                        for k in range(KT):
                            m = pe.matmul(banks[2 * s + h][:, :], tokring[s][:, k, :], wmix[:, k, 512 * h:512 * h + 512],
                                          start=(k == 0), stop=(k == KT - 1))
                        m.then_inc(sem("mix_ps"), 1)
            pe.sem_inc(sem("k_ps"), 2)
            norm_pe(pe, 8, TT)
            norm_pe(pe, 16, 2)
            pe.wait_ge(sem("hT_ready"), 4 + 2 * 18)
            with pe.Fori(0, KT // 2) as mm:
                for s in range(2):
                    pe.wait_ge(sem("wk_loaded0") if s == 0 else sem("wk_loaded1"), mm * 16 + 16)
                    pe.wait_ge(sem("kT_ready"), mm * 2 + (s + 1))
                    for k in range(KT):
                        m = pe.matmul(banks[s][:, 0:MEM], wkr[s][:, k, :], hM[:, k, :], start=(k == 0), stop=(k == KT - 1))
                    m.then_inc(sem("k_ps"), 1)
            pe.wait_ge(sem("wv_loaded"), 16)
            pe.wait_ge(sem("mix_added"), 4 + 2 * TT)
            for i in range(2):
                for h in range(2):
                    for k in range(KT):
                        m = pe.matmul(banks[2 + h + 2 * i][:, :], hM[:, k, i * P:(i + 1) * P], wvo[:, k, 512 * h:512 * h + 512],
                                      start=(k == 0), stop=(k == KT - 1))
                    m.then_inc(sem("v_ps"), 1)
            pe.wait_ge(sem("wq_loaded"), 16)
            pe.wait_ge(sem("kT_ready"), 2 + KT)
            pe.wait_ge(sem("vM_ready"), 4)

            def queries(t):
                for m in range(KT):
                    if m % 4 == 0:
                        pe.wait_ge(sem("qr_ready"), t * 2 + (m // 4 + 1))
                    for k in range(KT):
                        mm = pe.matmul(banks[m // 4][:, (m % 4) * P:(m % 4 + 1) * P], wq[:, k, m * P:(m + 1) * P], hB[:, k, ds(t * P, P)],
                                       start=(k == 0), stop=(k == KT - 1))
                    if m % 4 == 3:
                        mm.then_inc(sem("q_ps"), 1)

            def attend(t, s, last):
                pe.wait_ge(sem("qr_ready"), t * 2 + 4)
                pe.wait_ge(sem("p_ready"), t + 1)
                for h in range(XH):
                    for kk_ in range(2):
                        m = pe.matmul(banks[2 + h // 2][:, (h % 2) * MEM:(h % 2 + 1) * MEM], qr[s][:, 2 * h + kk_, :], kT[:, 2 * h + kk_, :],
                                      start=(kk_ == 0), stop=(kk_ == 1))
                m.then_inc(sem("s_ps"), 1)
                if not last:
                    queries(t + 1)
                pe.wait_ge(sem("p_ready"), t + 2)
                pe.wait_ge(sem("x_attn"), t * 2 + 4)
                for i in range(2):
                    for h in range(XH):
                        m = pe.transpose(banks[4 + i][:, h * P:(h + 1) * P], pr_[:, h, i * P:(i + 1) * P], ident[:, :])
                m.then_inc(sem("pT_ps"), 1)
                pe.wait_ge(sem("pT_ready"), t * 2 + 2)
                pe.wait_ge(sem("o_ready"), t * 2 + 2)
                for h in range(XH):
                    for dd in range(2):
                        c = 2 * h + dd
                        for i in range(2):
                            m = pe.matmul(banks[6 + c // 4][:, (c % 4) * P:(c % 4 + 1) * P], vM[:, i, c * P:(c + 1) * P], pT[:, i, h, :],
                                          start=(i == 0), stop=(i == 1))
                m.then_inc(sem("o_ps"), 1)
                pe.wait_ge(sem("o_ready"), t * 2 + 4)
                for h in range(2):
                    for k in range(KT):
                        m = pe.matmul(banks[4 + h][:, :], oR[s][:, k, :], wvo[:, k, 512 * h:512 * h + 512], start=(k == 0), stop=(k == KT - 1))
                    m.then_inc(sem("oproj_ps"), 1)

            queries(0)
            pe.wait_ge(sem("wo_loaded"), 16)
            with pe.Fori(0, TT // 2 - 1) as ii:
                for s in range(2):
                    attend(ii * 2 + s, s, False)
            attend(TT - 2, 0, False)
            attend(TT - 1, 1, True)
            norm_pe(pe, 18, TT)
            pe.wait_ge(sem("router_loaded"), 128)
            pe.wait_ge(sem("hT_ready"), 4 + 2 * 26)
            for i in range(TT):
                for k in range(KT):
                    m = pe.matmul(banks[0][:, i * 36:(i + 1) * 36], hB[:, k, i * P:(i + 1) * P], wrt[:, k, :], start=(k == 0), stop=(k == KT - 1))
            m.then_inc(*reach("logits_ps"))
            pe.wait_ge(*reached("marks_ready"))
            pe.wait_ge(*reached("consts_b"))
            pe.matmul(banks[1][:, 0:256], strictU[:, :], MS.rearrange("p i e -> p (i e)"), start=True, stop=False)
            pe.matmul(banks[1][:, 0:256], ones[:, :], MA.rearrange("p i e -> p (i e)"), start=False, stop=True)
            pe.matmul(banks[1][:, 256:288], ones[:, :], c32[0], start=True, stop=True).then_inc(*reach("ranks_ps"))
            pe.sem_inc(sem("xT_ps"), 4)
            pe.sem_inc(sem("up_ps"), 2)
            pe.sem_inc(sem("dn_ps"), 4)
            pe.sem_inc(sem("hidT_ps"), 1)

            def expert(s, n, ns):
                wg, wu, wd, xl = (sem("wg0"), sem("wu0"), sem("wd0"), sem("xb_loaded0")) if s == 0 else (sem("wg1"), sem("wu1"), sem("wd1"), sem("xb_loaded1"))
                pe.wait_ge(xl, ns * 16 + 16)
                for q in range(2):
                    pe.wait_ge(sem("xbT_ready"), n * 2 + (q + 1))
                    for k in range(4):
                        m = pe.transpose(banks[q][:, k * P:(k + 1) * P], xb[s][:, 4 * q + k:D:KT], ident[:, :])
                    m.then_inc(sem("xT_ps"), 1)
                pe.wait_ge(sem("xbT_ready"), n * 2 + 4)
                pe.wait_ge(wg, ns * 16 + 16)
                pe.wait_ge(sem("sg_ready"), n + 1)
                for k in range(KT):
                    m = pe.matmul(banks[2][:, :], xbT[s][:, k, :], WG[s][:, k, :], start=(k == 0), stop=(k == KT - 1))
                m.then_inc(sem("gate_ps"), 1)
                pe.wait_ge(wu, ns * 16 + 16)
                pe.wait_ge(sem("hid_ready"), n + 1)
                for k in range(KT):
                    m = pe.matmul(banks[3][:, :], xbT[s][:, k, :], WU[s][:, k, :], start=(k == 0), stop=(k == KT - 1))
                m.then_inc(sem("up_ps"), 1)
                pe.wait_ge(sem("hid_ready"), n + 2)
                pe.wait_ge(sem("hidT_ready"), n + 1)
                for k in range(4):
                    m = pe.transpose(banks[4][:, k * P:(k + 1) * P], hid[:, k:FE:4], ident[:, :])
                m.then_inc(sem("hidT_ps"), 1)
                pe.wait_ge(sem("hidT_ready"), n + 2)
                pe.wait_ge(wd, ns * 16 + 16)
                for h in range(2):
                    pe.wait_ge(sem("y_evac0") if h == 0 else sem("y_evac1"), n + 1)
                    for k in range(4):
                        m = pe.matmul(banks[5 + h][:, :], hidT[:, k, :], WD[s][:, k, 512 * h:512 * h + 512], start=(k == 0), stop=(k == 3))
                    m.then_inc(sem("dn_ps"), 1)

            with pe.Fori(0, NE // 2) as bb:
                for s in range(2):
                    expert(s, bb * 2 + s, bb)
            pe.wait_ge(*reached("slots_ready"))
            n_over = pe.value_load(nover_i[0:1, :], min_val=0, max_val=OVER)
            with pe.Fori(0, OVER) as o:
                with pe.If(o < n_over):
                    expert(0, o + NE, o + NE // 2)
                pe.nop()

        def norm_act(act, src, junk, base, tiles, use, stored=False, halves=None):
            with act.Fori(0, tiles) as i:
                if halves is not None:
                    act.wait_ge(halves, i * 2 + 6)
                act.activation(junk, src[:, ds(i, 1), :].rearrange("p o d -> p (o d)"), ACT.Square, accum_out=ss[:, ds(i, 1)]).then_inc(sem("ss_ready"), 1)
                act.drain()
            act.wait_ge(sem("ms_ready"), use)
            act.activation(rstd[:, 0:tiles], rstd[:, 0:tiles], ACT.Sqrt).then_inc(sem("rms_ready"), 1)
            act.wait_ge(sem("rstd_ready"), use)
            with act.Fori(0, tiles // 2) as i:
                for s in range(2):
                    act.wait_ge(sem("xs_free"), i * 2 + (base + s + 1))
                    if stored:
                        act.wait_ge(sem("xn_stored0") if s == 0 else sem("xn_stored1"), i * 16 + 16)
                    act.activation(xs[s], src[:, ds(i * 2 + s, 1), :].rearrange("p o (k d) -> p (o k) d", k=KT),
                                   ACT.Copy, scale=rstd[:, ds(i * 2 + s, 1)]).then_inc(sem("xs_ready"), 1)

        @block.scalar
        def _(act):
            act.wait_ge(*reached("pcol_ps"))
            act.activation(pcol[:, :], banks[7][:, 0:NROWS], ACT.Copy).then_inc(*reach("pcol_ready"))
            act.wait_ge(sem("x_loaded"), 16)
            norm_act(act, X, junk, 0, TT, 1)
            act.sem_inc(sem("z_evac"), 4)
            with act.Fori(0, 7) as mm:
                for s in range(2):
                    act.wait_ge(sem("pt_ready"), mm * 2 + (s + 1))
                    for h in range(2):
                        act.wait_ge(sem("z_done"), mm * 4 + (4 + 2 * s + h + 1))
                        act.activation(zbuf[s][:, 1 + 512 * h:513 + 512 * h], banks[2 * s + h][:, :], ACT.Copy).then_inc(sem("z_evac"), 1)
            for j in range(4):
                for h in range(2):
                    act.wait_ge(sem("z_done"), 4 + 28 + 2 * j + h + 1)
                    act.activation(uT[:, j, :].rearrange("p (a c) -> p a c", a=TAU)[:, :, 64 * h:64 * h + 64],
                                   banks[2 * (j % 2) + h][:, :].rearrange("p (c a) -> p a c", a=TAU), ACT.Copy).then_inc(sem("z_evac"), 1)
            act.wait_ge(sem("pt_ready"), 2 + 14)
            act.activation(PT[0:64, 12, :], PT[0:64, 12, :], ACT.Tanh)
            act.activation(PT[:, 13, :], PT[:, 13, :], ACT.Sigmoid)
            act.drain()
            act.activation(small[:, 63:64], small[:, 8:9], ACT.Copy).then_inc(*reach("dwda_ready"))
            for j in range(J):
                act.wait_ge(sem("rates_ps"), j + 1)
                if j > 0:
                    act.wait_ge(sem("elem_done"), j)
                for h in range(2):
                    act.activation(sig[:, 512 * h:512 * h + 512], banks[h][:, :], ACT.Sigmoid, bias=col("w0", j)).then_inc(sem("rates_ready"), 1)
                    act.activation(avec[:, 512 * h:512 * h + 512], banks[2 + h][:, :], ACT.Sigmoid, bias=col("a0", j)).then_inc(sem("rates_ready"), 1)
                act.wait_ge(sem("kk0_ready"), j + 1)
                act.activation(tmp, kk, ACT.Square).then_inc(sem("kk_sq"), 1)
                act.wait_ge(sem("kk_sum"), j + 1)
                act.wait_ge(sem("kk_sq"), j + 1)
                for h in range(2):
                    act.activation(tmp[:, 512 * h:512 * h + 512], banks[4 + h][:, :], ACT.Sqrt).then_inc(sem("kk_norm"), 1)
                act.wait_ge(sem("csum_ready"), j + 1)
                act.activation(gexp, csum, ACT.Exp, scale=-DECAY).then_inc(sem("gexp_ready"), 1)
                act.activation(ginv, csum, ACT.Exp, scale=DECAY).then_inc(sem("gexp_ready"), 1)
                act.wait_ge(sem("cprev_ready"), j + 1)
                act.activation(gprev, gprev, ACT.Exp, scale=-DECAY).then_inc(sem("gexp_ready"), 1)
            for i in range(TT):
                b = 4 * (i % 2)
                act.wait_ge(sem("tok_ps"), i + 1)
                act.activation(Gt[:, i, :], banks[b + 1][:, :], ACT.Copy).then_inc(sem("gates_evac"), 1)
                act.activation(rks[:, i, :], banks[b + 2][:, 0:8], ACT.Copy).then_inc(sem("gates_evac"), 1)
            act.sem_inc(sem("y_free"), 2)
            with act.Fori(0, NC // 2) as cc:
                for s in range(2):
                    act.wait_ge(sem("PM_ready"), cc * 4 + (2 * s + 2))
                    act.wait_ge(*reached("bd_zero"))
                    for p in range(2):
                        a = act.activation(LTbd[64 * p:64 * p + 64, :, 64 * p:64 * p + 64],
                                           PM[0:64, :, 0:64].rearrange("s (j q) t -> s q j t", q=2)[:, p, :, :], ACT.Copy)
                        pass
                    for lv in range(6):
                        act.wait_ge(sem("TS_new"), cc * 12 + (6 * s + lv + 1))
                        for p in range(2):
                            a = act.activation(TTbd[64 * p:64 * p + 64, :, 64 * p:64 * p + 64], TS[64 * p:64 * p + 64, 1, :, :], ACT.Copy)
                        a.then_inc(sem("TS_ready"), 1)
                    act.wait_ge(sem("U_ps"), cc * 2 + (s + 1))
                    for p in range(2):
                        act.activation(UV[s][0:64, :, :].rearrange("s (j q) t -> s q j t", q=2)[:, p, :, :],
                                       banks[6][64 * p:64 * p + 64, 0:256].rearrange("s (j v) -> s j v", j=J), ACT.Copy).then_inc(sem("U_ready"), 1)
                    act.wait_ge(sem("y_ps"), cc * 2 + (s + 1))
                    act.activation(Yt[64 * s:64 * s + 64, ds(cc, 1), :].rearrange("p o c -> p (o c)"),
                                   banks[7][64 * s:64 * s + 64, :], ACT.Copy).then_inc(sem("Y_ready"), 1)
                    act.wait_ge(sem("Y_ready"), cc * 2 + (s + 1))
                    act.sem_inc(sem("y_free"), 1)
            act.wait_ge(*reached("gn_centred"))
            act.activation(gtmp, unit(16, 4), ACT.Square).then_inc(*reach("gn_sq"))
            act.wait_ge(*reached("gn_var"))
            act.activation(gstat[:, 1, :], gstat[:, 1, :], ACT.Sqrt).then_inc(*reach("gn_std"))
            act.wait_ge(*reached("dt_ps"))
            act.activation(a5["dt"], banks[0][:, 0:16], ACT.Exp).then_inc(*reach("s5_dt"))
            act.wait_ge(*reached("s5_angle"))
            act.activation(a5["rho"], a5["are"], ACT.Exp)
            act.activation(a5["r8"], a5["are"], ACT.Exp, scale=float(TAU))
            act.activation(a5["sn"], a5["rr"], ACT.Sin)
            act.activation(a5["cs"], a5["ra"], ACT.Sin).then_inc(*reach("s5_trig"))
            act.wait_ge(*reached("c_ps"))
            act.wait_ge(sem("s5_loaded"), 96)
            for a in range(2):
                for h in range(2):
                    for r in range(4):
                        act.activation(Cst[a][64 * h:64 * h + 64, 4 * r:4 * r + 4, :],
                                       banks[1 + a][0:64, r * P:(r + 1) * P].rearrange("n (q h o) -> n h q o", h=2, o=GC)[:, h, :, :],
                                       ACT.Copy).then_inc(sem("c_evac"), 1)
            for n in range(8):
                act.wait_ge(sem("w1_ps"), n + 1)
                act.activation(W1[n // 4][:, 4 * (n % 4):4 * (n % 4) + 4, :].rearrange("p q x -> p (q x)"), banks[3 + n % 2][:, :], ACT.Copy).then_inc(sem("w1_evac"), 1)
            for n in range(8):
                act.wait_ge(sem("kk_ps"), n + 1)
                if n == 0:
                    act.wait_ge(*reached("gn_done"))
                q4, h = n // 2, n % 2
                act.activation(KK[:, 8 * q4 + h:8 * q4 + 8:2, :], banks[5 + h][0:16, :].rearrange("p (q x) -> p q x", q=4), ACT.Copy).then_inc(sem("kk_evac"), 1)
            for n in range(8):
                act.wait_ge(sem("e_ps"), n + 1)
                if n == 1:
                    act.wait_ge(sem("w1_evac"), 8)
                act.activation(E5[n % 2][:, 512 * (n // 2):512 * (n // 2) + 512], banks[n % 4][:, :], ACT.Copy).then_inc(sem("e_evac"), 1)
            for i in range(TT):
                act.wait_ge(sem("ymixT_ps"), i + 1)
                act.activation(ymixT[:, 0:4, i * P:(i + 1) * P], banks[4 + i % 2][:, :].rearrange("p (k t) -> p k t", k=4), ACT.Copy).then_inc(sem("ymix_rwkv"), 1)
            for n in range(8):
                act.wait_ge(sem("y5_ps"), n + 1)
                q4, h = n // 2, n % 2
                act.activation(y5.rearrange("p (g c) -> p g c", g=GROUPS)[:, 8 * q4 + h:8 * q4 + 8:2, :],
                               banks[n % 4][:, :].rearrange("p (q c) -> p q c", q=4), ACT.Gelu_apprx_tanh).then_inc(sem("gelu_done"), 1)
            for n in range(8):
                act.wait_ge(sem("glu_ps"), n + 1)
                if n >= 2:
                    act.wait_ge(sem("ymix_s5"), n - 1)
                act.activation(sglu[:, 512 * (n % 2):512 * (n % 2) + 512], banks[n % 4][:, :], ACT.Sigmoid, bias=col("b_glu", n // 2)).then_inc(sem("glu_evac"), 1)
            act.sem_inc(sem("kT_ready"), 2)
            act.sem_inc(sem("qr_ready"), 2)
            norm_act(act, Xr, junk2, 8, TT, 2, halves=sem("mix_added"))
            act.wait_ge(sem("xm_loaded"), 16)
            norm_act(act, Xm, junk2, 16, 2, 3)
            with act.Fori(0, KT // 2) as mm:
                for s in range(2):
                    act.wait_ge(sem("k_ps"), mm * 2 + (s + 3))
                    act.activation(kT[:, ds(mm * 2 + s, 1), :].rearrange("p o m -> p (o m)"), banks[s][:, 0:MEM], ACT.Copy).then_inc(sem("kT_ready"), 1)

            def queries_act(t, s):
                for h in range(2):
                    act.wait_ge(sem("q_ps"), t * 2 + (h + 1))
                    act.activation(qr[s][:, 4 * h:4 * h + 4, :].rearrange("p k t -> p (k t)"), banks[h][:, :], ACT.Copy).then_inc(sem("qr_ready"), 1)

            def attend_act(t, s, last):
                act.wait_ge(sem("smx_ready"), t + 1)
                for h in range(XH):
                    act.activation(pr_[:, h, :], banks[2 + h // 2][:, (h % 2) * MEM:(h % 2 + 1) * MEM], ACT.Exp, bias=smx[s][:, h:h + 1],
                                   scale=1.0 / 16.0, accum_out=ssum[s][:, h:h + 1]).then_inc(sem("exp_done"), 1)
                if not last:
                    queries_act(t + 1, 1 - s)
                act.wait_ge(sem("pT_ps"), t + 1)
                for i in range(2):
                    act.activation(pT[:, i, :, :].rearrange("p h t -> p (h t)"), banks[4 + i][:, :], ACT.Copy).then_inc(sem("pT_ready"), 1)
                act.wait_ge(sem("o_ps"), t + 1)
                for h in range(2):
                    act.activation(oR[s][:, 4 * h:4 * h + 4, :].rearrange("p k t -> p (k t)"), banks[6 + h][:, :], ACT.Copy).then_inc(sem("o_ready"), 1)

            act.sem_inc(sem("o_ready"), 2)
            queries_act(0, 0)
            with act.Fori(0, TT // 2 - 1) as ii:
                for s in range(2):
                    attend_act(ii * 2 + s, s, False)
            attend_act(TT - 2, 0, False)
            attend_act(TT - 1, 1, True)
            norm_act(act, Xr, junk, 18, TT, 4, stored=True, halves=sem("x_attn"))
            act.wait_ge(*reached("l1_ready"))
            act.activation(e8[0][:, :, 0:NG], e8[0][:, :, 0:NG], ACT.Exp).then_inc(*reach("exp_l1"))
            act.wait_ge(*reached("dv_ready"))
            act.activation(s8[6], s8[6], ACT.Exp).then_inc(*reach("exp_dv"))
            act.wait_ge(*reached("slots_ready"))
            act.sem_inc(sem("sg_ready"), 1)
            act.sem_inc(sem("hidT_ready"), 1)
            act.sem_inc(sem("y_evac0"), 1)
            act.sem_inc(sem("y_stored0"), 16)
            act.sem_inc(sem("y_stored1"), 16)

            def expert_act(s, n, ns):
                stored = sem("y_stored0") if s == 0 else sem("y_stored1")
                act.wait_ge(sem("gate_ps"), n + 1)
                act.wait_ge(sem("hid_ready"), n + 1)
                act.activation(sg, banks[2][:, :], ACT.Silu).then_inc(sem("sg_ready"), 1)
                act.wait_ge(sem("hidT_ps"), n + 2)
                act.wait_ge(sem("dn_ps"), n * 2 + 4)
                act.activation(hidT.rearrange("p k t -> p (k t)"), banks[4][:, :], ACT.Copy).then_inc(sem("hidT_ready"), 1)
                act.wait_ge(sem("dn_ps"), n * 2 + 5)
                act.wait_ge(stored, ns * 16 + 16)
                act.activation(ysb[s][:, 0:512], banks[5][:, :], ACT.Copy).then_inc(sem("y_evac0"), 1)
                act.wait_ge(sem("y_evac0"), n + 2)
                act.wait_ge(sem("y_evac1"), n + 2)
                act.dma_start(d_y[ds(n * P, P), :], ysb[s]).then_inc(stored, 16)

            with act.Fori(0, NE // 2) as bb:
                for s in range(2):
                    expert_act(s, bb * 2 + s, bb)
            n_over = act.value_load(nover_i[0:1, :], min_val=0, max_val=OVER)
            with act.Fori(0, OVER) as o:
                with act.If(o < n_over):
                    expert_act(0, o + NE, o + NE // 2)
                act.nop()
            act.wait_ge(sem("y_added"), 2 * TT)
            with act.Fori(0, TT) as i:
                act.activation(unit(16), Xr[:, ds(i, 1), :].rearrange("p o d -> p (o d)"), ACT.Square, accum_out=ss[:, ds(i, 1)]).then_inc(sem("ss_ready"), 1)
                act.drain()
            act.wait_ge(sem("ms_ready"), 5)
            act.activation(rstd[:, :], rstd[:, :], ACT.Sqrt).then_inc(sem("rms_ready"), 1)


        def norm_dve(dve, wname, dst, base, tiles, use):
            dve.wait_ge(sem("ss_ready"), base + tiles)
            dve.tensor_scalar(rstd[:, 0:tiles], ss[:, 0:tiles], 1.0 / D, EPS, ALU.mult, ALU.add).then_inc(sem("ms_ready"), 1)
            dve.wait_ge(sem("rms_ready"), use)
            dve.reciprocal(rstd[:, 0:tiles], rstd[:, 0:tiles]).then_inc(sem("rstd_ready"), 1)
            gain = cols(wname).rearrange("p (k o) -> p k o", o=1)
            with dve.Fori(0, tiles // 2) as i:
                for s in range(2):
                    for q in range(2):
                        dve.wait_ge(sem("xsT_ps"), i * 4 + (2 * base + 2 * s + q + 1))
                        if q == 1:
                            dve.sem_inc(sem("xs_free"), 1)
                        dve.tensor_tensor(dst[:, 4 * q:4 * q + 4, ds(i * 256 + s * 128, P)],
                                          banks[4 + 2 * s + q][:, :].rearrange("p (k t) -> p k t", k=4),
                                          gain[:, 4 * q:4 * q + 4, :].to_broadcast((P, 4, P)), ALU.mult).then_inc(sem("hT_ready"), 1)

        @block.vector
        def _(dve):
            dve.sem_inc(sem("hT_ready"), 4)
            dve.sem_inc(sem("xs_free"), 2)
            dve.sem_inc(sem("pt_ready"), 2)
            for z in zbuf:
                dve.memset(z[:, 0:1], 0.0)
            dve.wait_ge(*reached("pcol_ready"))
            norm_dve(dve, "norm_mix_w", hT, 0, TT, 1)
            dve.tensor_scalar(omka[:, :], cols("k_a"), -1.0, 1.0, ALU.mult, ALU.add)
            dve.memset(rkc[:, :, :], 0.0)
            dve.drain()
            for p in range(2):
                m = dve.tensor_copy(rkc[64 * p:64 * p + 64, :, p:p + 1],
                                cols("r_k")[64 * p:64 * p + 64, :].rearrange("p (j o) -> p j o", o=1))
            m.then_inc(*reach("rkc_ready"))
            with dve.Fori(0, 7) as mm:
                for s in range(2):
                    dve.wait_ge(sem("z_evac"), mm * 4 + (4 + 2 * s + 2))
                    dve.tensor_tensor(shift_d, zbuf[s][:, 0:1024], zbuf[s][:, 1:1025], ALU.subtract)
                    dve.drain()
                    dve.scalar_tensor_tensor(PT[:, ds(mm * 2 + s, 1), :].rearrange("p o t -> p (o t)"), shift_d,
                                             cols("mu_shift")[:, ds(mm * 2 + s, 1)], zbuf[s][:, 1:1025], ALU.mult, ALU.add
                                             ).then_inc(sem("pt_ready"), 1)
                    dve.drain()
            dve.wait_ge(sem("pt_ready"), 16)
            dve.wait_ge(*reached("reset_ready"))
            dve.wait_ge(sem("y_zeroed"), 16)
            for j in range(J):
                ch = lambda v: v.rearrange("p (c x) -> p c x", x=CH)
                r, k = PT[:, j, :], PT[:, 4 + j, :]
                dve.tensor_scalar(kk, k, col("k_k", j), None, ALU.mult).then_inc(sem("kk0_ready"), 1)
                dve.wait_ge(sem("rates_ready"), 4 * j + 4)
                dve.tensor_tensor_scan(csum, reset, sig, 0.0, ALU.mult, ALU.add).then_inc(sem("csum_ready"), 1)
                dve.wait_ge(sem("csum_ready"), j + 1)
                dve.tensor_tensor(gprev, csum, sig, ALU.subtract).then_inc(sem("cprev_ready"), 1)
                dve.wait_ge(sem("cprev_ready"), j + 1)
                dve.tensor_scalar(sig, avec, col("k_a", j), omka[:, j:j + 1], ALU.mult, ALU.add)
                dve.drain()
                dve.tensor_tensor(k, k, sig, ALU.mult)
                dve.wait_ge(sem("kk_norm"), 2 * j + 2)
                dve.tensor_scalar(tmp, tmp, 1e-12, None, ALU.max)
                dve.drain()
                dve.reciprocal(tmp, tmp)
                dve.drain()
                dve.tensor_tensor(kk, kk, tmp, ALU.mult)
                dve.wait_ge(sem("gexp_ready"), 3 * j + 3)
                dve.drain()
                dve.scalar_tensor_tensor(AR[:, j, :, 0:64], ch(kk), -1.0, ch(gprev), ALU.mult, ALU.mult)
                dve.tensor_tensor(AR[:, j, :, 64:128], ch(r), ch(gexp), ALU.mult)
                dve.tensor_tensor(avec, avec, kk, ALU.mult)
                dve.tensor_tensor(BK[:, j, :, 64:128], ch(k), ch(ginv), ALU.mult)
                dve.drain()
                dve.tensor_tensor(BK[:, j, :, 0:64], ch(avec), ch(ginv), ALU.mult)
                dve.tensor_tensor(r, r, k, ALU.mult)
                dve.tensor_copy(gcol[:, :, j:j + 1], ch(gexp)[:, :, 63:64]).then_inc(sem("elem_done"), 1)
                dve.drain()
            for i in range(TT):
                dve.wait_ge(sem("tok_ps"), i + 1)
                if i == 0:
                    dve.wait_ge(sem("elem_done"), J)
                dve.tensor_copy(Vt[:, i, :], banks[4 * (i % 2)][:, :]).then_inc(sem("values_evac"), 1)
            dve.wait_ge(*reached("bd_zero"))
            dve.wait_ge(*reached("consts_b"))
            dve.sem_inc(sem("Z_ready"), 1)
            heads = lambda m, n: m.rearrange("p (o x) -> p o x", o=1).to_broadcast((m.shape[0], n, m.shape[1]))
            with dve.Fori(0, NC // 2) as cc:
                for s in range(2):
                    dve.wait_ge(sem("y_free"), cc * 2 + (s + 2))
                    for q in range(2):
                        dve.wait_ge(sem("pm_ps"), cc * 4 + (2 * s + q + 1))
                        dve.tensor_tensor(PM[:, 4 * q:4 * q + 4, :], banks[q][:, :].rearrange("p (h x) -> p h x", h=4),
                                          heads(pmask[:, :], 4), ALU.mult).then_inc(sem("PM_ready"), 1)
                    dve.wait_ge(sem("L_ps"), cc * 2 + (s + 1))
                    dve.tensor_tensor(TS[:, 0, :, :], banks[2][:, 0:256].rearrange("p (j x) -> p j x", j=J), heads(lmask[:, 0, :], J), ALU.mult)
                    dve.wait_ge(sem("PM_ready"), cc * 4 + (2 * s + 2))
                    for p in range(2):
                        dve.tensor_tensor(TS[64 * p:64 * p + 64, 1, :, :], PM[0:64, p:HEADS:2, 0:64], heads(lmask1T[0:64, :], J), ALU.mult)
                    dve.drain()
                    dve.tensor_tensor(TS.rearrange("p a j x -> p (a j) x"), TS.rearrange("p a j x -> p (a j) x"), heads(eye[:, :], 2 * J), ALU.add).then_inc(sem("TS_new"), 1)
                    dve.wait_ge(sem("bkt_ps"), cc * 2 + (s + 1))
                    dve.tensor_copy(BKT.rearrange("p j x -> p (j x)"), banks[3][:, :])
                    for lv in range(1, 6):
                        dve.wait_ge(sem("LxT_ps"), cc * 10 + (5 * s + lv))
                        dve.tensor_tensor(Xst, banks[4][:, 0:256].rearrange("p (j x) -> p j x", j=J), heads(lmask[:, lv, :], J), ALU.mult).then_inc(sem("Xst_ready"), 1)
                        dve.wait_ge(sem("dT_ps"), cc * 10 + (5 * s + lv))
                        dve.wait_ge(sem("TS_new"), cc * 12 + (6 * s + lv))
                        v = TS.rearrange("p a j x -> p (a j x)")
                        dve.tensor_tensor(v, v, banks[5][:, :], ALU.add).then_inc(sem("TS_new"), 1)
                        dve.drain()
                    dve.wait_ge(sem("Q_ps"), cc * 2 + (s + 1))
                    dve.tensor_copy(Qst.rearrange("p j x -> p (j x)"), banks[4][:, 256:512]).then_inc(sem("Q_ready"), 1)
                    dve.wait_ge(sem("M_ps"), cc * 2 + (s + 1))
                    dve.tensor_tensor(Ztmp, Zst, banks[6][:, 256:512].rearrange("p (j x) -> p j x", j=J), ALU.add)
                    dve.drain()
                    g = gcol[:, ds(cc * 2 + s, 1), :].rearrange("p o j -> p (o j)").rearrange("p (j o) -> p j o", o=1)
                    dve.tensor_tensor(Zst, Ztmp, g.to_broadcast((P, J, 64)), ALU.mult)
                    for p in range(2):
                        gp = gcol[64 * p:64 * p + 64, ds(cc * 2 + s, 1), :].rearrange("p o j -> p (o j)").rearrange("p (j o) -> p j o", o=1)
                        m = dve.tensor_tensor(Zbd[64 * p:64 * p + 64, :, 64 * p:64 * p + 64], Ztmp[64 * p:64 * p + 64, :, :],
                                              gp.to_broadcast((64, J, 64)), ALU.mult)
                    m.then_inc(sem("Z_ready"), 1)
                    dve.drain()
            act_y = unit(16, 4)
            Y3 = act_y.rearrange("p (g x) -> p g x", x=HD)
            bc = lambda v: v.rearrange("p (g o) -> p g o", o=1).to_broadcast((P, TT * HEADS, HD))

            def tt(o, a, b, op):
                dve.tensor_tensor(o, a, b, op)
                dve.drain()

            def tsc(o, a, s1, s2, o1, o2=None):
                if o2 is None:
                    dve.tensor_scalar(o, a, s1, None, o1)
                else:
                    dve.tensor_scalar(o, a, s1, s2, o1, o2)
                dve.drain()

            dve.wait_ge(sem("Y_ready"), NC)
            dve.tensor_reduce(gstat[:, 0, :], Y3, AX_X, ALU.add)
            dve.drain()
            tsc(gstat[:, 0, :], gstat[:, 0, :], 1.0 / HD, None, ALU.mult)
            dve.tensor_tensor(Y3, Y3, bc(gstat[:, 0, :]), ALU.subtract).then_inc(*reach("gn_centred"))
            Vg = unit(12, 4).rearrange("p (g x) -> p g x", x=HD)
            tt(Vg, Vg, bc(rks.rearrange("p i h -> p (i h)")), ALU.mult)
            dve.wait_ge(*reached("gn_sq"))
            dve.tensor_reduce(gstat[:, 1, :], gtmp.rearrange("p (g x) -> p g x", x=HD), AX_X, ALU.add)
            dve.drain()
            dve.tensor_scalar(gstat[:, 1, :], gstat[:, 1, :], 1.0 / HD, 64e-5, ALU.mult, ALU.add).then_inc(*reach("gn_var"))
            dve.wait_ge(*reached("gn_std"))
            dve.reciprocal(gstat[:, 2, :], gstat[:, 1, :])
            dve.drain()
            tt(Y3, Y3, bc(gstat[:, 2, :]), ALU.mult)
            ln = lambda a: lnwb[:, 512 * a:512 * a + 512].rearrange("p (o c) -> p o c", o=1).to_broadcast((P, TT, 512))
            dve.wait_ge(sem("ln_loaded"), 32)
            tt(Yt, Yt, ln(0), ALU.mult)
            tt(Yt, Yt, ln(1), ALU.add)
            tt(Yt, Yt, Vt, ALU.add)
            dve.tensor_tensor(Yt, Yt, Gt, ALU.mult).then_inc(*reach("gn_done"))
            dve.drain()
            dve.wait_ge(sem("s5_loaded"), 96)
            dve.tensor_copy(ldrow.rearrange("p (h n) -> p h n", h=2), ldt.rearrange("p (h o) -> p h o", o=1).to_broadcast((16, 2, NS))).then_inc(*reach("ldrow_ready"))
            lre, lim = cols("s5_lam_re"), cols("s5_lam_im")
            A = a5
            dve.wait_ge(*reached("s5_dt"))
            tt(A["are"], lre, A["dt"], ALU.mult)
            tt(A["th"], lim, A["dt"], ALU.mult)
            tsc(A["kr"], A["th"], 1.0 / TWO_PI, None, ALU.mult)
            tsc(A["kr"], A["kr"], 12582912.0, None, ALU.add)
            tsc(A["kr"], A["kr"], -12582912.0, None, ALU.add)
            c1 = 6.28125
            c2 = float(np.float32(np.round((TWO_PI - c1) * 2 ** 20) / 2 ** 20))
            c3 = float(np.float32(TWO_PI - c1 - c2))
            dve.scalar_tensor_tensor(A["rr"], A["kr"], -c1, A["th"], ALU.mult, ALU.add)
            dve.drain()
            for c in (c2, c3):
                dve.scalar_tensor_tensor(A["rr"], A["kr"], -c, A["rr"], ALU.mult, ALU.add)
                dve.drain()
            tsc(A["rr"], A["rr"], 3.1415925, -3.1415925, ALU.min, ALU.max)
            dve.scalar_tensor_tensor(A["ra"], A["rr"], -1.0, A["rr"], ALU.mult, ALU.min)
            dve.drain()
            dve.tensor_scalar(A["ra"], A["ra"], float(np.pi / 2), None, ALU.add).then_inc(*reach("s5_angle"))
            dve.wait_ge(*reached("s5_trig"))
            tt(A["lr"], A["rho"], A["cs"], ALU.mult)
            tt(A["li"], A["rho"], A["sn"], ALU.mult)

            def cmul(o, a, b, t, conj=False):
                dve.tensor_tensor(t[0], a[0], b[0], ALU.mult)
                dve.tensor_tensor(t[1], a[1], b[1], ALU.mult)
                dve.tensor_tensor(t[2], a[0], b[1], ALU.mult)
                dve.tensor_tensor(t[3], a[1], b[0], ALU.mult)
                dve.drain()
                dve.tensor_tensor(o[0], t[0], t[1], ALU.add if conj else ALU.subtract)
                dve.tensor_tensor(o[1], t[2], t[3], ALU.subtract if conj else ALU.add)
                dve.drain()

            T4 = [A["t1"], A["t2"], A["t3"], A["t4"]]
            tsc(A["nr"], A["lr"], -1.0, None, ALU.add)
            tt(A["t1"], lre, lre, ALU.mult)
            tt(A["t2"], lim, lim, ALU.mult)
            tt(A["den"], A["t1"], A["t2"], ALU.add)
            dve.reciprocal(A["den"], A["den"])
            dve.drain()
            cmul((A["cr"], A["ci"]), (lre, lim), (A["nr"], A["li"]), T4, conj=True)
            tt(A["cr"], A["cr"], A["den"], ALU.mult)
            tt(A["ci"], A["ci"], A["den"], ALU.mult)
            q_ = lambda v, n: v.rearrange("p (q o) -> p q o", o=1).to_broadcast((P, PAIRS, n))
            tmp4 = [Rtab[:, 256 * i:256 * i + 256].rearrange("p (q i) -> p q i", q=PAIRS) for i in range(4)]
            cmul(Bbar, (q_(A["cr"], GC), q_(A["ci"], GC)), Braw, tmp4)
            dve.memset(pw[0][:, 0, :], 1.0)
            dve.memset(pw[1][:, 0, :], 0.0)
            dve.tensor_copy(pw[0][:, 1, :], A["lr"])
            dve.tensor_copy(pw[1][:, 1, :], A["li"])
            dve.drain()
            for n in range(2, TAU + 1):
                cmul((pw[0][:, n, :], pw[1][:, n, :]), (pw[0][:, n - 1, :], pw[1][:, n - 1, :]), (A["lr"], A["li"]), T4)
            dve.wait_ge(sem("c_evac"), 16)
            def kq(v, k0, n, rev=False):
                return v[:, k0:k0 + n, :].rearrange("p k (q o) -> p q k o", o=1).to_broadcast((P, PAIRS, n, GC))
            def qx(v, n):
                return v.rearrange("p q (o x) -> p q o x", o=1).to_broadcast((P, PAIRS, n, GC))
            w4 = lambda v: v.rearrange("p q (k x) -> p q k x", x=GC)
            sc = [arena[:, 42 * 1024 + 2304 * i:42 * 1024 + 2304 * (i + 1)].rearrange("p (q k x) -> p q k x", q=PAIRS, k=9) for i in range(2)]
            for a in range(2):
                dve.tensor_tensor(w4(W2[a]), kq(pw[0], 0, 9), qx(Cst[a], 9), ALU.mult)
                dve.tensor_tensor(sc[0], kq(pw[1], 0, 9), qx(Cst[1 - a], 9), ALU.mult)
                dve.drain()
                if a == 0:
                    tt(w4(W2[0]), w4(W2[0]), sc[0], ALU.subtract)
                else:
                    dve.scalar_tensor_tensor(W2[1].rearrange("p q x -> p (q x)"), W2[1].rearrange("p q x -> p (q x)"), -1.0,
                                             sc[0].rearrange("p q k x -> p (q k x)"), ALU.mult, ALU.subtract).then_inc(*reach("w2_ready"))
                    dve.drain()
            for a in range(2):
                for k in range(TAU):
                    dve.tensor_copy(pwr[a][:, k, :], pw[a][:, TAU - 1 - k, :])
            dve.drain()
            sv = unit(42, 2).rearrange("p (q k x) -> p q k x", q=PAIRS, k=TAU)
            for a in range(2):
                dve.tensor_tensor(w4(V1[a]), kq(pwr[0], 0, 8), qx(Bbar[a], 8), ALU.mult)
                dve.tensor_tensor(sv, kq(pwr[1], 0, 8), qx(Bbar[1 - a], 8), ALU.mult)
                dve.drain()
                m = dve.tensor_tensor(w4(V1[a]), w4(V1[a]), sv, ALU.subtract if a == 0 else ALU.add)
                dve.drain()
            m.then_inc(*reach("v1_ready"))
            dve.wait_ge(sem("kk_evac"), 8)
            d3 = arena[0:16, 44 * 1024:44 * 1024 + 512].rearrange("p (g x) -> p g x", g=GROUPS)
            tt(d3, ident[0:16, 0:16].rearrange("p (o x) -> p o x", o=1).to_broadcast((16, GROUPS, GC)),
               s5d.rearrange("p (g o) -> p g o", o=1).to_broadcast((16, GROUPS, GC)), ALU.mult)
            dve.tensor_tensor(KK[:, :, 0:GC], KK[:, :, 0:GC], d3, ALU.add).then_inc(*reach("kk_ready"))
            dve.drain()
            p1, p2 = ("pr", "pi"), ("pr2", "pi2")
            cmul((A["pr"], A["pi"]), (A["cs"], A["sn"]), (A["cs"], A["sn"]), T4)
            cmul((A["pr2"], A["pi2"]), (A["pr"], A["pi"]), (A["pr"], A["pi"]), T4)
            cmul((A["pr"], A["pi"]), (A["pr2"], A["pi2"]), (A["pr2"], A["pi2"]), T4)
            tg = [v.rearrange("p (q c) -> p q c", q=PAIRS) for v in trig]
            dve.memset(tg[0][:, :, 0:1], 1.0)
            dve.memset(tg[1][:, :, 0:1], 0.0)
            dve.drain()
            n = 1
            while n < SC:
                b = [v.rearrange("p (q o) -> p q o", o=1).to_broadcast((P, PAIRS, n)) for v in (A[p1[0]], A[p1[1]])]
                t = [unit(1 + i)[:, 0:16 * n].rearrange("p (q c) -> p q c", q=PAIRS) for i in range(4)]
                cmul([v[:, :, n:2 * n] for v in tg], [v[:, :, 0:n] for v in tg], b, t)
                cmul([A[x] for x in p2], [A[x] for x in p1], [A[x] for x in p1], T4)
                p1, p2 = p2, p1
                n *= 2
            dve.wait_ge(sem("w1_evac"), 8)
            dve.tensor_copy(Rtab.rearrange("p (q c) -> p q c", q=PAIRS), q_(A["r8"], SC))
            dve.drain()
            dve.memset(Rtab.rearrange("p (q c) -> p q c", q=PAIRS)[:, :, 0:1], 0.0)
            dve.wait_ge(sem("e_evac"), 8)
            dve.wait_ge(sem("toe_loaded"), 16 * TAU)
            z4 = [zst[0], zst[1], rot[0], rot[1]]
            cmul((E5[0], E5[1]), (trig[0], trig[1]), (E5[0], E5[1]), z4, conj=True)
            for a in range(2):
                dve.tensor_tensor_scan(zst[a], Rtab, E5[a], 0.0, ALU.mult, ALU.add)
            dve.drain()
            tg1 = [v.rearrange("p (q c) -> p q c", q=PAIRS)[:, :, 0:SC - 1] for v in (*trig, *zst, *Sprev, *E5)]
            sh = [v.rearrange("p (q c) -> p q c", q=PAIRS) for v in Sprev]
            for o, c in enumerate((ALU.subtract, ALU.add)):
                dve.tensor_tensor(tg1[6], tg1[0], tg1[2 + o], ALU.mult)
                dve.tensor_tensor(tg1[7], tg1[1], tg1[3 - o], ALU.mult)
                dve.memset(sh[o][:, :, 0:1], 0.0)
                dve.drain()
                m = dve.tensor_tensor(sh[o][:, :, 1:SC], tg1[6], tg1[7], c)
                if o == 1:
                    m.then_inc(*reach("sprev_ready"))
                dve.drain()
            for n in range(8):
                m4, h = n // 2, n % 2
                dve.wait_ge(sem("glu_evac"), n + 1)
                if n == 0:
                    dve.wait_ge(sem("zT_loaded"), 16)
                o = ymixT[:, 4 + m4, :].rearrange("p (c a) -> p a c", a=TAU)[:, 4 * h:4 * h + 4, :]
                dve.tensor_tensor(o, sglu[:, 512 * (n % 2):512 * (n % 2) + 512].rearrange("p (a c) -> p a c", a=4),
                                  zT[:, m4, 512 * h:512 * h + 512].rearrange("p (a c) -> p a c", a=4), ALU.mult).then_inc(sem("ymix_s5"), 1)
            dve.sem_inc(sem("mix_added"), 4)
            dve.wait_ge(sem("xr_loaded"), 16)
            with dve.Fori(0, TT // 2) as ii:
                for s in range(2):
                    for h in range(2):
                        dve.wait_ge(sem("mix_ps"), ii * 4 + (4 + 2 * s + h + 1))
                        v = Xr[:, ds(ii * 2 + s, 1), 512 * h:512 * h + 512].rearrange("p o d -> p (o d)")
                        dve.tensor_tensor(v, v, banks[2 * s + h][:, :], ALU.add).then_inc(sem("mix_added"), 1)
            dve.wait_ge(sem("mix_added"), 4 + 2 * TT)
            norm_dve(dve, "norm_xattn_w", hB, 8, TT, 2)
            norm_dve(dve, "norm_mem_w", hM, 16, 2, 3)
            for i in range(2):
                for h in range(2):
                    dve.wait_ge(sem("v_ps"), 2 * i + h + 1)
                    dve.tensor_copy(vM[:, i, 512 * h:512 * h + 512], banks[2 + h + 2 * i][:, :]).then_inc(sem("vM_ready"), 1)
            dve.sem_inc(sem("p_ready"), 1)
            dve.sem_inc(sem("x_attn"), 4)

            def attend_dve(t, s):
                dve.wait_ge(sem("s_ps"), t + 1)
                for h in range(2):
                    dve.tensor_reduce(smx[s][:, 2 * h:2 * h + 2], banks[2 + h][:, :].rearrange("p (h m) -> p h m", h=2), AX_X, ALU.max)
                dve.drain()
                dve.tensor_scalar(smx[s], smx[s], -1.0 / 16.0, None, ALU.mult).then_inc(sem("smx_ready"), 1)
                dve.wait_ge(sem("exp_done"), t * 4 + 4)
                dve.reciprocal(ssum[s], ssum[s])
                dve.drain()
                dve.tensor_tensor(pr_, pr_, ssum[s].rearrange("p (h o) -> p h o", o=1).to_broadcast((P, XH, MEM)), ALU.mult).then_inc(sem("p_ready"), 1)
                for h in range(2):
                    dve.wait_ge(sem("oproj_ps"), t * 2 + (h + 1))
                    v = Xr[:, ds(t, 1), 512 * h:512 * h + 512].rearrange("p o d -> p (o d)")
                    dve.tensor_tensor(v, v, banks[4 + h][:, :], ALU.add).then_inc(sem("x_attn"), 1)

            with dve.Fori(0, TT // 2) as ii:
                for s in range(2):
                    attend_dve(ii * 2 + s, s)
            dve.sem_inc(sem("xn_stored0"), 16)
            dve.sem_inc(sem("xn_stored1"), 16)
            norm_dve(dve, "norm_moe_w", hB, 18, TT, 4)
            dve.wait_ge(*reached("logits_ps"))
            dve.wait_ge(*reached("router_consts"))
            b3 = lambda v, n: v.rearrange("p (o e) -> p o e", o=1).to_broadcast((P, TT, n))
            c3 = lambda v, n: v.rearrange("p (i o) -> p i o", o=1).to_broadcast((P, TT, n))
            tt(LG, banks[0][:, 0:288].rearrange("p (i e) -> p i e", i=TT), b3(brt, 36), ALU.add)
            l1 = LG[:, :, 0:NG]

            def red(o, a, op):
                dve.tensor_reduce(o, a, AX_X, op)
                dve.drain()

            def first_of_max(o, best, a, n, iob, t):
                red(best, a, ALU.max)
                tt(t, a, c3(best, n), ALU.is_equal)
                tsc(t, t, -2.0 * EPG, None, ALU.mult)
                tt(t, t, b3(iob, n), ALU.add)
                red(o, t, ALU.min)

            grp, m1, s1, i0, v0, i1, v1 = s8[0], s8[1], s8[2], s8[3], s8[4], s8[5], s8[7]
            first_of_max(grp, m1, l1, NG, io4b, e8[1][:, :, 0:NG])
            tsc(grp, grp, float(EPG), None, ALU.add)
            dve.tensor_tensor(e8[0][:, :, 0:NG], l1, c3(m1, NG), ALU.subtract).then_inc(*reach("l1_ready"))
            tt(e8[1][:, :, 0:NG], b3(io32[:, 0:NG], NG), c3(grp, NG), ALU.is_equal)
            tt(l2.rearrange("p i (g e) -> p i g e", g=NG), LG[:, :, NG:36].rearrange("p i (g e) -> p i g e", g=NG),
               e8[1][:, :, 0:NG].rearrange("p i (g o) -> p i g o", o=1).to_broadcast((P, TT, NG, EPG)), ALU.mult)
            red(e8[2], l2.rearrange("p i (g e) -> p i e g", g=NG), ALU.add)
            first_of_max(i0, v0, e8[2], EPG, io8b, e8[3])
            tt(e8[3], b3(io32[:, 0:EPG], EPG), c3(i0, EPG), ALU.is_equal)
            tsc(e8[3], e8[3], -3.0e38, None, ALU.mult)
            tt(e8[2], e8[2], e8[3], ALU.add)
            first_of_max(i1, v1, e8[2], EPG, io8b, e8[3])
            dve.tensor_tensor(s8[6], v1, v0, ALU.subtract).then_inc(*reach("dv_ready"))
            dve.drain()
            dve.wait_ge(*reached("exp_dv"))
            red(s1, e8[0][:, :, 0:NG], ALU.add)
            tsc(s8[8], s8[6], 1.0, None, ALU.add)
            tt(s8[8], s8[8], s1, ALU.mult)
            dve.reciprocal(gates[:, 0:8], s8[8])
            dve.drain()
            tt(gates[:, 8:16], gates[:, 0:8], s8[6], ALU.mult)
            tsc(grp, grp, float(EPG), None, ALU.mult)
            for a, i in enumerate((i0, i1)):
                tt(i, i, grp, ALU.add)
                tt(O2[a], b3(io32, NE), c3(i, NE), ALU.is_equal)
            tt(MS, O2[0], O2[1], ALU.add)
            dve.memset(MA[:, 0, :], 0.0)
            dve.drain()
            for i in range(1, TT):
                tt(MA[:, i, :], MA[:, i - 1, :], MS[:, i - 1, :], ALU.add)
            dve.tensor_tensor(c32[0], MA[:, TT - 1, :], MS[:, TT - 1, :], ALU.add).then_inc(*reach("marks_ready"))
            dve.wait_ge(*reached("ranks_ps"))
            tt(cmpb, banks[1][:, 256:288].rearrange("p (e o) -> p e o", o=1).to_broadcast((P, NE, 7)),
               ioM.rearrange("p (o m) -> p o m", o=1).to_broadcast((P, NE, 7)), ALU.is_gt)
            red(c32[1], cmpb, ALU.add)
            dve.tensor_tensor_scan(c32[2], ones[:, 0:NE], c32[1], 0.0, ALU.mult, ALU.add)
            dve.drain()
            tt(c32[3], c32[2], c32[1], ALU.subtract)
            dve.scalar_tensor_tensor(c32[4], c32[3], float(P), io128, ALU.mult, ALU.subtract)
            dve.drain()
            tsc(c32[4], c32[4], float(NE * P - P), None, ALU.add)
            tt(RK, banks[1][:, 0:256].rearrange("p (i e) -> p i e", i=TT), b3(io128, NE), ALU.add)
            tsc(RT, banks[1][:, 0:256].rearrange("p (i e) -> p i e", i=TT), float(P), None, ALU.is_ge)
            tt(RT, RT, b3(c32[4], NE), ALU.mult)
            tt(RK, RK, RT, ALU.add)
            for a in range(2):
                tt(RT, RK, O2[a], ALU.mult)
                red(s8[9 + a], RT, ALU.add)
                dve.tensor_copy(slots_i[:, 8 * a:8 * a + 8], s8[9 + a])
            tt(cmpo, c32[2].rearrange("p (o e) -> p o e", o=1).to_broadcast((P, OVER, NE)),
               ioO.rearrange("p (b o) -> p b o", o=1).to_broadcast((P, OVER, NE)), ALU.is_le)
            red(e8[4].rearrange("p i e -> p (i e)")[:, 0:OVER], cmpo, ALU.add)
            tsc(e8[4].rearrange("p i e -> p (i e)")[:, 0:OVER], e8[4].rearrange("p i e -> p (i e)")[:, 0:OVER], float(NE - 1), None, ALU.min)
            dve.tensor_copy(eid_i, e8[4].rearrange("p i e -> p (i e)")[:, 0:OVER])
            dve.tensor_copy(nover_i, c32[2][:, NE - 1:NE])
            dve.drain()
            dve.tensor_copy(eid_i[:, 0:1], eid_i[:, 0:1]).then_inc(*reach("slots_ready"))
            dve.drain()
            dve.sem_inc(sem("xbT_ready"), 2)
            dve.sem_inc(sem("hid_ready"), 1)
            dve.sem_inc(sem("y_evac1"), 1)
            gp = gainp.rearrange("p (k o) -> p k o", o=1)

            def expert_dve(s, n, ns, lead):
                dve.wait_ge(sem("up_ps"), n + lead)
                for q in range(2):
                    dve.wait_ge(sem("xT_ps"), n * 2 + (4 + q + 1))
                    dve.tensor_tensor(xbT[s][:, 4 * q:4 * q + 4, :], banks[q][:, :].rearrange("p (k t) -> p k t", k=4),
                                      gp[:, 4 * q:4 * q + 4, :].to_broadcast((P, 4, P)), ALU.mult).then_inc(sem("xbT_ready"), 1)
                dve.wait_ge(sem("sg_ready"), n + 2)
                dve.wait_ge(sem("up_ps"), n + 3)
                dve.wait_ge(sem("hidT_ps"), n + 1)
                dve.tensor_tensor(hid, sg, banks[3][:, :], ALU.mult).then_inc(sem("hid_ready"), 1)
                dve.wait_ge(sem("dn_ps"), n * 2 + 6)
                dve.wait_ge(sem("y_stored0") if s == 0 else sem("y_stored1"), ns * 16 + 16)
                dve.tensor_copy(ysb[s][:, 512:1024], banks[6][:, :]).then_inc(sem("y_evac1"), 1)

            with dve.Fori(0, NE // 2) as bb:
                for s in range(2):
                    expert_dve(s, bb * 2 + s, bb, 1)
            n_over = dve.value_load(nover_i[0:1, :], min_val=0, max_val=OVER)
            with dve.Fori(0, OVER) as o:
                with dve.If(o < n_over):
                    expert_dve(0, o + NE, o + NE // 2, 2)
                dve.nop()
            for i in range(TT):
                dve.wait_ge(sem("yg_loaded0") if i % 2 == 0 else sem("yg_loaded1"), 32 * (i // 2 + 1))
                for a in range(2):
                    dve.scalar_tensor_tensor(Xr[:, i, :], yg[i % 2][a], gates[:, 8 * a + i:8 * a + i + 1], Xr[:, i, :], ALU.mult, ALU.add).then_inc(sem("y_added"), 1)
                    dve.drain()
            dve.wait_ge(sem("ss_ready"), 26 + TT)
            dve.tensor_scalar(rstd[:, :], ss[:, :], 1.0 / D, EPS, ALU.mult, ALU.add).then_inc(sem("ms_ready"), 1)
            dve.wait_ge(sem("rms_ready"), 5)
            dve.reciprocal(rstd[:, :], rstd[:, :])
            dve.drain()
            dve.wait_ge(sem("wfin_loaded"), 16)
            for i in range(TT):
                if i >= 2:
                    dve.wait_ge(sem("out0") if i % 2 == 0 else sem("out1"), 16 * (i // 2))
                dve.scalar_tensor_tensor(ost[i % 2], Xr[:, i, :], rstd[:, i:i + 1], wfin, ALU.mult, ALU.mult).then_inc(sem("out_ready"), 1)


def kernel(**inputs):
    import concourse.bacc as bacc
    from concourse.bass_utils import run_bass_kernel_spmd

    nc = bacc.Bacc("TRN2", target_bir_lowering=False, num_devices=1)
    arrays, views = {}, {}
    for name, value in inputs.items():
        a = np.ascontiguousarray(value)
        arrays["in_" + name] = a
        views[name] = nc.dram_tensor("in_" + name, a.shape, mybir.dt.from_np(a.dtype), kind="ExternalInput").ap()
    out = nc.dram_tensor("out_0_dram", (1, T, D), F32, kind="ExternalOutput").ap()
    program(nc, views, out)
    result = run_bass_kernel_spmd(nc, [arrays], core_ids=[0])
    return result.results[0]["out_0_dram"]
```

```python
from contextlib import ExitStack

import concourse.bass as bass
import numpy as np
from concourse import mybir

F32 = mybir.dt.float32
I32 = mybir.dt.int32
U32 = mybir.dt.uint32
ALU = mybir.AluOpType
ACT = mybir.ActivationFunctionType
AX_X = mybir.AxisListType.X
ds = bass.ds

P = 128
D = 1024
T = 1024
KT = D // P
TT = T // P
HEADS, HD = 8, 64
J = HEADS * HD // P
CH = 64
NC = T // CH
N_SHIFT = 14
GROUPS, GC, NS = 32, 16, 64
PAIRS = GROUPS // 2
TAU = P // GC
SC = T // TAU
MEM = 256
XH = 4
NE, NG, EPG = 32, 4, 8
FE = 512
OVER = 2 * T // P - 1
SLOTS = (NE + OVER) * P
EPS = 1e-6
DECAY = float(np.exp(-0.5))
TWO_PI = 2.0 * np.pi

ROWS = {}
_at = 0
for _n, _k in (("norm_mix_w", 8), ("mu_shift", 14), ("w0", 4), ("a0", 4), ("k_k", 4), ("k_a", 4), ("r_k", 4),
               ("norm_xattn_w", 8), ("norm_mem_w", 8), ("norm_moe_w", 8), ("b_glu", 4),
               ("s5_lam_re", 16), ("s5_lam_im", 16)):
    ROWS[_n] = (_at, _k)
    _at += _k
NROWS = _at


def program(nc, I, out):
    ctx = ExitStack()
    with ctx:
        def sb(name, shape, dt=F32):
            return ctx.enter_context(nc.sbuf_tensor(name, shape, dt))

        sems = {}

        def sem(name):
            if name not in sems:
                sems[name] = ctx.enter_context(nc.semaphore(name))
            return sems[name]

        ONCE = {
            "dve_marks": ["ldrow_ready", "s5_angle", "w2_ready", "rkc_ready", "v1_ready", "trig_ready", "kk_ready", "states_done",
                          "sprev_ready", "gn_centred", "gn_var", "gn_done", "l1_ready", "dv_ready", "marks_ready", "slots_ready"],
            "act_marks": ["pcol_ready", "s5_dt", "s5_trig", "dwda_ready", "gn_sq", "gn_std", "exp_l1", "exp_dv"],
            "pe_marks": ["pcol_ps", "dt_ps", "c_ps", "logits_ps", "ranks_ps"],
            "pool_marks": ["consts_a", "consts_b", "reset_a", "reset_b", "bd_zero", "toe_zero", "router_consts"],
        }

        def once(event):
            return next((name, events.index(event) + 1) for name, events in ONCE.items() if event in events)

        def reach(event):
            return sem(once(event)[0]), 1

        def reached(event):
            return sem(once(event)[0]), once(event)[1]

        arena = sb("arena", [P, 50 * 1024])

        def unit(a, n=1):
            return arena[:, a * 1024:(a + n) * 1024]

        ident = sb("ident", [P, P])
        ones = sb("ones", [P, P])
        blockones = sb("blockones", [P, P])
        pmask = sb("pmask", [P, P])
        strictU = sb("strictU", [P, P])
        lmask = sb("lmask", [P, 6, HD])
        lmask1T = sb("lmask1T", [P, HD])
        eye = sb("eye", [P, HD])
        prow = sb("prow", [P, P])
        pcol = sb("pcol", [P, NROWS])
        omka = sb("omka", [P, J])
        rkc = sb("rkc", [P, J, 2])
        small = sb("small", [P, 64])
        banks = [ctx.enter_context(nc.psum_tensor(f"bank{i}", [P, 512], F32)) for i in range(8)]

        def col(name, k=0):
            return pcol[:, ROWS[name][0] + k:ROWS[name][0] + k + 1]

        def cols(name):
            a, n = ROWS[name]
            return pcol[:, a:a + n]

        hT = unit(0, 8).rearrange("p (k t) -> p k t", k=KT)
        PT = unit(8, 14).rearrange("p (m t) -> p m t", m=N_SHIFT)
        uT = unit(22, 4).rearrange("p (j t) -> p j t", j=4)
        AR = unit(26, 8).rearrange("p (j c x) -> p j c x", j=J, c=NC)
        BK = unit(34, 8).rearrange("p (j c x) -> p j c x", j=J, c=NC)
        X = unit(8, 8).rearrange("p (i d) -> p i d", i=TT)
        wring = [unit(42 + s).rearrange("p (k m) -> p k m", k=KT) for s in range(2)]
        zbuf = [arena[:, (44 * 1024 + s * 1088):(44 * 1024 + s * 1088) + 1025] for s in range(2)]
        shift_d = unit(47)
        xs = [unit(48 + s).rearrange("p (k t) -> p k t", k=KT) for s in range(2)]
        junk = unit(16)
        zeros = unit(17)
        SHIFTED = [12, 13] + [4 * kind + j for j in range(J) for kind in range(3)]

        ss = small[:, 0:8]
        rstd = small[:, 8:16]

        d_u = nc.dram_tensor("d_u", (4 * P, TAU, SC), F32).ap()
        d_z = nc.dram_tensor("d_z", (4 * P, TAU, SC), F32).ap()

        w_in = I["w_in"][0].rearrange("(k p) n -> p k n", p=P)

        sig, csum, gexp, ginv = (unit(22 + n) for n in range(4))
        gprev, kk = unit(48), unit(49)
        avecs = [unit(32 if j < J - 1 else 12) for j in range(J)]
        tmps = [unit(33 if j < J - 1 else 13) for j in range(J)]
        gcol = sb("gcol", [P, NC, J])
        wdi = unit(46)[:, 128:640]
        wgu = unit(6)[:, 0:512]
        resets = [unit(40 if j < J - 1 else 14) for j in range(J)]
        Vt = unit(12, 4).rearrange("p (i c) -> p i c", i=TT)
        Gt = unit(0, 4).rearrange("p (i c) -> p i c", i=TT)
        rks = sb("rks", [P, TT, HEADS])
        Yt = unit(16, 4).rearrange("p (i c) -> p i c", i=TT)
        def half(u, i):
            return unit(u + i // 2)[:, 512 * (i % 2):512 * (i % 2) + 512]

        jx = lambda v: v.rearrange("p (j x) -> p j x", j=J)
        ARc = [jx(half(42, i)) for i in range(4)]
        BKz = [unit(44 + s).rearrange("p (h x) -> p h x", h=HEADS) for s in range(2)]
        BKT = [jx(half(46, i)) for i in range(4)]
        UV = [half(48, i).rearrange("p (h v) -> p h v", h=HEADS) for i in range(2)]
        V0 = [half(49, i).rearrange("p (h v) -> p h v", h=HEADS) for i in range(2)]
        PM = [unit(8 + i).rearrange("p (h x) -> p h x", h=HEADS) for i in range(4)]
        TTbd = [jx(half(5, 0)), jx(half(5, 1)), jx(half(20, 0)), jx(half(20, 1))]
        LTbd = [jx(half(21, i)) for i in range(2)]
        Xbd = [jx(half(22, i)) for i in range(2)]
        TS = [half(23, i).rearrange("p (a j x) -> p a j x", a=2, j=J) for i in range(2)]
        Xst = [jx(unit(24)[:, 256 * i:256 * i + 256]) for i in range(2)]
        Qst = jx(unit(24)[:, 512:768])
        Zbd = jx(unit(7)[:, 0:512])
        Zst = jx(unit(7)[:, 512:768])
        Ztmp = jx(unit(7)[:, 768:1024])
        LB = [banks[2], banks[6]]
        PIECES = {(1, 0): (0, 0), (1, 1): (0, 1), (2, 0): (0, 2), (2, 1): (0, 3),
                  (3, 0): (1, 0), (3, 1): (1, 1), (4, 0): (1, 2), (4, 1): (1, 3)}

        def pairs(eng, pair):
            pair(eng, -1, 1, True, False)
            with eng.Fori(0, 3) as i:
                pair(eng, i * 2, 0, True, True)
                pair(eng, i * 2 + 1, 1, True, True)
            pair(eng, 6, 0, True, True)
            pair(eng, 7, 1, False, True)

        gtmp = unit(42, 4)
        lnwb = unit(24)
        gstat = unit(25)[:, 0:192].rearrange("p (a g) -> p a g", a=3)
        ymixT = unit(26, 8).rearrange("p (k t) -> p k t", k=KT)
        Xg = unit(35, 4).rearrange("p (g c) -> p g c", g=GROUPS)
        Toe = unit(4, 4).rearrange("p (g x) -> p g x", g=GROUPS)
        W1 = [unit(26 + 2 * a, 2).rearrange("p (q x) -> p q x", q=PAIRS) for a in range(2)]
        W2 = [arena[:, 30 * 1024 + 2304 * a:30 * 1024 + 2304 * (a + 1)].rearrange("p (q x) -> p q x", q=PAIRS) for a in range(2)]
        w2all = arena[:, 30 * 1024:30 * 1024 + 4608]
        V1 = [unit(38 + 2 * a, 2).rearrange("p (q x) -> p q x", q=PAIRS) for a in range(2)]
        trig0 = [unit(38, 2), unit(40, 2)]
        Braw = [unit(35)[:, 256 * a:256 * a + 256].rearrange("p (q i) -> p q i", q=PAIRS) for a in range(2)]
        Bbar = [unit(35)[:, 512 + 256 * a:768 + 256 * a].rearrange("p (q i) -> p q i", q=PAIRS) for a in range(2)]
        Cst = [unit(37)[:, 256 * a:256 * a + 256].rearrange("p (q o) -> p q o", q=PAIRS) for a in range(2)]
        Craw = [unit(37)[:, 512 + 256 * a:768 + 256 * a].rearrange("p (r n) -> p r n", r=4) for a in range(2)]
        KK = unit(8, 4)[0:16, :].rearrange("p (g x) -> p g x", g=GROUPS)
        s5_tmp = unit(18, 4)
        d_w1 = nc.dram_tensor("d_w1", (P, 4096), F32).ap()
        d_w2 = nc.dram_tensor("d_w2", (P, 4608), F32).ap()
        d_trig = nc.dram_tensor("d_trig", (P, 4096), F32).ap()
        d_kk = nc.dram_tensor("d_kk", (16, 4096), F32).ap()
        r8 = sb("r8", [P, PAIRS])
        E5 = [unit(46, 2), unit(48, 2)]
        trig = [unit(42, 2), unit(44, 2)]
        Rtab = unit(39, 2)
        rot = [unit(20 + 2 * a, 2) for a in range(2)]
        zst = [unit(8 + 2 * a, 2) for a in range(2)]
        Sprev = rot
        y5 = unit(46, 4)
        zT = unit(34, 4).rearrange("p (j t) -> p j t", j=4)
        wglu = unit(39, 2).rearrange("p (k m) -> p k m", k=4)
        sglu = unit(41)
        s5d = unit(36)[0:16, 992:1024]
        ldt = unit(36)[0:16, 988:990]
        ldrow = unit(36)[0:16, 856:984]
        names5 = ["dt", "are", "th", "rho", "kr", "rr", "ra", "sn", "cs", "lr", "li", "nr", "den", "cr", "ci", "t1", "t2", "t3", "t4",
                  "pr", "pi", "pr2", "pi2"]
        a5 = {n: unit(36)[:, 16 * i:16 * i + 16] for i, n in enumerate(names5)}
        a5["r8"] = r8[:, :]
        pw = [unit(36)[:, 400 + 144 * a:544 + 144 * a].rearrange("p (k q) -> p k q", k=9) for a in range(2)]
        pwr = [unit(34)[:, 512 + 128 * a:640 + 128 * a].rearrange("p (k q) -> p k q", k=8) for a in range(2)]
        Xr = unit(0, 8).rearrange("p (i d) -> p i d", i=TT)
        wmix = unit(8, 8).rearrange("p (k n) -> p k n", k=KT)
        tokring = [unit(16 + s).rearrange("p (k t) -> p k t", k=KT) for s in range(2)]

        hB = unit(18, 8).rearrange("p (k t) -> p k t", k=KT)
        wq = unit(26, 8).rearrange("p (k n) -> p k n", k=KT)
        wvo = unit(8, 8).rearrange("p (k n) -> p k n", k=KT)
        Xm = unit(34, 2).rearrange("p (i d) -> p i d", i=2)
        hM = unit(36, 2).rearrange("p (k m) -> p k m", k=KT)
        kT = unit(38, 2).rearrange("p (k m) -> p k m", k=KT)
        vM = unit(40, 2).rearrange("p (i d) -> p i d", i=2)
        wkr = [unit(42 + s).rearrange("p (k m) -> p k m", k=KT) for s in range(2)]
        qr = [unit(44 + s).rearrange("p (k t) -> p k t", k=KT) for s in range(2)]
        oR = [unit(46 + s).rearrange("p (k t) -> p k t", k=KT) for s in range(2)]
        pr_ = unit(16).rearrange("p (h m) -> p h m", h=XH)
        pT = unit(17).rearrange("p (i h t) -> p i h t", i=2, h=XH)
        junk2 = unit(47)
        smx = [small[:, 16 + 4 * s:20 + 4 * s] for s in range(2)]
        ssum = [small[:, 24 + 4 * s:28 + 4 * s] for s in range(2)]
        wrt = unit(47)[:, 0:288].rearrange("p (k e) -> p k e", k=KT)
        brt = unit(47)[:, 288:324]
        LG = unit(16)[:, 0:288].rearrange("p (i e) -> p i e", i=TT)
        l2 = unit(16)[:, 288:544].rearrange("p (i e) -> p i e", i=TT)
        io32 = unit(16)[:, 544:576]
        io4b, io8b = unit(16)[:, 576:580], unit(16)[:, 580:588]
        io128 = unit(16)[:, 588:620]
        ioM = unit(16)[:, 620:627]
        ioO = unit(16)[:, 628:643]
        e8 = [unit(16)[:, 644 + 64 * i:708 + 64 * i].rearrange("p (i e) -> p i e", i=TT) for i in range(5)]
        O2 = [unit(17)[:, 256 * a:256 * a + 256].rearrange("p (i e) -> p i e", i=TT) for a in range(2)]
        MS = unit(17)[:, 512:768].rearrange("p (i e) -> p i e", i=TT)
        MA = unit(17)[:, 768:1024].rearrange("p (i e) -> p i e", i=TT)
        RK = unit(46)[:, 0:256].rearrange("p (i e) -> p i e", i=TT)
        RT = unit(46)[:, 256:512].rearrange("p (i e) -> p i e", i=TT)
        c32 = [unit(46)[:, 512 + 32 * i:544 + 32 * i] for i in range(5)]
        cmpb = unit(46)[:, 672:672 + 224].rearrange("p (e m) -> p e m", m=7)
        cmpo = unit(45)[:, 0:480].rearrange("p (b e) -> p b e", e=NE)
        v8 = [small[:, 8 * i:8 * i + 8] for i in range(8)]
        s8 = [unit(46)[:, 896 + 8 * i:904 + 8 * i] for i in range(14)]
        gates = sb("gates", [P, 16])
        ints = sb("ints", [P, 48], I32)
        slots_i = ints[:, 0:16]
        tokid = ints[:, 16:24]
        nover_i = ints[:, 24:25]
        eid_i = ints[:, 25:40]
        idx = [ints[:, 40 + s:41 + s] for s in range(2)]
        zint = unit(44)[:, 0:47].bitcast(I32)
        d_slot = nc.dram_tensor("d_slot", (SLOTS, 1), I32).ap()
        d_xn = nc.dram_tensor("d_xn", (T, D), F32).ap()
        d_y = nc.dram_tensor("d_y", (SLOTS, D), F32).ap()
        WG = [unit(a, 4).rearrange("p (k n) -> p k n", k=KT) for a in (26, 8)]
        WU = [unit(a, 4).rearrange("p (k n) -> p k n", k=KT) for a in (30, 12)]
        WD = [unit(a, 4).rearrange("p (k n) -> p k n", k=4) for a in (34, 38)]
        xb = [unit(42 + s) for s in range(2)]
        xbT = [unit(44 + s).rearrange("p (k t) -> p k t", k=KT) for s in range(2)]
        sg = unit(46)[:, 0:512]
        hid = unit(46)[:, 512:1024]
        hidT = unit(47)[:, 0:512].rearrange("p (k t) -> p k t", k=4)
        gainp = unit(47)[:, 512:520]
        ysb = [unit(48 + s) for s in range(2)]

        def blocks(eng, block_of):
            with eng.Fori(0, NE // 2 - 1) as b:
                for s in range(2):
                    block_of(eng, s, b * 2 + s, b)
            block_of(eng, 0, NE - 2, NE // 2 - 1)
            block_of(eng, 1, NE - 1, NE // 2 - 1, last=True)

        yg = [[unit(8 + 2 * s + a) for a in range(2)] for s in range(2)]
        wfin = unit(12)
        ost = [unit(13 + s) for s in range(2)]

        block = ctx.enter_context(nc.Block())

        @block.gpsimd
        def _(pool):
            n = [0]

            def step(ins):
                ins.then_inc(sem("pool_chain"), 1)
                n[0] += 1
                pool.wait_ge(sem("pool_chain"), n[0])

            def keep(view, op, base, pattern, cm, fill=0.0):
                step(pool.affine_select(out=view, in_=view, compare_op=op, fill=fill, base=base,
                                        pattern=pattern, channel_multiplier=cm))

            step(pool.memset(ident[:, :], 0.0))
            keep(ident[:, :], ALU.not_equal, 0, [[-1, P]], 1, 1.0)
            step(pool.memset(ones[:, :], 1.0))
            step(pool.memset(blockones[:, :], 0.0))
            step(pool.memset(blockones[0:64, 0:64], 1.0))
            step(pool.memset(blockones[64:128, 64:128], 1.0))
            step(pool.memset(prow[:, :], 0.0))
            step(pool.memset(zeros, 0.0))
            pool.nop().then_inc(*reach("consts_a"))
            step(pool.memset(pmask[:, :], 1.0))
            step(pool.memset(strictU[:, :], 1.0))
            keep(strictU[:, :], ALU.is_ge, -1, [[1, P]], -1)
            step(pool.memset(eye[:, :], 0.0))
            step(pool.memset(lmask1T[:, :], 0.0))
            step(pool.memset(lmask[:, :, :], 0.0))
            for h in (0, 64):
                keep(eye[h:h + 64, :], ALU.not_equal, 0, [[-1, 64]], 1, 1.0)
                keep(pmask[h:h + 64, 0:64], ALU.is_ge, -1, [[1, 64]], -1)
                keep(pmask[h:h + 64, 64:128], ALU.is_ge, 0, [[1, 64]], -1)
                keep(lmask1T[h:h + 64, 1:64:2], ALU.not_equal, 0, [[-2, 32]], 1, 1.0)
                for lv in range(6):
                    m = 1 << lv
                    v = lmask[h:h + 64, lv, :].rearrange("p (b x) -> p b x", x=2 * m)
                    step(pool.memset(v[:, :, 0:m], 1.0))
                    keep(v, ALU.is_ge, -m, [[-2 * m, 32 // m], [0, 2 * m]], 1)
                    keep(v, ALU.is_ge, 2 * m - 1, [[2 * m, 32 // m], [0, 2 * m]], -1)
            pool.nop().then_inc(*reach("consts_b"))
            pool.wait_ge(sem("w1_evac"), 8)
            pool.dma_start(d_w1, unit(26, 4)).then_inc(sem("s5_stored"), 16)
            pool.wait_ge(*reached("w2_ready"))
            pool.dma_start(d_w2, w2all).then_inc(sem("s5_stored"), 16)
            pool.wait_ge(*reached("trig_ready"))
            pool.dma_start(d_trig, unit(38, 4)).then_inc(sem("s5_stored"), 16)
            pool.wait_ge(*reached("kk_ready"))
            pool.dma_start(d_kk, unit(8, 4)[0:16, :]).then_inc(sem("s5_stored"), 16)
            pool.wait_ge(sem("z_evac"), 4 + 8)
            pool.dma_start(d_u.rearrange("(j p) a c -> p j (a c)", p=P), uT).then_inc(sem("u_stored"), 16)
            for event, unit_ in (("reset_a", resets[0]), ("reset_b", resets[J - 1])):
                if event == "reset_a":
                    pool.wait_ge(sem("s5_stored"), 64)
                else:
                    pool.wait_ge(sem("elem_done"), J - 1)
                step(pool.memset(unit_, 1.0))
                step(pool.memset(unit_.rearrange("p (c x) -> p c x", x=CH)[:, :, 0:1], 0.0))
                pool.sem_inc(*reach(event))
            pool.wait_ge(sem("elem_done"), J)
            pool.wait_ge(sem("values_evac"), TT)
            pool.wait_ge(sem("gates_evac"), 2 * TT)
            pool.wait_ge(sem("u_stored"), 16)
            for v in (unit(5), unit(20, 3), unit(7)[:, 0:768], unit(44, 2), unit(49)[0:64, :]):
                step(pool.memset(v, 0.0))
            pool.sem_inc(*reach("bd_zero"))
            pool.wait_ge(sem("Y_ready"), 2 + NC)
            pool.wait_ge(*reached("states_done"))
            step(pool.memset(Toe, 0.0))
            pool.sem_inc(*reach("toe_zero"))
            pool.wait_ge(sem("x_attn"), 4 + 2 * TT)
            for v, pat, base in ((io32, [[1, NE]], 0), (io4b, [[1, NG]], 8), (io8b, [[1, EPG]], 16), (io128, [[P, NE]], 0),
                                 (ioM, [[P, 7]], P), (ioO, [[1, OVER]], 0)):
                step(pool.iota(v, pat, base=base, channel_multiplier=0, allow_small_or_imprecise_dtypes=True))
            step(pool.iota(tokid, [[P, TT]], base=0, channel_multiplier=1))
            step(pool.memset(zint, 0))
            pool.sem_inc(*reach("router_consts"))
            pool.dma_start(d_slot.rearrange("(p b) o -> p (b o)", p=P), zint).then_inc(sem("slot_zero"), 16)
            pool.wait_ge(sem("slot_zero"), 16)
            pool.wait_ge(*reached("slots_ready"))
            for k in range(2 * TT):
                pool.indirect_dma_start(d_slot, bass.IndirectOffsetOnAxis(ap=slots_i[:, k:k + 1], axis=0),
                                        tokid[:, k % TT:k % TT + 1], None).then_inc(sem("slot_written"), 16)
            pool.wait_ge(sem("slot_written"), 16 * 2 * TT)
            pool.wait_ge(sem("xn_stored0"), 16 + 64)
            pool.wait_ge(sem("xn_stored1"), 16 + 64)

            def gather_block(s, n, ns, lead):
                idx_loaded, xb_loaded = (sem("idx_loaded0"), sem("xb_loaded0")) if s == 0 else (sem("idx_loaded1"), sem("xb_loaded1"))
                pool.wait_ge(sem("xT_ps"), n * 2 + 2 * lead)
                pool.dma_start(idx[s], d_slot[ds(n * P, P), :]).then_inc(idx_loaded, 16)
                pool.wait_ge(idx_loaded, ns * 16 + 16)
                pool.sem_inc(sem("pool_waits"), 1)
                pool.indirect_dma_start(xb[s], None, d_xn, bass.IndirectOffsetOnAxis(ap=idx[s], axis=0)).then_inc(xb_loaded, 16)

            with pool.Fori(0, NE // 2) as bb:
                for s in range(2):
                    gather_block(s, bb * 2 + s, bb, 1)
            n_over = pool.value_load(nover_i[0:1, :], min_val=0, max_val=OVER)
            with pool.Fori(0, OVER) as o:
                with pool.If(o < n_over):
                    gather_block(0, o + NE, o + NE // 2, 2)
                pool.nop()
            pool.wait_ge(sem("y_stored0"), n_over * 16 + (16 + 16 * (NE // 2)))
            pool.sem_inc(sem("pool_waits"), 1)
            pool.wait_ge(sem("y_stored1"), 16 + 16 * (NE // 2))
            for i in range(TT):
                if i >= 2:
                    pool.wait_ge(sem("y_added"), 2 * (i - 1))
                for a in range(2):
                    pool.indirect_dma_start(yg[i % 2][a], None, d_y, bass.IndirectOffsetOnAxis(ap=slots_i[:, a * TT + i:a * TT + i + 1], axis=0)
                                            ).then_inc(sem("yg_loaded0") if i % 2 == 0 else sem("yg_loaded1"), 16)

        @block.sync
        def _(sp):
            sp.wait_ge(*reached("consts_a"))
            for name, (a, k) in ROWS.items():
                src = I[name][0]
                if name == "r_k":
                    src = src.rearrange("(j h) c -> j (h c)", j=J)
                elif name.startswith("s5_lam"):
                    src = src.rearrange("(q h) c -> q (h c)", q=PAIRS)
                else:
                    src = src.rearrange("(k p) -> k p", p=P)
                sp.dma_start(prow[a:a + k, :], src).then_inc(sem("params_loaded"), 16)
            sp.dma_start(X, I["x"][0].rearrange("(i p) d -> p i d", p=P)).then_inc(sem("x_loaded"), 16)
            sp.dma_start(d_y[NE * P:SLOTS, :].rearrange("(b p) d -> p b d", p=P),
                         zeros.rearrange("p (o d) -> p o d", o=1).to_broadcast((P, OVER, D))).then_inc(sem("y_zeroed"), 16)
            sp.dma_start(wdi[0:64, :], I["w_decay_up"][0]).then_inc(sem("lora_loaded"), 16)
            sp.dma_start(wdi[64:128, :], I["w_iclr_up"][0]).then_inc(sem("lora_loaded"), 16)

            def load_tile(pos, s, column):
                sp.wait_ge(sem("z_done"), pos * 2 + 2)
                sp.dma_start(wring[s], w_in[:, :, ds(column, P)]).then_inc(sem("win_loaded0") if s == 0 else sem("win_loaded1"), 16)

            with sp.Fori(0, 2) as i:
                for s in range(2):
                    load_tile(i * 2 + s, s, i * 256 + (14 + s) * P)
            for s in range(2):
                load_tile(4 + s, s, (12 + s) * P)
            with sp.Fori(0, J // 2) as jj:
                for x in range(6):
                    load_tile(jj * 6 + (6 + x), x % 2, jj * 256 + (4 * (x % 3) + x // 3) * P)
            sp.wait_ge(sem("z_done"), 4 + 36)
            sp.dma_start(wgu[:, :], I["w_gate_up"][0]).then_inc(sem("wgu_loaded"), 16)
            sp.wait_ge(*reached("bd_zero"))
            sp.wait_ge(sem("values_evac"), TT)

            def stage(p, par):
                for h in range(2):
                    c = p * 2 + h
                    loaded = sem("ops_loaded0") if h == 0 else sem("ops_loaded1")
                    sp.wait_ge(sem("bkt_ps"), c + 1)
                    sp.wait_ge(sem("y_ps"), c + 1)
                    for q in range(2):
                        sp.dma_start(BKz[h][64 * q:64 * q + 64, q:HEADS:2, :],
                                     BK[64 * q:64 * q + 64, :, ds(c, 1), :].rearrange("p j o x -> p j (o x)")).then_inc(loaded, 16)
                    sp.dma_start(ARc[2 * par + h], AR[:, :, ds(c, 1), :].rearrange("p j o x -> p j (o x)")).then_inc(loaded, 16)

            def stage_values(p):
                for h in range(2):
                    loaded = sem("uv_loaded0") if h == 0 else sem("uv_loaded1")
                    sp.wait_ge(sem("y_ps"), p * 2 + (h + 3))
                    for v in (UV, V0):
                        sp.dma_start(v[h][64:128, :, :], Vt[64 * h:64 * h + 64, ds(p, 1), :].rearrange("p o (h v) -> p (o h) v", h=HEADS)
                                     ).then_inc(loaded, 16)

            def stage_pair(sp, p, par, prep, state):
                if prep:
                    stage(p + 1, 1 - par)
                if state:
                    stage_values(p)

            pairs(sp, stage_pair)
            sp.wait_ge(sem("ops_loaded0"), 48 * (NC // 2))
            sp.wait_ge(sem("ops_loaded1"), 48 * (NC // 2))
            sp.wait_ge(sem("s5_stored"), 64)
            sp.wait_ge(sem("u_stored"), 16)
            sp.dma_start(unit(26, 4), d_w1).then_inc(sem("w1_loaded"), 16)
            for a in range(TAU):
                sp.dma_start(Xg[GC * a:GC * a + GC, :, :], d_u[:, a, :].rearrange("(g i) c -> i g c", i=GC)).then_inc(sem("xg_loaded"), 16)
            sp.dma_start(w2all, d_w2).then_inc(sem("w2_loaded"), 16)
            sp.wait_ge(sem("Y_ready"), 2 + NC)
            sp.dma_start(unit(42, 4), d_trig).then_inc(sem("trig_loaded"), 16)
            sp.wait_ge(*reached("toe_zero"))
            for a in range(TAU):
                sp.dma_start(Toe[GC * a:GC * a + GC, :, GC * a:P], d_kk.rearrange("p (g x) -> p g x", g=GROUPS)[:, :, 0:P - GC * a]).then_inc(sem("toe_loaded"), 16)
            sp.dma_start(lnwb[:, 0:512], I["ln_x_w"].to_broadcast((P, 512))).then_inc(sem("ln_loaded"), 16)
            sp.dma_start(lnwb[:, 512:1024], I["ln_x_b"].to_broadcast((P, 512))).then_inc(sem("ln_loaded"), 16)
            sp.wait_ge(*reached("sprev_ready"))
            sp.dma_start(wglu, I["w_glu"][0].rearrange("(k p) m -> p k m", p=P)).then_inc(sem("wglu_loaded"), 16)
            wm = I["w_mix_out"][0].rearrange("(k p) n -> p k n", p=P)
            sp.dma_start(wmix[:, 0:4, :], wm[:, 0:4, :]).then_inc(sem("wmix_loaded"), 16)
            for a in range(TAU):
                if a == 0:
                    sp.wait_ge(sem("gelu_done"), 8)
                sp.dma_start(d_z[:, a, :].rearrange("(g o) c -> o g c", o=GC),
                             y5[GC * a:GC * a + GC, :].rearrange("p (g c) -> p g c", g=GROUPS)).then_inc(sem("z_stored"), 16)
            xrows = I["x"][0].rearrange("(i p) d -> p i d", p=P)
            sp.wait_ge(sem("z_stored"), 16 * TAU)
            sp.dma_start(zT, d_z.rearrange("(j p) a c -> p j (a c)", p=P)).then_inc(sem("zT_loaded"), 16)
            sp.dma_start(Xr[:, 4:8, :], xrows[:, 4:8, :]).then_inc(sem("xr_loaded"), 16)
            sp.wait_ge(*reached("gn_done"))
            sp.dma_start(wmix[:, 4:8, :], wm[:, 4:8, :]).then_inc(sem("wmix_loaded"), 16)
            sp.dma_start(Xr[:, 0:4, :], xrows[:, 0:4, :]).then_inc(sem("xr_loaded"), 16)
            sp.wait_ge(sem("ymix_rwkv"), TT)
            sp.wait_ge(sem("ymix_s5"), 8)
            sp.wait_ge(sem("z_stored"), 16 * TAU)
            with sp.Fori(0, TT // 2) as ii:
                for s in range(2):
                    sp.wait_ge(sem("mix_ps"), ii * 4 + (2 * s + 2))
                    sp.dma_start(tokring[s], ymixT[:, :, ds(ii * 256 + s * 128, P)]).then_inc(sem("tok0_loaded") if s == 0 else sem("tok1_loaded"), 16)
            sp.wait_ge(sem("mix_added"), 4 + 2 * TT)
            sp.dma_start(Xm, I["mem"][0].rearrange("(i p) d -> p i d", p=P)).then_inc(sem("xm_loaded"), 16)
            sp.dma_start(wvo, I["w_v"][0].rearrange("(k p) n -> p k n", p=P)).then_inc(sem("wv_loaded"), 16)
            sp.dma_start(wq, I["w_q"][0].rearrange("(k p) n -> p k n", p=P)).then_inc(sem("wq_loaded"), 16)
            wk = I["w_k"][0].rearrange("(k p) n -> p k n", p=P)
            with sp.Fori(0, KT // 2) as mm:
                for s in range(2):
                    sp.wait_ge(sem("k_ps"), mm * 2 + (s + 1))
                    sp.dma_start(wkr[s], wk[:, :, ds(mm * 256 + s * P, P)]).then_inc(sem("wk_loaded0") if s == 0 else sem("wk_loaded1"), 16)
            sp.wait_ge(sem("v_ps"), 4)
            sp.dma_start(wvo, I["w_o"][0].rearrange("(k p) n -> p k n", p=P)).then_inc(sem("wo_loaded"), 16)
            sp.wait_ge(sem("x_attn"), 4 + 2 * TT)
            sp.dma_start(wrt[:, :, 0:NG], I["w_router_group"][0].rearrange("(k p) g -> p k g", p=P)).then_inc(sem("router_loaded"), 16)
            for g in range(NG):
                sp.dma_start(wrt[:, :, NG + EPG * g:NG + EPG * g + EPG], I["w_router_expert"][0, g].rearrange("(k p) e -> p k e", p=P)).then_inc(sem("router_loaded"), 16)
            sp.dma_start(brt[:, 0:NG], I["b_router_group"].to_broadcast((P, NG))).then_inc(sem("router_loaded"), 16)
            sp.dma_start(brt[:, NG:NG + NE], I["b_router_expert"].rearrange("a g e -> a (g e)").to_broadcast((P, NE))).then_inc(sem("router_loaded"), 16)
            sp.dma_start(gainp, I["norm_moe_w"][0].rearrange("(p k) -> p k", p=P)).then_inc(sem("router_loaded"), 16)

            def load_expert(s, e, n, lead):
                g, u, d = (sem("wg0"), sem("wu0"), sem("wd0")) if s == 0 else (sem("wg1"), sem("wu1"), sem("wd1"))
                if lead:
                    sp.wait_ge(sem("gate_ps"), n + (lead - 2))
                sp.dma_start(WG[s], I["w_exp_gate"][0, ds(e, 1)].rearrange("o (p k) n -> p (o k) n", p=P)).then_inc(g, 16)
                if lead:
                    sp.wait_ge(sem("up_ps"), n + lead)
                sp.dma_start(WU[s], I["w_exp_up"][0, ds(e, 1)].rearrange("o (p k) n -> p (o k) n", p=P)).then_inc(u, 16)
                if lead:
                    sp.wait_ge(sem("dn_ps"), n * 2 + 2 * lead)
                sp.dma_start(WD[s], I["w_exp_down"][0, ds(e, 1)].rearrange("o (p k) n -> p (o k) n", p=P)).then_inc(d, 16)

            load_expert(0, 0, 0, None)
            for i in range(TT):
                sp.wait_ge(sem("xs_ready"), 18 + i + 1)
                sp.dma_start(d_xn[i * P:(i + 1) * P, :], xs[i % 2].rearrange("p k d -> p (k d)")).then_inc(sem("xn_stored0") if i % 2 == 0 else sem("xn_stored1"), 16)
            load_expert(1, 1, 1, None)
            with sp.Fori(0, NE // 2 - 1) as bb:
                for s in range(2):
                    load_expert(s, bb * 2 + (2 + s), bb * 2 + (2 + s), 1)
            sp.wait_ge(*reached("slots_ready"))
            n_over = sp.value_load(nover_i[0:1, :], min_val=0, max_val=OVER)
            with sp.Fori(0, OVER) as o:
                with sp.If(o < n_over):
                    e = sp.value_load(eid_i[0:1, ds(o, 1)], min_val=0, max_val=NE - 1)
                    load_expert(0, e, o + NE, 2)
                sp.nop()
            sp.wait_ge(sem("dn_ps"), n_over * 2 + (4 + 2 * NE))
            sp.dma_start(wfin, I["norm_final_w"].rearrange("(o d) -> o d", o=1).to_broadcast((P, D))).then_inc(sem("wfin_loaded"), 16)
            for i in range(TT):
                sp.wait_ge(sem("out_ready"), i + 1)
                sp.dma_start(out[0, i * P:(i + 1) * P, :], ost[i % 2]).then_inc(sem("out0") if i % 2 == 0 else sem("out1"), 16)
            sp.wait_ge(sem("out0"), 64)
            sp.wait_ge(sem("out1"), 64)
        def norm_pe(pe, base, tiles):
            with pe.Fori(0, tiles // 2) as i:
                for s in range(2):
                    pe.wait_ge(sem("xs_ready"), i * 2 + (base + s + 1))
                    for q in range(2):
                        pe.wait_ge(sem("hT_ready"), i * 4 + (2 * base + 2 * s + q + 1))
                        for k in range(4):
                            t = pe.transpose(banks[4 + 2 * s + q][:, k * P:(k + 1) * P], xs[s][:, 4 * q + k, :], ident[:, :])
                        t.then_inc(sem("xsT_ps"), 1)

        @block.tensor
        def _(pe):
            pe.sem_inc(sem("z_done"), 4)
            pe.wait_ge(*reached("consts_a"))
            pe.wait_ge(sem("params_loaded"), 16 * len(ROWS))
            pe.transpose(banks[7][:, 0:NROWS], prow[0:NROWS, :], ident[0:NROWS, 0:NROWS]).then_inc(*reach("pcol_ps"))
            pe.wait_ge(*reached("ldrow_ready"))
            pe.transpose(banks[0][:, 0:16], ldrow, ident[0:16, 0:16]).then_inc(*reach("dt_ps"))
            pe.wait_ge(sem("s5_loaded"), 96)
            for a in range(2):
                for r in range(4):
                    m = pe.transpose(banks[1 + a][0:64, r * P:(r + 1) * P], Craw[a][:, r, :], ident[:, :])
            m.then_inc(*reach("c_ps"))
            norm_pe(pe, 0, TT)
            pe.wait_ge(sem("hT_ready"), 4 + 2 * TT)
            pe.wait_ge(sem("c_evac"), 16)

            def project(pos):
                s = pos % 2
                pe.wait_ge(sem("win_loaded0") if s == 0 else sem("win_loaded1"), pos // 2 * 16 + 16)
                for h in range(2):
                    pe.wait_ge(sem("z_evac"), pos * 2 + h + 1)
                    for k in range(KT):
                        m = pe.matmul(banks[2 * s + h][:, :], wring[s][:, k, :], hT[:, k, 512 * h:512 * h + 512],
                                      start=(k == 0), stop=(k == KT - 1))
                    m.then_inc(sem("z_done"), 1)

            project(0)
            project(1)
            pe.wait_ge(*reached("v1_ready"))
            for a in range(2):
                for q4 in range(4):
                    n = 4 * a + q4
                    if n >= 2:
                        pe.wait_ge(sem("w1_evac"), n - 1)
                    for x in range(4):
                        m = pe.transpose(banks[4 + n % 2][:, x * P:(x + 1) * P], V1[a][:, 4 * q4 + x, :], ident[:, :])
                    m.then_inc(sem("w1_ps"), 1)
            project(2)
            project(3)
            pe.wait_ge(*reached("w2_ready"))
            for q4 in range(4):
                for h in range(2):
                    n = 2 * q4 + h
                    if q4 > 0:
                        pe.wait_ge(sem("kk_evac"), n - 1)
                    for x in range(4):
                        q = 4 * q4 + x
                        o = banks[6 + h][0:16, x * P:(x + 1) * P]
                        r = slice(64 * h, 64 * h + 64)
                        pe.matmul(o, Bbar[0][r, q, :], W2[0][r, q, 0:P], start=True, stop=False)
                        m = pe.matmul(o, Bbar[1][r, q, :], W2[1][r, q, 0:P], start=False, stop=True)
                    m.then_inc(sem("kk_ps"), 1)
            project(4)
            project(5)
            pe.wait_ge(sem("lora_loaded"), 32)
            pe.wait_ge(sem("w1_evac"), 8)
            pe.wait_ge(sem("kk_evac"), 8)
            for j in range(J):
                project(6 + 3 * j)
                project(7 + 3 * j)
                if j == 0:
                    pe.wait_ge(*reached("dwda_ready"))
                else:
                    pe.wait_ge(sem("kk_norm"), 2 * j)
                for h in range(2):
                    pe.matmul(banks[4 + h][:, :], wdi[0:64, j * P:(j + 1) * P], PT[0:64, 12, 512 * h:512 * h + 512],
                              start=True, stop=True)
                    m = pe.matmul(banks[6 + h][:, :], wdi[64:128, j * P:(j + 1) * P],
                                  PT[64:128, 12, 512 * h:512 * h + 512], start=True, stop=True)
                m.then_inc(sem("rates_ps"), 1)
                project(8 + 3 * j)
                pe.wait_ge(sem("kk_sq"), j + 1)
                pe.wait_ge(sem("rates_ready"), 4 * j + 4)
                for h in range(2):
                    m = pe.matmul(banks[4 + h][:, :], blockones[:, :], tmps[j][:, 512 * h:512 * h + 512], start=True, stop=True)
                m.then_inc(sem("kk_sum"), 1)
            pe.wait_ge(*reached("pcol_ready"))
            pe.wait_ge(sem("elem_done"), J)
            pe.wait_ge(*reached("rkc_ready"))
            pe.wait_ge(sem("wgu_loaded"), 16)
            pe.wait_ge(sem("z_evac"), 4 + 36)
            pe.wait_ge(sem("kk_norm"), 2 * J)
            for i in range(TT):
                b = 4 * (i % 2)
                if i >= 2:
                    pe.wait_ge(sem("gates_evac"), 2 * (i - 1))
                    pe.wait_ge(sem("values_evac"), i - 1)
                for j in range(J):
                    pe.transpose(banks[b][:, j * P:(j + 1) * P], PT[:, 8 + j, i * P:(i + 1) * P], ident[:, :])
                pe.matmul(banks[b + 1][:, :], PT[:, 13, i * P:(i + 1) * P], wgu[:, :], start=True, stop=True)
                for j in range(J):
                    m = pe.matmul(banks[b + 2][:, 2 * j:2 * j + 2], PT[:, j, i * P:(i + 1) * P], rkc[:, j, :], start=True, stop=True)
                m.then_inc(sem("tok_ps"), 1)
            pe.wait_ge(sem("gates_evac"), 2 * TT)
            pe.wait_ge(sem("values_evac"), TT)
            pe.wait_ge(*reached("consts_b"))
            pe.wait_ge(*reached("bd_zero"))
            pe.sem_inc(sem("bkt_ps"), 2)
            pe.sem_inc(sem("y_ps"), 4)

            def state_pe(p, par, h, piece):
                c, q = p * 2 + h, 2 * par + h
                if piece == 0:
                    pe.wait_ge(sem("Z_ready"), c + 1)
                    pe.wait_ge(sem("uv_loaded0") if h == 0 else sem("uv_loaded1"), p * 32 + 32)
                    for x in range(HEADS):
                        o = banks[5][64 * (x % 2):64 * (x % 2) + 64, (x // 2) * 64:(x // 2) * 64 + 64]
                        pe.matmul(o, ARc[q][:, x // 2, 0:64], Zbd[:, x // 2, 64 * (x % 2):64 * (x % 2) + 64], start=True, stop=False)
                        m = pe.matmul(o, PM[q][:, x, 0:64], V0[h][:, x, :], start=False, stop=True)
                    m.then_inc(sem("Q_ps"), 1)
                    pe.wait_ge(sem("Y_ready"), c + 1)
                    for j in range(J):
                        pe.matmul(banks[7][64 * h:64 * h + 64, j * P:(j + 1) * P], ARc[q][:, j, 64:128], Zbd[:, j, :],
                                  start=(j == 0), stop=False, skip_group_check=True)
                elif piece == 1:
                    pe.wait_ge(sem("Q_ready"), c + 1)
                    pe.wait_ge(sem("TS_ready"), p * 12 + (11 + h))
                    for j in range(J):
                        m = pe.matmul(banks[5][:, 256 + j * 64:256 + j * 64 + 64], TTbd[q][:, j, :], Qst[:, j, :], start=True, stop=True)
                    m.then_inc(sem("U_ps"), 1)
                elif piece == 2:
                    pe.wait_ge(sem("U_ready"), c * 2 + 2)
                    for x in range(HEADS):
                        o = banks[5][64 * (x % 2):64 * (x % 2) + 64, (x // 2) * 64:(x // 2) * 64 + 64]
                        m = pe.matmul(o, BKT[q][:, x // 2, 64 * (x % 2):64 * (x % 2) + 64], UV[h][:, x, :], start=True, stop=True)
                    m.then_inc(sem("M_ps"), 1)
                else:
                    for x in range(HEADS):
                        m = pe.matmul(banks[7][64 * h:64 * h + 64, x * 64:x * 64 + 64], PM[q][:, x, 64:128], UV[h][:, x, :],
                                      start=False, stop=(x == HEADS - 1), skip_group_check=True)
                    m.then_inc(sem("y_ps"), 1)

            def prepare_pe(n, par, h, first):
                c, q = n * 2 + h, 2 * par + h
                pe.wait_ge(sem("ops_loaded0") if h == 0 else sem("ops_loaded1"), n * 48 + 48)
                for x in range(HEADS):
                    if x % 4 == 0:
                        pe.wait_ge(sem("PM_ready"), c * 2 + (x // 4 + 1))
                    m = pe.matmul(banks[x // 4][:, (x % 4) * P:(x % 4 + 1) * P], BKz[h][:, x, :], ARc[q][:, x // 2, :], start=True, stop=True)
                    if x % 4 == 3:
                        m.then_inc(sem("pm_ps"), 1)
                for x in range(HEADS):
                    o = LB[h][64 * (x % 2):64 * (x % 2) + 64, (x // 2) * 64:(x // 2) * 64 + 64]
                    m = pe.matmul(o, ARc[q][:, x // 2, 0:64], BKz[h][:, x, 0:64], start=True, stop=True)
                m.then_inc(sem("L_ps"), 1)
                if not first:
                    pe.wait_ge(sem("TS_ready"), n * 12 + (h - 1))
                for x in range(HEADS):
                    m = pe.matmul(banks[3 + h][:, x * 64:x * 64 + 64], BKz[h][:, x, :], ident[:, 64 * (x % 2):64 * (x % 2) + 64], start=True, stop=True)
                m.then_inc(sem("bkt_ps"), 1)

            def pair_pe(pe, p, par, prep, state):
                n, np_ = p + 1, 1 - par
                if prep:
                    for h in range(2):
                        prepare_pe(n, np_, h, not state)
                for lv in range(1, 6):
                    for gap in range(2):
                        for h in range(2 if prep else 0):
                            if gap == 0:
                                pe.wait_ge(sem("TS_ready"), n * 12 + (2 * lv - 1 + h))
                                for j in range(J):
                                    m = pe.matmul(LB[h][:, j * 64:j * 64 + 64], LTbd[h][:, j, :], TS[h][:, 0, j, :], start=True, stop=True)
                                m.then_inc(sem("X_ps"), 1)
                            else:
                                pe.wait_ge(sem("Xst_ready"), n * 10 + (2 * lv - 1 + h))
                                for j in range(J):
                                    pe.matmul(banks[3 + h][:, j * 64:j * 64 + 64], TTbd[2 * np_ + h][:, j, :], Xst[h][:, j, :], start=True, stop=True)
                                pe.wait_ge(sem("Xbd_ready"), n * 10 + (2 * lv - 1 + h))
                                for j in range(J):
                                    m = pe.matmul(banks[3 + h][:, 256 + j * 64:256 + j * 64 + 64], Xbd[h][:, j, :], TS[h][:, 1, j, :], start=True, stop=True)
                                m.then_inc(sem("D_ps"), 1)
                        if state and (lv, gap) in PIECES:
                            state_pe(p, par, *PIECES[lv, gap])

            pairs(pe, pair_pe)
            pe.wait_ge(sem("xg_loaded"), 16 * TAU)
            pe.wait_ge(sem("w1_loaded"), 16)
            for q4 in range(4):
                for a in range(2):
                    n = 2 * q4 + a
                    if n >= 4:
                        pe.wait_ge(sem("e_evac"), n - 3)
                    for x in range(4):
                        for h in range(2):
                            q = 4 * q4 + x
                            m = pe.matmul(banks[n % 4][64 * h:64 * h + 64, x * P:(x + 1) * P], W1[a][:, q, 64 * h:64 * h + 64],
                                          Xg[:, 2 * q + h, :], start=True, stop=True)
                    m.then_inc(sem("e_ps"), 1)
            pe.wait_ge(sem("toe_loaded"), 16 * TAU)
            pe.wait_ge(sem("w2_loaded"), 16)
            pe.wait_ge(*reached("sprev_ready"))
            pe.wait_ge(sem("e_evac"), 8)
            for q4 in range(4):
                for h in range(2):
                    n = 2 * q4 + h
                    if n >= 4:
                        pe.wait_ge(sem("gelu_done"), n - 3)
                    for x in range(4):
                        q = 4 * q4 + x
                        o = banks[n % 4][:, x * P:(x + 1) * P]
                        r = slice(64 * h, 64 * h + 64)
                        pe.matmul(o, Toe[:, 2 * q + h, :], Xg[:, 2 * q + h, :], start=True, stop=False)
                        pe.matmul(o, W2[0][r, q, GC:GC + P], Sprev[0].rearrange("p (q c) -> p q c", q=PAIRS)[r, q, :], start=False, stop=False)
                        m = pe.matmul(o, W2[1][r, q, GC:GC + P], Sprev[1].rearrange("p (q c) -> p q c", q=PAIRS)[r, q, :], start=False, stop=True)
                    m.then_inc(sem("y5_ps"), 1)
            pe.wait_ge(sem("wglu_loaded"), 16)
            pe.wait_ge(sem("zT_loaded"), 16)
            pe.wait_ge(sem("gelu_done"), 8)
            for m4 in range(4):
                for h in range(2):
                    n = 2 * m4 + h
                    if n >= 4:
                        pe.wait_ge(sem("glu_evac"), n - 3)
                    for k in range(4):
                        m = pe.matmul(banks[n % 4][:, :], wglu[:, k, m4 * P:(m4 + 1) * P], zT[:, k, 512 * h:512 * h + 512],
                                      start=(k == 0), stop=(k == 3))
                    m.then_inc(sem("glu_ps"), 1)
            pe.wait_ge(*reached("gn_done"))
            for i in range(TT):
                if i >= 2:
                    pe.wait_ge(sem("ymix_rwkv"), i - 1)
                for j in range(J):
                    m = pe.transpose(banks[4 + i % 2][:, j * P:(j + 1) * P], Yt[:, i, j * P:(j + 1) * P], ident[:, :])
                m.then_inc(sem("ymixT_ps"), 1)
            pe.sem_inc(sem("mix_ps"), 4)
            pe.wait_ge(sem("wmix_loaded"), 32)
            pe.wait_ge(sem("glu_evac"), 8)
            pe.wait_ge(sem("ymix_rwkv"), TT)
            with pe.Fori(0, TT // 2) as ii:
                for s in range(2):
                    pe.wait_ge(sem("tok0_loaded") if s == 0 else sem("tok1_loaded"), ii * 16 + 16)
                    pe.wait_ge(sem("mix_added"), ii * 4 + (2 * s + 2))
                    for h in range(2):
                        for k in range(KT):
                            m = pe.matmul(banks[2 * s + h][:, :], tokring[s][:, k, :], wmix[:, k, 512 * h:512 * h + 512],
                                          start=(k == 0), stop=(k == KT - 1))
                        m.then_inc(sem("mix_ps"), 1)
            pe.sem_inc(sem("k_ps"), 2)
            norm_pe(pe, 8, TT)
            norm_pe(pe, 16, 2)
            pe.wait_ge(sem("hT_ready"), 4 + 2 * 18)
            with pe.Fori(0, KT // 2) as mm:
                for s in range(2):
                    pe.wait_ge(sem("wk_loaded0") if s == 0 else sem("wk_loaded1"), mm * 16 + 16)
                    pe.wait_ge(sem("kT_ready"), mm * 2 + (s + 1))
                    for k in range(KT):
                        m = pe.matmul(banks[s][:, 0:MEM], wkr[s][:, k, :], hM[:, k, :], start=(k == 0), stop=(k == KT - 1))
                    m.then_inc(sem("k_ps"), 1)
            pe.wait_ge(sem("wv_loaded"), 16)
            pe.wait_ge(sem("mix_added"), 4 + 2 * TT)
            for i in range(2):
                for h in range(2):
                    for k in range(KT):
                        m = pe.matmul(banks[2 + h + 2 * i][:, :], hM[:, k, i * P:(i + 1) * P], wvo[:, k, 512 * h:512 * h + 512],
                                      start=(k == 0), stop=(k == KT - 1))
                    m.then_inc(sem("v_ps"), 1)
            pe.wait_ge(sem("wq_loaded"), 16)
            pe.wait_ge(sem("kT_ready"), 2 + KT)
            pe.wait_ge(sem("vM_ready"), 4)

            def queries(t):
                for m in range(KT):
                    if m % 4 == 0:
                        pe.wait_ge(sem("qr_ready"), t * 2 + (m // 4 + 1))
                    for k in range(KT):
                        mm = pe.matmul(banks[m // 4][:, (m % 4) * P:(m % 4 + 1) * P], wq[:, k, m * P:(m + 1) * P], hB[:, k, ds(t * P, P)],
                                       start=(k == 0), stop=(k == KT - 1))
                    if m % 4 == 3:
                        mm.then_inc(sem("q_ps"), 1)

            def attend(t, s, last):
                pe.wait_ge(sem("qr_ready"), t * 2 + 4)
                pe.wait_ge(sem("p_ready"), t + 1)
                for h in range(XH):
                    for kk_ in range(2):
                        m = pe.matmul(banks[2 + h // 2][:, (h % 2) * MEM:(h % 2 + 1) * MEM], qr[s][:, 2 * h + kk_, :], kT[:, 2 * h + kk_, :],
                                      start=(kk_ == 0), stop=(kk_ == 1))
                m.then_inc(sem("s_ps"), 1)
                if not last:
                    queries(t + 1)
                pe.wait_ge(sem("p_ready"), t + 2)
                pe.wait_ge(sem("x_attn"), t * 2 + 4)
                for i in range(2):
                    for h in range(XH):
                        m = pe.transpose(banks[4 + i][:, h * P:(h + 1) * P], pr_[:, h, i * P:(i + 1) * P], ident[:, :])
                m.then_inc(sem("pT_ps"), 1)
                pe.wait_ge(sem("pT_ready"), t * 2 + 2)
                pe.wait_ge(sem("o_ready"), t * 2 + 2)
                for h in range(XH):
                    for dd in range(2):
                        c = 2 * h + dd
                        for i in range(2):
                            m = pe.matmul(banks[6 + c // 4][:, (c % 4) * P:(c % 4 + 1) * P], vM[:, i, c * P:(c + 1) * P], pT[:, i, h, :],
                                          start=(i == 0), stop=(i == 1))
                m.then_inc(sem("o_ps"), 1)
                pe.wait_ge(sem("o_ready"), t * 2 + 4)
                for h in range(2):
                    for k in range(KT):
                        m = pe.matmul(banks[4 + h][:, :], oR[s][:, k, :], wvo[:, k, 512 * h:512 * h + 512], start=(k == 0), stop=(k == KT - 1))
                    m.then_inc(sem("oproj_ps"), 1)

            queries(0)
            pe.wait_ge(sem("wo_loaded"), 16)
            with pe.Fori(0, TT // 2 - 1) as ii:
                for s in range(2):
                    attend(ii * 2 + s, s, False)
            attend(TT - 2, 0, False)
            attend(TT - 1, 1, True)
            norm_pe(pe, 18, TT)
            pe.wait_ge(sem("router_loaded"), 128)
            pe.wait_ge(sem("hT_ready"), 4 + 2 * 26)
            for i in range(TT):
                for k in range(KT):
                    m = pe.matmul(banks[0][:, i * 36:(i + 1) * 36], hB[:, k, i * P:(i + 1) * P], wrt[:, k, :], start=(k == 0), stop=(k == KT - 1))
            m.then_inc(*reach("logits_ps"))
            pe.wait_ge(*reached("marks_ready"))
            pe.wait_ge(*reached("consts_b"))
            pe.matmul(banks[1][:, 0:256], strictU[:, :], MS.rearrange("p i e -> p (i e)"), start=True, stop=False)
            pe.matmul(banks[1][:, 0:256], ones[:, :], MA.rearrange("p i e -> p (i e)"), start=False, stop=True)
            pe.matmul(banks[1][:, 256:288], ones[:, :], c32[0], start=True, stop=True).then_inc(*reach("ranks_ps"))
            pe.sem_inc(sem("xT_ps"), 4)
            pe.sem_inc(sem("up_ps"), 2)
            pe.sem_inc(sem("dn_ps"), 4)
            pe.sem_inc(sem("hidT_ps"), 1)

            def tokens_pe(s, n, ns):
                pe.wait_ge(sem("xb_loaded0") if s == 0 else sem("xb_loaded1"), ns * 16 + 16)
                for q in range(2):
                    pe.wait_ge(sem("xbT_ready"), n * 2 + (q + 1))
                    for k in range(4):
                        m = pe.transpose(banks[q][:, k * P:(k + 1) * P], xb[s][:, 4 * q + k:D:KT], ident[:, :])
                    m.then_inc(sem("xT_ps"), 1)

            def gate_pe(s, n, ns):
                pe.wait_ge(sem("xbT_ready"), n * 2 + 4)
                pe.wait_ge(sem("wg0") if s == 0 else sem("wg1"), ns * 16 + 16)
                pe.wait_ge(sem("sg_ready"), n + 1)
                for k in range(KT):
                    m = pe.matmul(banks[2][:, :], xbT[s][:, k, :], WG[s][:, k, :], start=(k == 0), stop=(k == KT - 1))
                m.then_inc(sem("gate_ps"), 1)

            def up_pe(s, n, ns):
                pe.wait_ge(sem("wu0") if s == 0 else sem("wu1"), ns * 16 + 16)
                pe.wait_ge(sem("hid_ready"), n + 1)
                for k in range(KT):
                    m = pe.matmul(banks[3][:, :], xbT[s][:, k, :], WU[s][:, k, :], start=(k == 0), stop=(k == KT - 1))
                m.then_inc(sem("up_ps"), 1)

            def hidden_pe(n):
                pe.wait_ge(sem("hid_ready"), n + 2)
                pe.wait_ge(sem("hidT_ready"), n + 1)
                for k in range(4):
                    m = pe.transpose(banks[4][:, k * P:(k + 1) * P], hid[:, k:FE:4], ident[:, :])
                m.then_inc(sem("hidT_ps"), 1)

            def down_pe(s, n, ns):
                pe.wait_ge(sem("hidT_ready"), n + 2)
                pe.wait_ge(sem("wd0") if s == 0 else sem("wd1"), ns * 16 + 16)
                for h in range(2):
                    pe.wait_ge(sem("y_evac0") if h == 0 else sem("y_evac1"), n + 1)
                    for k in range(4):
                        m = pe.matmul(banks[5 + h][:, :], hidT[:, k, :], WD[s][:, k, 512 * h:512 * h + 512], start=(k == 0), stop=(k == 3))
                    m.then_inc(sem("dn_ps"), 1)

            def experts_pe(pe, s, n, ns, last=False):
                up_pe(s, n, ns)
                if not last:
                    tokens_pe(1 - s, n + 1, ns + s)
                hidden_pe(n)
                if not last:
                    gate_pe(1 - s, n + 1, ns + s)
                down_pe(s, n, ns)

            tokens_pe(0, 0, 0)
            gate_pe(0, 0, 0)
            blocks(pe, experts_pe)
            pe.wait_ge(*reached("slots_ready"))
            n_over = pe.value_load(nover_i[0:1, :], min_val=0, max_val=OVER)
            with pe.Fori(0, OVER) as o:
                with pe.If(o < n_over):
                    n, ns = o + NE, o + NE // 2
                    tokens_pe(0, n, ns)
                    gate_pe(0, n, ns)
                    up_pe(0, n, ns)
                    hidden_pe(n)
                    down_pe(0, n, ns)
                pe.nop()

        def norm_act(act, src, junk, base, tiles, use, stored=False, halves=None):
            with act.Fori(0, tiles) as i:
                if halves is not None:
                    act.wait_ge(halves, i * 2 + 6)
                act.activation(junk, src[:, ds(i, 1), :].rearrange("p o d -> p (o d)"), ACT.Square, accum_out=ss[:, ds(i, 1)]).then_inc(sem("ss_ready"), 1)
                act.drain()
            act.wait_ge(sem("ms_ready"), use)
            act.activation(rstd[:, 0:tiles], rstd[:, 0:tiles], ACT.Sqrt).then_inc(sem("rms_ready"), 1)
            act.wait_ge(sem("rstd_ready"), use)
            with act.Fori(0, tiles // 2) as i:
                for s in range(2):
                    act.wait_ge(sem("xs_free"), i * 2 + (base + s + 1))
                    if stored:
                        act.wait_ge(sem("xn_stored0") if s == 0 else sem("xn_stored1"), i * 16 + 16)
                    act.activation(xs[s], src[:, ds(i * 2 + s, 1), :].rearrange("p o (k d) -> p (o k) d", k=KT),
                                   ACT.Copy, scale=rstd[:, ds(i * 2 + s, 1)]).then_inc(sem("xs_ready"), 1)

        @block.scalar
        def _(act):
            act.dma_start(ldt, I["s5_log_dt"][0].rearrange("(q h) -> q h", q=PAIRS)).then_inc(sem("s5_loaded"), 16)
            for a, n in enumerate(("re", "im")):
                act.dma_start(Braw[a], I["s5_b_" + n][0].rearrange("(q h) n i -> (h n) q i", h=2)).then_inc(sem("s5_loaded"), 16)
                act.dma_start(Craw[a], I["s5_c_" + n][0].rearrange("(r g) o n -> (g o) r n", r=4)).then_inc(sem("s5_loaded"), 16)
            with nc.allow_non_contiguous_dma(reason="512 skip weights, once"):
                act.dma_start(s5d, I["s5_d"][0].rearrange("g i -> i g")).then_inc(sem("s5_loaded"), 16)
            act.wait_ge(*reached("pcol_ps"))
            act.activation(pcol[:, :], banks[7][:, 0:NROWS], ACT.Copy).then_inc(*reach("pcol_ready"))
            act.wait_ge(*reached("dt_ps"))
            act.activation(a5["dt"], banks[0][:, 0:16], ACT.Exp).then_inc(*reach("s5_dt"))
            act.wait_ge(*reached("s5_angle"))
            act.activation(a5["rho"], a5["are"], ACT.Exp)
            act.activation(a5["r8"], a5["are"], ACT.Exp, scale=float(TAU))
            act.activation(a5["sn"], a5["rr"], ACT.Sin)
            act.activation(a5["cs"], a5["ra"], ACT.Sin).then_inc(*reach("s5_trig"))
            act.wait_ge(*reached("c_ps"))
            act.wait_ge(sem("s5_loaded"), 96)
            for a in range(2):
                for h in range(2):
                    for r in range(4):
                        act.activation(Cst[a][64 * h:64 * h + 64, 4 * r:4 * r + 4, :],
                                       banks[1 + a][0:64, r * P:(r + 1) * P].rearrange("n (q h o) -> n h q o", h=2, o=GC)[:, h, :, :],
                                       ACT.Copy).then_inc(sem("c_evac"), 1)
            act.wait_ge(sem("x_loaded"), 16)
            norm_act(act, X, junk, 0, TT, 1)
            act.sem_inc(sem("z_evac"), 4)

            def u_act(j):
                for h in range(2):
                    act.wait_ge(sem("z_done"), 4 + 2 * j + h + 1)
                    act.activation(uT[:, j, :].rearrange("p (a c) -> p a c", a=TAU)[:, :, 64 * h:64 * h + 64],
                                   banks[2 * (j % 2) + h][:, :].rearrange("p (c a) -> p a c", a=TAU), ACT.Copy).then_inc(sem("z_evac"), 1)

            def tile_act(pos):
                s = pos % 2
                act.wait_ge(sem("pt_ready"), pos - 4 + 1)
                for h in range(2):
                    act.wait_ge(sem("z_done"), 4 + 2 * pos + h + 1)
                    act.activation(zbuf[s][:, 1 + 512 * h:513 + 512 * h], banks[2 * s + h][:, :], ACT.Copy).then_inc(sem("z_evac"), 1)

            u_act(0)
            u_act(1)
            for n in range(8):
                act.wait_ge(sem("w1_ps"), n + 1)
                act.activation(W1[n // 4][:, 4 * (n % 4):4 * (n % 4) + 4, :].rearrange("p q x -> p (q x)"), banks[4 + n % 2][:, :], ACT.Copy).then_inc(sem("w1_evac"), 1)
            u_act(2)
            u_act(3)
            for n in range(8):
                act.wait_ge(sem("kk_ps"), n + 1)
                q4, h = n // 2, n % 2
                act.activation(KK[:, 8 * q4 + h:8 * q4 + 8:2, :], banks[6 + h][0:16, :].rearrange("p (q x) -> p q x", q=4), ACT.Copy).then_inc(sem("kk_evac"), 1)
            tile_act(4)
            tile_act(5)
            tile_act(6)
            act.wait_ge(sem("pt_ready"), 2 + 2)
            act.activation(PT[0:64, 12, :], PT[0:64, 12, :], ACT.Tanh)
            act.activation(PT[:, 13, :], PT[:, 13, :], ACT.Sigmoid)
            act.drain()
            act.activation(small[:, 63:64], small[:, 8:9], ACT.Copy).then_inc(*reach("dwda_ready"))
            for j in range(J):
                avec, tmp = avecs[j], tmps[j]
                if j > 0:
                    tile_act(6 + 3 * j)
                tile_act(7 + 3 * j)
                act.wait_ge(sem("rates_ps"), j + 1)
                if j > 0:
                    act.wait_ge(sem("elem_done"), j)
                else:
                    act.wait_ge(sem("u_stored"), 16)
                    act.wait_ge(sem("s5_stored"), 64)
                for h in range(2):
                    act.activation(sig[:, 512 * h:512 * h + 512], banks[4 + h][:, :], ACT.Sigmoid, bias=col("w0", j)).then_inc(sem("rates_ready"), 1)
                    act.activation(avec[:, 512 * h:512 * h + 512], banks[6 + h][:, :], ACT.Sigmoid, bias=col("a0", j)).then_inc(sem("rates_ready"), 1)
                act.wait_ge(sem("kk0_ready"), j + 1)
                act.activation(tmp, kk, ACT.Square).then_inc(sem("kk_sq"), 1)
                act.wait_ge(sem("csum_ready"), j + 1)
                act.activation(gexp, csum, ACT.Exp, scale=-DECAY).then_inc(sem("gexp_ready"), 1)
                act.activation(ginv, csum, ACT.Exp, scale=DECAY).then_inc(sem("gexp_ready"), 1)
                act.wait_ge(sem("cprev_ready"), j + 1)
                act.activation(gprev, gprev, ACT.Exp, scale=-DECAY).then_inc(sem("gexp_ready"), 1)
                tile_act(8 + 3 * j)
                act.wait_ge(sem("kk_sum"), j + 1)
                act.wait_ge(sem("kk_sq"), j + 1)
                for h in range(2):
                    act.activation(tmp[:, 512 * h:512 * h + 512], banks[4 + h][:, :], ACT.Sqrt).then_inc(sem("kk_norm"), 1)
            for i in range(TT):
                b = 4 * (i % 2)
                act.wait_ge(sem("tok_ps"), i + 1)
                act.activation(Gt[:, i, :], banks[b + 1][:, :], ACT.Copy).then_inc(sem("gates_evac"), 1)
                act.activation(rks[:, i, :], banks[b + 2][:, 0:8], ACT.Copy).then_inc(sem("gates_evac"), 1)
            act.sem_inc(sem("Y_ready"), 2)
            act.wait_ge(*reached("bd_zero"))

            def diag(dst, src, event=None):
                for q in range(2):
                    a = act.activation(dst[64 * q:64 * q + 64, :, 64 * q:64 * q + 64], src(q), ACT.Copy)
                a.then_inc(event, 1)

            def pair_act(act, p, par, prep, state):
                n, np_ = p + 1, 1 - par
                for h in range(2 if prep else 0):
                    q, c = 2 * np_ + h, n * 2 + h
                    act.wait_ge(sem("PM_ready"), c * 2 + 4)
                    diag(LTbd[h], lambda a: PM[q][0:64, a:HEADS:2, 0:64], sem("LTbd_ready"))
                    act.wait_ge(sem("bkt_ps"), c + 3)
                    act.activation(BKT[q].rearrange("p j x -> p (j x)"), banks[3 + h][:, :], ACT.Copy)
                    act.wait_ge(sem("TS_new"), n * 12 + (h + 1))
                    diag(TTbd[q], lambda a: TS[h][64 * a:64 * a + 64, 1, :, :], sem("TS_ready"))
                for lv in range(1, 6):
                    for gap in range(2):
                        for h in range(2 if prep else 0):
                            if gap == 0:
                                act.wait_ge(sem("Xst_ready"), n * 10 + (2 * lv - 1 + h))
                                diag(Xbd[h], lambda a: Xst[h][64 * a:64 * a + 64, :, :], sem("Xbd_ready"))
                            else:
                                act.wait_ge(sem("TS_new"), n * 12 + (2 * lv + 1 + h))
                                diag(TTbd[2 * np_ + h], lambda a: TS[h][64 * a:64 * a + 64, 1, :, :], sem("TS_ready"))
                        if state and (lv, gap) in PIECES:
                            h, piece = PIECES[lv, gap]
                            c = p * 2 + h
                            if piece == 1:
                                act.wait_ge(sem("U_ps"), c + 1)
                                for q in range(2):
                                    act.activation(UV[h][0:64, q:HEADS:2, :], jx(banks[5][64 * q:64 * q + 64, 256:512]), ACT.Copy).then_inc(sem("U_ready"), 1)
                            elif piece == 3:
                                act.wait_ge(sem("y_ps"), c + 5)
                                act.activation(Yt[64 * h:64 * h + 64, ds(p, 1), :].rearrange("p o c -> p (o c)"),
                                               banks[7][64 * h:64 * h + 64, :], ACT.Copy).then_inc(sem("Y_ready"), 1)

            pairs(act, pair_act)
            for n in range(8):
                act.wait_ge(sem("e_ps"), n + 1)
                act.activation(E5[n % 2][:, 512 * (n // 2):512 * (n // 2) + 512], banks[n % 4][:, :], ACT.Copy).then_inc(sem("e_evac"), 1)
            for n in range(8):
                act.wait_ge(sem("y5_ps"), n + 1)
                q4, h = n // 2, n % 2
                act.activation(y5.rearrange("p (g c) -> p g c", g=GROUPS)[:, 8 * q4 + h:8 * q4 + 8:2, :],
                               banks[n % 4][:, :].rearrange("p (q c) -> p q c", q=4), ACT.Gelu_apprx_tanh).then_inc(sem("gelu_done"), 1)
                if n == 3:
                    act.wait_ge(*reached("gn_centred"))
                    act.activation(gtmp, unit(16, 4), ACT.Square).then_inc(*reach("gn_sq"))
            act.wait_ge(*reached("gn_var"))
            act.activation(gstat[:, 1, :], gstat[:, 1, :], ACT.Sqrt).then_inc(*reach("gn_std"))
            for n in range(8):
                act.wait_ge(sem("glu_ps"), n + 1)
                if n >= 2:
                    act.wait_ge(sem("ymix_s5"), n - 1)
                act.activation(sglu[:, 512 * (n % 2):512 * (n % 2) + 512], banks[n % 4][:, :], ACT.Sigmoid, bias=col("b_glu", n // 2)).then_inc(sem("glu_evac"), 1)
            for i in range(TT):
                act.wait_ge(sem("ymixT_ps"), i + 1)
                act.activation(ymixT[:, 0:4, i * P:(i + 1) * P], banks[4 + i % 2][:, :].rearrange("p (k t) -> p k t", k=4), ACT.Copy).then_inc(sem("ymix_rwkv"), 1)
            act.sem_inc(sem("kT_ready"), 2)
            act.sem_inc(sem("qr_ready"), 2)
            norm_act(act, Xr, junk2, 8, TT, 2, halves=sem("mix_added"))
            act.wait_ge(sem("xm_loaded"), 16)
            norm_act(act, Xm, junk2, 16, 2, 3)
            with act.Fori(0, KT // 2) as mm:
                for s in range(2):
                    act.wait_ge(sem("k_ps"), mm * 2 + (s + 3))
                    act.activation(kT[:, ds(mm * 2 + s, 1), :].rearrange("p o m -> p (o m)"), banks[s][:, 0:MEM], ACT.Copy).then_inc(sem("kT_ready"), 1)

            def queries_act(t, s):
                for h in range(2):
                    act.wait_ge(sem("q_ps"), t * 2 + (h + 1))
                    act.activation(qr[s][:, 4 * h:4 * h + 4, :].rearrange("p k t -> p (k t)"), banks[h][:, :], ACT.Copy).then_inc(sem("qr_ready"), 1)

            def attend_act(t, s, last):
                act.wait_ge(sem("smx_ready"), t + 1)
                for h in range(XH):
                    act.activation(pr_[:, h, :], banks[2 + h // 2][:, (h % 2) * MEM:(h % 2 + 1) * MEM], ACT.Exp, bias=smx[s][:, h:h + 1],
                                   scale=1.0 / 16.0, accum_out=ssum[s][:, h:h + 1]).then_inc(sem("exp_done"), 1)
                if not last:
                    queries_act(t + 1, 1 - s)
                act.wait_ge(sem("pT_ps"), t + 1)
                for i in range(2):
                    act.activation(pT[:, i, :, :].rearrange("p h t -> p (h t)"), banks[4 + i][:, :], ACT.Copy).then_inc(sem("pT_ready"), 1)
                act.wait_ge(sem("o_ps"), t + 1)
                for h in range(2):
                    act.activation(oR[s][:, 4 * h:4 * h + 4, :].rearrange("p k t -> p (k t)"), banks[6 + h][:, :], ACT.Copy).then_inc(sem("o_ready"), 1)

            act.sem_inc(sem("o_ready"), 2)
            queries_act(0, 0)
            with act.Fori(0, TT // 2 - 1) as ii:
                for s in range(2):
                    attend_act(ii * 2 + s, s, False)
            attend_act(TT - 2, 0, False)
            attend_act(TT - 1, 1, True)
            norm_act(act, Xr, unit(17), 18, TT, 4, stored=True, halves=sem("x_attn"))
            act.wait_ge(*reached("l1_ready"))
            act.activation(e8[0][:, :, 0:NG], e8[0][:, :, 0:NG], ACT.Exp).then_inc(*reach("exp_l1"))
            act.wait_ge(*reached("dv_ready"))
            act.activation(s8[6], s8[6], ACT.Exp).then_inc(*reach("exp_dv"))
            act.wait_ge(*reached("slots_ready"))
            act.sem_inc(sem("sg_ready"), 1)
            act.sem_inc(sem("hidT_ready"), 1)
            act.sem_inc(sem("y_evac0"), 1)
            act.sem_inc(sem("y_stored0"), 16)
            act.sem_inc(sem("y_stored1"), 16)

            def gate_act(n):
                act.wait_ge(sem("gate_ps"), n + 1)
                act.wait_ge(sem("hid_ready"), n + 1)
                act.activation(sg, banks[2][:, :], ACT.Silu).then_inc(sem("sg_ready"), 1)

            def hidden_act(n):
                act.wait_ge(sem("hidT_ps"), n + 2)
                act.wait_ge(sem("dn_ps"), n * 2 + 4)
                act.activation(hidT.rearrange("p k t -> p (k t)"), banks[4][:, :], ACT.Copy).then_inc(sem("hidT_ready"), 1)

            def down_act(s, n, ns):
                stored = sem("y_stored0") if s == 0 else sem("y_stored1")
                act.wait_ge(sem("dn_ps"), n * 2 + 5)
                act.wait_ge(stored, ns * 16 + 16)
                act.activation(ysb[s][:, 0:512], banks[5][:, :], ACT.Copy).then_inc(sem("y_evac0"), 1)
                act.wait_ge(sem("y_evac0"), n + 2)
                act.wait_ge(sem("y_evac1"), n + 2)
                act.dma_start(d_y[ds(n * P, P), :], ysb[s]).then_inc(stored, 16)

            def experts_act(act, s, n, ns, last=False):
                hidden_act(n)
                if not last:
                    gate_act(n + 1)
                down_act(s, n, ns)

            gate_act(0)
            blocks(act, experts_act)
            n_over = act.value_load(nover_i[0:1, :], min_val=0, max_val=OVER)
            with act.Fori(0, OVER) as o:
                with act.If(o < n_over):
                    gate_act(o + NE)
                    hidden_act(o + NE)
                    down_act(0, o + NE, o + NE // 2)
                act.nop()
            act.wait_ge(sem("y_added"), 2 * TT)
            with act.Fori(0, TT) as i:
                act.activation(unit(16), Xr[:, ds(i, 1), :].rearrange("p o d -> p (o d)"), ACT.Square, accum_out=ss[:, ds(i, 1)]).then_inc(sem("ss_ready"), 1)
                act.drain()
            act.wait_ge(sem("ms_ready"), 5)
            act.activation(rstd[:, :], rstd[:, :], ACT.Sqrt).then_inc(sem("rms_ready"), 1)


        def norm_dve(dve, wname, dst, base, tiles, use):
            dve.wait_ge(sem("ss_ready"), base + tiles)
            dve.tensor_scalar(rstd[:, 0:tiles], ss[:, 0:tiles], 1.0 / D, EPS, ALU.mult, ALU.add).then_inc(sem("ms_ready"), 1)
            dve.wait_ge(sem("rms_ready"), use)
            dve.reciprocal(rstd[:, 0:tiles], rstd[:, 0:tiles]).then_inc(sem("rstd_ready"), 1)
            gain = cols(wname).rearrange("p (k o) -> p k o", o=1)
            with dve.Fori(0, tiles // 2) as i:
                for s in range(2):
                    for q in range(2):
                        dve.wait_ge(sem("xsT_ps"), i * 4 + (2 * base + 2 * s + q + 1))
                        if q == 1:
                            dve.sem_inc(sem("xs_free"), 1)
                        dve.tensor_tensor(dst[:, 4 * q:4 * q + 4, ds(i * 256 + s * 128, P)],
                                          banks[4 + 2 * s + q][:, :].rearrange("p (k t) -> p k t", k=4),
                                          gain[:, 4 * q:4 * q + 4, :].to_broadcast((P, 4, P)), ALU.mult).then_inc(sem("hT_ready"), 1)

        @block.vector
        def _(dve):
            dve.sem_inc(sem("hT_ready"), 4)
            dve.sem_inc(sem("xs_free"), 2)
            dve.sem_inc(sem("pt_ready"), 2)
            for z in zbuf:
                dve.memset(z[:, 0:1], 0.0)
            dve.wait_ge(*reached("pcol_ready"))

            def tt(o, a, b, op):
                dve.tensor_tensor(o, a, b, op)
                dve.drain()

            def tsc(o, a, s1, s2, o1, o2=None):
                if o2 is None:
                    dve.tensor_scalar(o, a, s1, None, o1)
                else:
                    dve.tensor_scalar(o, a, s1, s2, o1, o2)
                dve.drain()

            dve.wait_ge(sem("s5_loaded"), 96)
            dve.tensor_copy(ldrow.rearrange("p (h n) -> p h n", h=2), ldt.rearrange("p (h o) -> p h o", o=1).to_broadcast((16, 2, NS))).then_inc(*reach("ldrow_ready"))
            lre, lim = cols("s5_lam_re"), cols("s5_lam_im")
            A = a5
            dve.wait_ge(*reached("s5_dt"))
            tt(A["are"], lre, A["dt"], ALU.mult)
            tt(A["th"], lim, A["dt"], ALU.mult)
            tsc(A["kr"], A["th"], 1.0 / TWO_PI, None, ALU.mult)
            tsc(A["kr"], A["kr"], 12582912.0, None, ALU.add)
            tsc(A["kr"], A["kr"], -12582912.0, None, ALU.add)
            c1 = 6.28125
            c2 = float(np.float32(np.round((TWO_PI - c1) * 2 ** 20) / 2 ** 20))
            c3 = float(np.float32(TWO_PI - c1 - c2))
            dve.scalar_tensor_tensor(A["rr"], A["kr"], -c1, A["th"], ALU.mult, ALU.add)
            dve.drain()
            for c in (c2, c3):
                dve.scalar_tensor_tensor(A["rr"], A["kr"], -c, A["rr"], ALU.mult, ALU.add)
                dve.drain()
            tsc(A["rr"], A["rr"], 3.1415925, -3.1415925, ALU.min, ALU.max)
            dve.scalar_tensor_tensor(A["ra"], A["rr"], -1.0, A["rr"], ALU.mult, ALU.min)
            dve.drain()
            dve.tensor_scalar(A["ra"], A["ra"], float(np.pi / 2), None, ALU.add).then_inc(*reach("s5_angle"))
            dve.wait_ge(*reached("s5_trig"))
            tt(A["lr"], A["rho"], A["cs"], ALU.mult)
            tt(A["li"], A["rho"], A["sn"], ALU.mult)

            def cmul(o, a, b, t, conj=False):
                dve.tensor_tensor(t[0], a[0], b[0], ALU.mult)
                dve.tensor_tensor(t[1], a[1], b[1], ALU.mult)
                dve.tensor_tensor(t[2], a[0], b[1], ALU.mult)
                dve.tensor_tensor(t[3], a[1], b[0], ALU.mult)
                dve.drain()
                dve.tensor_tensor(o[0], t[0], t[1], ALU.add if conj else ALU.subtract)
                dve.tensor_tensor(o[1], t[2], t[3], ALU.subtract if conj else ALU.add)
                dve.drain()

            T4 = [A["t1"], A["t2"], A["t3"], A["t4"]]
            tsc(A["nr"], A["lr"], -1.0, None, ALU.add)
            tt(A["t1"], lre, lre, ALU.mult)
            tt(A["t2"], lim, lim, ALU.mult)
            tt(A["den"], A["t1"], A["t2"], ALU.add)
            dve.reciprocal(A["den"], A["den"])
            dve.drain()
            cmul((A["cr"], A["ci"]), (lre, lim), (A["nr"], A["li"]), T4, conj=True)
            tt(A["cr"], A["cr"], A["den"], ALU.mult)
            tt(A["ci"], A["ci"], A["den"], ALU.mult)
            q_ = lambda v, n: v.rearrange("p (q o) -> p q o", o=1).to_broadcast((P, PAIRS, n))
            tmp4 = [s5_tmp[:, 256 * i:256 * i + 256].rearrange("p (q i) -> p q i", q=PAIRS) for i in range(4)]
            cmul(Bbar, (q_(A["cr"], GC), q_(A["ci"], GC)), Braw, tmp4)
            dve.memset(pw[0][:, 0, :], 1.0)
            dve.memset(pw[1][:, 0, :], 0.0)
            dve.tensor_copy(pw[0][:, 1, :], A["lr"])
            dve.tensor_copy(pw[1][:, 1, :], A["li"])
            dve.drain()
            for n in range(2, TAU + 1):
                cmul((pw[0][:, n, :], pw[1][:, n, :]), (pw[0][:, n - 1, :], pw[1][:, n - 1, :]), (A["lr"], A["li"]), T4)
            dve.wait_ge(sem("c_evac"), 16)
            def kq(v, k0, n, rev=False):
                return v[:, k0:k0 + n, :].rearrange("p k (q o) -> p q k o", o=1).to_broadcast((P, PAIRS, n, GC))
            def qx(v, n):
                return v.rearrange("p q (o x) -> p q o x", o=1).to_broadcast((P, PAIRS, n, GC))
            w4 = lambda v: v.rearrange("p q (k x) -> p q k x", x=GC)
            sc = s5_tmp[:, 0:2304].rearrange("p (q k x) -> p q k x", q=PAIRS, k=9)
            for a in range(2):
                dve.tensor_tensor(w4(W2[a]), kq(pw[0], 0, 9), qx(Cst[a], 9), ALU.mult)
                dve.tensor_tensor(sc, kq(pw[1], 0, 9), qx(Cst[1 - a], 9), ALU.mult)
                dve.drain()
                if a == 0:
                    tt(w4(W2[0]), w4(W2[0]), sc, ALU.subtract)
                else:
                    dve.scalar_tensor_tensor(W2[1].rearrange("p q x -> p (q x)"), W2[1].rearrange("p q x -> p (q x)"), -1.0,
                                             sc.rearrange("p q k x -> p (q k x)"), ALU.mult, ALU.subtract).then_inc(*reach("w2_ready"))
                    dve.drain()
            norm_dve(dve, "norm_mix_w", hT, 0, TT, 1)
            dve.tensor_scalar(omka[:, :], cols("k_a"), -1.0, 1.0, ALU.mult, ALU.add)
            dve.memset(rkc[:, :, :], 0.0)
            dve.drain()
            for p in range(2):
                m = dve.tensor_copy(rkc[64 * p:64 * p + 64, :, p:p + 1],
                                cols("r_k")[64 * p:64 * p + 64, :].rearrange("p (j o) -> p j o", o=1))
            m.then_inc(*reach("rkc_ready"))
            for a in range(2):
                for k in range(TAU):
                    dve.tensor_copy(pwr[a][:, k, :], pw[a][:, TAU - 1 - k, :])
            dve.drain()
            sv = s5_tmp[:, 0:2048].rearrange("p (q k x) -> p q k x", q=PAIRS, k=TAU)
            for a in range(2):
                dve.tensor_tensor(w4(V1[a]), kq(pwr[0], 0, 8), qx(Bbar[a], 8), ALU.mult)
                dve.tensor_tensor(sv, kq(pwr[1], 0, 8), qx(Bbar[1 - a], 8), ALU.mult)
                dve.drain()
                m = dve.tensor_tensor(w4(V1[a]), w4(V1[a]), sv, ALU.subtract if a == 0 else ALU.add)
                dve.drain()
            m.then_inc(*reach("v1_ready"))
            p1, p2 = ("pr", "pi"), ("pr2", "pi2")
            cmul((A["pr"], A["pi"]), (A["cs"], A["sn"]), (A["cs"], A["sn"]), T4)
            cmul((A["pr2"], A["pi2"]), (A["pr"], A["pi"]), (A["pr"], A["pi"]), T4)
            cmul((A["pr"], A["pi"]), (A["pr2"], A["pi2"]), (A["pr2"], A["pi2"]), T4)
            dve.wait_ge(sem("w1_evac"), 8)
            tg = [v.rearrange("p (q c) -> p q c", q=PAIRS) for v in trig0]
            dve.memset(tg[0][:, :, 0:1], 1.0)
            dve.memset(tg[1][:, :, 0:1], 0.0)
            dve.drain()
            n = 1
            while n < SC:
                b = [v.rearrange("p (q o) -> p q o", o=1).to_broadcast((P, PAIRS, n)) for v in (A[p1[0]], A[p1[1]])]
                t = [s5_tmp[:, 1024 * i:1024 * i + 16 * n].rearrange("p (q c) -> p q c", q=PAIRS) for i in range(4)]
                cmul([v[:, :, n:2 * n] for v in tg], [v[:, :, 0:n] for v in tg], b, t)
                cmul([A[x] for x in p2], [A[x] for x in p1], [A[x] for x in p1], T4)
                p1, p2 = p2, p1
                n *= 2
            dve.sem_inc(*reach("trig_ready"))
            dve.wait_ge(sem("kk_evac"), 8)
            d3 = s5_tmp[0:16, 0:512].rearrange("p (g x) -> p g x", g=GROUPS)
            tt(d3, ident[0:16, 0:16].rearrange("p (o x) -> p o x", o=1).to_broadcast((16, GROUPS, GC)),
               s5d.rearrange("p (g o) -> p g o", o=1).to_broadcast((16, GROUPS, GC)), ALU.mult)
            dve.tensor_tensor(KK[:, :, 0:GC], KK[:, :, 0:GC], d3, ALU.add).then_inc(*reach("kk_ready"))
            dve.drain()

            def shift_tile(pos):
                s, m = pos % 2, SHIFTED[pos - 4]
                dve.wait_ge(sem("z_evac"), 4 + 2 * pos + 2)
                dve.tensor_tensor(shift_d, zbuf[s][:, 0:1024], zbuf[s][:, 1:1025], ALU.subtract)
                dve.drain()
                dve.scalar_tensor_tensor(PT[:, m, :], shift_d, col("mu_shift", m), zbuf[s][:, 1:1025], ALU.mult, ALU.add).then_inc(sem("pt_ready"), 1)
                dve.drain()

            dve.wait_ge(*reached("consts_b"))
            shift_tile(4)
            shift_tile(5)
            dve.wait_ge(sem("y_zeroed"), 16)
            dve.wait_ge(sem("s5_stored"), 64)
            dve.wait_ge(sem("u_stored"), 16)
            for j in range(J):
                avec, tmp = avecs[j], tmps[j]
                shift_tile(6 + 3 * j)
                shift_tile(7 + 3 * j)
                ch = lambda v: v.rearrange("p (c x) -> p c x", x=CH)
                r, k = PT[:, j, :], PT[:, 4 + j, :]
                dve.tensor_scalar(kk, k, col("k_k", j), None, ALU.mult).then_inc(sem("kk0_ready"), 1)
                dve.wait_ge(sem("rates_ready"), 4 * j + 4)
                dve.wait_ge(*reached("reset_a" if j < J - 1 else "reset_b"))
                dve.tensor_tensor_scan(csum, resets[j], sig, 0.0, ALU.mult, ALU.add).then_inc(sem("csum_ready"), 1)
                dve.wait_ge(sem("csum_ready"), j + 1)
                dve.tensor_tensor(gprev, csum, sig, ALU.subtract).then_inc(sem("cprev_ready"), 1)
                dve.wait_ge(sem("cprev_ready"), j + 1)
                dve.tensor_scalar(sig, avec, col("k_a", j), omka[:, j:j + 1], ALU.mult, ALU.add)
                dve.drain()
                dve.tensor_tensor(k, k, sig, ALU.mult)
                shift_tile(8 + 3 * j)
                dve.wait_ge(sem("kk_norm"), 2 * j + 2)
                dve.tensor_scalar(tmp, tmp, 1e-12, None, ALU.max)
                dve.drain()
                dve.reciprocal(tmp, tmp)
                dve.drain()
                dve.tensor_tensor(kk, kk, tmp, ALU.mult)
                dve.wait_ge(sem("gexp_ready"), 3 * j + 3)
                dve.drain()
                dve.scalar_tensor_tensor(AR[:, j, :, 0:64], ch(kk), -1.0, ch(gprev), ALU.mult, ALU.mult)
                dve.tensor_tensor(AR[:, j, :, 64:128], ch(r), ch(gexp), ALU.mult)
                dve.tensor_tensor(avec, avec, kk, ALU.mult)
                dve.tensor_tensor(BK[:, j, :, 64:128], ch(k), ch(ginv), ALU.mult)
                dve.drain()
                dve.tensor_tensor(BK[:, j, :, 0:64], ch(avec), ch(ginv), ALU.mult)
                dve.tensor_tensor(r, r, k, ALU.mult)
                dve.tensor_copy(gcol[:, :, j:j + 1], ch(gexp)[:, :, 63:64]).then_inc(sem("elem_done"), 1)
                dve.drain()
            for i in range(TT):
                dve.wait_ge(sem("tok_ps"), i + 1)
                if i == 0:
                    dve.wait_ge(sem("elem_done"), J)
                dve.tensor_copy(Vt[:, i, :], banks[4 * (i % 2)][:, :]).then_inc(sem("values_evac"), 1)
            dve.wait_ge(*reached("bd_zero"))
            dve.wait_ge(*reached("consts_b"))
            dve.sem_inc(sem("Z_ready"), 1)
            heads = lambda m, n: m.rearrange("p (o x) -> p o x", o=1).to_broadcast((m.shape[0], n, m.shape[1]))
            dve.sem_inc(sem("PM_ready"), 2)

            def prepare_dve(n, par, h, first):
                c, q = n * 2 + h, 2 * par + h
                dve.wait_ge(sem("y_ps"), c + 1)
                for x in range(2):
                    dve.wait_ge(sem("pm_ps"), c * 2 + (x + 1))
                    dve.tensor_tensor(PM[q][:, 4 * x:4 * x + 4, :], banks[x][:, :].rearrange("p (h x) -> p h x", h=4),
                                      heads(pmask[:, :], 4), ALU.mult).then_inc(sem("PM_ready"), 1)
                if not first:
                    dve.wait_ge(sem("TS_ready"), n * 12 + (h - 1))
                dve.wait_ge(sem("L_ps"), c + 1)
                dve.tensor_tensor(TS[h][:, 0, :, :], jx(LB[h][:, 0:256]), heads(lmask[:, 0, :], J), ALU.mult)
                dve.drain()
                for x in range(2):
                    dve.tensor_tensor(TS[h][64 * x:64 * x + 64, 1, :, :], PM[q][0:64, x:HEADS:2, 0:64], heads(lmask1T[0:64, :], J), ALU.mult)
                dve.drain()
                v = TS[h].rearrange("p a j x -> p (a j) x")
                dve.tensor_tensor(v, v, heads(eye[:, :], 2 * J), ALU.add).then_inc(sem("TS_new"), 1)

            def pair_dve(dve, p, par, prep, state):
                n, np_ = p + 1, 1 - par
                if prep:
                    for h in range(2):
                        prepare_dve(n, np_, h, not state)
                for lv in range(1, 6):
                    for gap in range(2):
                        if gap == 1:
                            dve.drain()
                        for h in range(2 if prep else 0):
                            if gap == 0:
                                dve.wait_ge(sem("X_ps"), n * 10 + (2 * lv - 1 + h))
                                dve.tensor_tensor(Xst[h], jx(LB[h][:, 0:256]), heads(lmask[:, lv, :], J), ALU.mult).then_inc(sem("Xst_ready"), 1)
                            else:
                                dve.wait_ge(sem("D_ps"), n * 10 + (2 * lv - 1 + h))
                                v = TS[h].rearrange("p a j x -> p (a j x)")
                                dve.tensor_tensor(v, v, banks[3 + h][:, :], ALU.add).then_inc(sem("TS_new"), 1)
                        if state and (lv, gap) in PIECES:
                            h, piece = PIECES[lv, gap]
                            c = p * 2 + h
                            if piece == 0:
                                dve.wait_ge(sem("Q_ps"), c + 1)
                                dve.tensor_copy(Qst.rearrange("p j x -> p (j x)"), banks[5][:, 0:256]).then_inc(sem("Q_ready"), 1)
                            elif piece == 2:
                                dve.drain()
                                dve.wait_ge(sem("M_ps"), c + 1)
                                dve.tensor_tensor(Ztmp, Zst, jx(banks[5][:, 0:256]), ALU.add)
                                dve.drain()
                                gc = gcol[:, ds(c, 1), :].rearrange("p o j -> p (o j)").rearrange("p (j o) -> p j o", o=1)
                                for x in range(2):
                                    r = slice(64 * x, 64 * x + 64)
                                    gx = gcol[64 * x:64 * x + 64, ds(c, 1), :].rearrange("p o j -> p (o j)").rearrange("p (j o) -> p j o", o=1)
                                    m = dve.tensor_tensor(Zbd[r, :, 64 * x:64 * x + 64], Ztmp[r, :, :], gx.to_broadcast((64, J, 64)), ALU.mult)
                                m.then_inc(sem("Z_ready"), 1)
                                dve.tensor_tensor(Zst, Ztmp, gc.to_broadcast((P, J, 64)), ALU.mult)
                dve.drain()

            pairs(dve, pair_dve)
            dve.sem_inc(*reach("states_done"))
            dve.wait_ge(sem("xg_loaded"), 16 * TAU)
            dve.tensor_copy(Rtab.rearrange("p (q c) -> p q c", q=PAIRS), q_(A["r8"], SC))
            dve.drain()
            dve.memset(Rtab.rearrange("p (q c) -> p q c", q=PAIRS)[:, :, 0:1], 0.0)
            dve.wait_ge(sem("e_evac"), 8)
            dve.wait_ge(sem("trig_loaded"), 16)
            z4 = [zst[0], zst[1], rot[0], rot[1]]
            cmul((E5[0], E5[1]), (trig[0], trig[1]), (E5[0], E5[1]), z4, conj=True)
            for a in range(2):
                dve.tensor_tensor_scan(zst[a], Rtab, E5[a], 0.0, ALU.mult, ALU.add)
            dve.drain()
            tg1 = [v.rearrange("p (q c) -> p q c", q=PAIRS)[:, :, 0:SC - 1] for v in (*trig, *zst, *Sprev, *E5)]
            sh = [v.rearrange("p (q c) -> p q c", q=PAIRS) for v in Sprev]
            for o, c in enumerate((ALU.subtract, ALU.add)):
                dve.tensor_tensor(tg1[6], tg1[0], tg1[2 + o], ALU.mult)
                dve.tensor_tensor(tg1[7], tg1[1], tg1[3 - o], ALU.mult)
                dve.memset(sh[o][:, :, 0:1], 0.0)
                dve.drain()
                m = dve.tensor_tensor(sh[o][:, :, 1:SC], tg1[6], tg1[7], c)
                if o == 1:
                    m.then_inc(*reach("sprev_ready"))
                dve.drain()
            act_y = unit(16, 4)
            Y3 = act_y.rearrange("p (g x) -> p g x", x=HD)
            bc = lambda v: v.rearrange("p (g o) -> p g o", o=1).to_broadcast((P, TT * HEADS, HD))

            dve.wait_ge(sem("Y_ready"), 2 + NC)
            dve.tensor_reduce(gstat[:, 0, :], Y3, AX_X, ALU.add)
            dve.drain()
            tsc(gstat[:, 0, :], gstat[:, 0, :], 1.0 / HD, None, ALU.mult)
            dve.tensor_tensor(Y3, Y3, bc(gstat[:, 0, :]), ALU.subtract).then_inc(*reach("gn_centred"))
            Vg = unit(12, 4).rearrange("p (g x) -> p g x", x=HD)
            tt(Vg, Vg, bc(rks.rearrange("p i h -> p (i h)")), ALU.mult)
            dve.wait_ge(*reached("gn_sq"))
            dve.tensor_reduce(gstat[:, 1, :], gtmp.rearrange("p (g x) -> p g x", x=HD), AX_X, ALU.add)
            dve.drain()
            dve.tensor_scalar(gstat[:, 1, :], gstat[:, 1, :], 1.0 / HD, 64e-5, ALU.mult, ALU.add).then_inc(*reach("gn_var"))
            dve.wait_ge(*reached("gn_std"))
            dve.reciprocal(gstat[:, 2, :], gstat[:, 1, :])
            dve.drain()
            tt(Y3, Y3, bc(gstat[:, 2, :]), ALU.mult)
            ln = lambda a: lnwb[:, 512 * a:512 * a + 512].rearrange("p (o c) -> p o c", o=1).to_broadcast((P, TT, 512))
            dve.wait_ge(sem("ln_loaded"), 32)
            tt(Yt, Yt, ln(0), ALU.mult)
            tt(Yt, Yt, ln(1), ALU.add)
            tt(Yt, Yt, Vt, ALU.add)
            dve.tensor_tensor(Yt, Yt, Gt, ALU.mult).then_inc(*reach("gn_done"))
            dve.drain()
            for n in range(8):
                m4, h = n // 2, n % 2
                dve.wait_ge(sem("glu_evac"), n + 1)
                if n == 0:
                    dve.wait_ge(sem("zT_loaded"), 16)
                o = ymixT[:, 4 + m4, :].rearrange("p (c a) -> p a c", a=TAU)[:, 4 * h:4 * h + 4, :]
                dve.tensor_tensor(o, sglu[:, 512 * (n % 2):512 * (n % 2) + 512].rearrange("p (a c) -> p a c", a=4),
                                  zT[:, m4, 512 * h:512 * h + 512].rearrange("p (a c) -> p a c", a=4), ALU.mult).then_inc(sem("ymix_s5"), 1)
            dve.sem_inc(sem("mix_added"), 4)
            dve.wait_ge(sem("xr_loaded"), 32)
            with dve.Fori(0, TT // 2) as ii:
                for s in range(2):
                    for h in range(2):
                        dve.wait_ge(sem("mix_ps"), ii * 4 + (4 + 2 * s + h + 1))
                        v = Xr[:, ds(ii * 2 + s, 1), 512 * h:512 * h + 512].rearrange("p o d -> p (o d)")
                        dve.tensor_tensor(v, v, banks[2 * s + h][:, :], ALU.add).then_inc(sem("mix_added"), 1)
            dve.wait_ge(sem("mix_added"), 4 + 2 * TT)
            norm_dve(dve, "norm_xattn_w", hB, 8, TT, 2)
            norm_dve(dve, "norm_mem_w", hM, 16, 2, 3)
            for i in range(2):
                for h in range(2):
                    dve.wait_ge(sem("v_ps"), 2 * i + h + 1)
                    dve.tensor_copy(vM[:, i, 512 * h:512 * h + 512], banks[2 + h + 2 * i][:, :]).then_inc(sem("vM_ready"), 1)
            dve.sem_inc(sem("p_ready"), 1)
            dve.sem_inc(sem("x_attn"), 4)

            def attend_dve(t, s):
                dve.wait_ge(sem("s_ps"), t + 1)
                for h in range(2):
                    dve.tensor_reduce(smx[s][:, 2 * h:2 * h + 2], banks[2 + h][:, :].rearrange("p (h m) -> p h m", h=2), AX_X, ALU.max)
                dve.drain()
                dve.tensor_scalar(smx[s], smx[s], -1.0 / 16.0, None, ALU.mult).then_inc(sem("smx_ready"), 1)
                dve.wait_ge(sem("exp_done"), t * 4 + 4)
                dve.reciprocal(ssum[s], ssum[s])
                dve.drain()
                dve.tensor_tensor(pr_, pr_, ssum[s].rearrange("p (h o) -> p h o", o=1).to_broadcast((P, XH, MEM)), ALU.mult).then_inc(sem("p_ready"), 1)
                for h in range(2):
                    dve.wait_ge(sem("oproj_ps"), t * 2 + (h + 1))
                    v = Xr[:, ds(t, 1), 512 * h:512 * h + 512].rearrange("p o d -> p (o d)")
                    dve.tensor_tensor(v, v, banks[4 + h][:, :], ALU.add).then_inc(sem("x_attn"), 1)

            with dve.Fori(0, TT // 2) as ii:
                for s in range(2):
                    attend_dve(ii * 2 + s, s)
            dve.sem_inc(sem("xn_stored0"), 16)
            dve.sem_inc(sem("xn_stored1"), 16)
            norm_dve(dve, "norm_moe_w", hB, 18, TT, 4)
            dve.wait_ge(*reached("logits_ps"))
            dve.wait_ge(*reached("router_consts"))
            b3 = lambda v, n: v.rearrange("p (o e) -> p o e", o=1).to_broadcast((P, TT, n))
            c3 = lambda v, n: v.rearrange("p (i o) -> p i o", o=1).to_broadcast((P, TT, n))
            tt(LG, banks[0][:, 0:288].rearrange("p (i e) -> p i e", i=TT), b3(brt, 36), ALU.add)
            l1 = LG[:, :, 0:NG]

            def red(o, a, op):
                dve.tensor_reduce(o, a, AX_X, op)
                dve.drain()

            def first_of_max(o, best, a, n, iob, t):
                red(best, a, ALU.max)
                tt(t, a, c3(best, n), ALU.is_equal)
                tsc(t, t, -2.0 * EPG, None, ALU.mult)
                tt(t, t, b3(iob, n), ALU.add)
                red(o, t, ALU.min)

            grp, m1, s1, i0, v0, i1, v1 = s8[0], s8[1], s8[2], s8[3], s8[4], s8[5], s8[7]
            first_of_max(grp, m1, l1, NG, io4b, e8[1][:, :, 0:NG])
            tsc(grp, grp, float(EPG), None, ALU.add)
            dve.tensor_tensor(e8[0][:, :, 0:NG], l1, c3(m1, NG), ALU.subtract).then_inc(*reach("l1_ready"))
            tt(e8[1][:, :, 0:NG], b3(io32[:, 0:NG], NG), c3(grp, NG), ALU.is_equal)
            tt(l2.rearrange("p i (g e) -> p i g e", g=NG), LG[:, :, NG:36].rearrange("p i (g e) -> p i g e", g=NG),
               e8[1][:, :, 0:NG].rearrange("p i (g o) -> p i g o", o=1).to_broadcast((P, TT, NG, EPG)), ALU.mult)
            red(e8[2], l2.rearrange("p i (g e) -> p i e g", g=NG), ALU.add)
            first_of_max(i0, v0, e8[2], EPG, io8b, e8[3])
            tt(e8[3], b3(io32[:, 0:EPG], EPG), c3(i0, EPG), ALU.is_equal)
            tsc(e8[3], e8[3], -3.0e38, None, ALU.mult)
            tt(e8[2], e8[2], e8[3], ALU.add)
            first_of_max(i1, v1, e8[2], EPG, io8b, e8[3])
            dve.tensor_tensor(s8[6], v1, v0, ALU.subtract).then_inc(*reach("dv_ready"))
            dve.drain()
            dve.wait_ge(*reached("exp_dv"))
            red(s1, e8[0][:, :, 0:NG], ALU.add)
            tsc(s8[8], s8[6], 1.0, None, ALU.add)
            tt(s8[8], s8[8], s1, ALU.mult)
            dve.reciprocal(gates[:, 0:8], s8[8])
            dve.drain()
            tt(gates[:, 8:16], gates[:, 0:8], s8[6], ALU.mult)
            tsc(grp, grp, float(EPG), None, ALU.mult)
            for a, i in enumerate((i0, i1)):
                tt(i, i, grp, ALU.add)
                tt(O2[a], b3(io32, NE), c3(i, NE), ALU.is_equal)
            tt(MS, O2[0], O2[1], ALU.add)
            dve.memset(MA[:, 0, :], 0.0)
            dve.drain()
            for i in range(1, TT):
                tt(MA[:, i, :], MA[:, i - 1, :], MS[:, i - 1, :], ALU.add)
            dve.tensor_tensor(c32[0], MA[:, TT - 1, :], MS[:, TT - 1, :], ALU.add).then_inc(*reach("marks_ready"))
            dve.wait_ge(*reached("ranks_ps"))
            tt(cmpb, banks[1][:, 256:288].rearrange("p (e o) -> p e o", o=1).to_broadcast((P, NE, 7)),
               ioM.rearrange("p (o m) -> p o m", o=1).to_broadcast((P, NE, 7)), ALU.is_gt)
            red(c32[1], cmpb, ALU.add)
            dve.tensor_tensor_scan(c32[2], ones[:, 0:NE], c32[1], 0.0, ALU.mult, ALU.add)
            dve.drain()
            tt(c32[3], c32[2], c32[1], ALU.subtract)
            dve.scalar_tensor_tensor(c32[4], c32[3], float(P), io128, ALU.mult, ALU.subtract)
            dve.drain()
            tsc(c32[4], c32[4], float(NE * P - P), None, ALU.add)
            tt(RK, banks[1][:, 0:256].rearrange("p (i e) -> p i e", i=TT), b3(io128, NE), ALU.add)
            tsc(RT, banks[1][:, 0:256].rearrange("p (i e) -> p i e", i=TT), float(P), None, ALU.is_ge)
            tt(RT, RT, b3(c32[4], NE), ALU.mult)
            tt(RK, RK, RT, ALU.add)
            for a in range(2):
                tt(RT, RK, O2[a], ALU.mult)
                red(s8[9 + a], RT, ALU.add)
                dve.tensor_copy(slots_i[:, 8 * a:8 * a + 8], s8[9 + a])
            tt(cmpo, c32[2].rearrange("p (o e) -> p o e", o=1).to_broadcast((P, OVER, NE)),
               ioO.rearrange("p (b o) -> p b o", o=1).to_broadcast((P, OVER, NE)), ALU.is_le)
            red(e8[4].rearrange("p i e -> p (i e)")[:, 0:OVER], cmpo, ALU.add)
            tsc(e8[4].rearrange("p i e -> p (i e)")[:, 0:OVER], e8[4].rearrange("p i e -> p (i e)")[:, 0:OVER], float(NE - 1), None, ALU.min)
            dve.tensor_copy(eid_i, e8[4].rearrange("p i e -> p (i e)")[:, 0:OVER])
            dve.tensor_copy(nover_i, c32[2][:, NE - 1:NE])
            dve.drain()
            dve.tensor_copy(eid_i[:, 0:1], eid_i[:, 0:1]).then_inc(*reach("slots_ready"))
            dve.drain()
            dve.sem_inc(sem("xbT_ready"), 2)
            dve.sem_inc(sem("hid_ready"), 1)
            dve.sem_inc(sem("y_evac1"), 1)
            gp = gainp.rearrange("p (k o) -> p k o", o=1)

            def tokens_dve(s, n, lead):
                dve.wait_ge(sem("up_ps"), n + lead)
                for q in range(2):
                    dve.wait_ge(sem("xT_ps"), n * 2 + (4 + q + 1))
                    dve.tensor_tensor(xbT[s][:, 4 * q:4 * q + 4, :], banks[q][:, :].rearrange("p (k t) -> p k t", k=4),
                                      gp[:, 4 * q:4 * q + 4, :].to_broadcast((P, 4, P)), ALU.mult).then_inc(sem("xbT_ready"), 1)

            def hidden_dve(n):
                dve.wait_ge(sem("sg_ready"), n + 2)
                dve.wait_ge(sem("up_ps"), n + 3)
                dve.wait_ge(sem("hidT_ps"), n + 1)
                dve.tensor_tensor(hid, sg, banks[3][:, :], ALU.mult).then_inc(sem("hid_ready"), 1)

            def down_dve(s, n, ns):
                dve.wait_ge(sem("dn_ps"), n * 2 + 6)
                dve.wait_ge(sem("y_stored0") if s == 0 else sem("y_stored1"), ns * 16 + 16)
                dve.tensor_copy(ysb[s][:, 512:1024], banks[6][:, :]).then_inc(sem("y_evac1"), 1)

            def experts_dve(dve, s, n, ns, last=False):
                hidden_dve(n)
                if not last:
                    tokens_dve(1 - s, n + 1, 1)
                down_dve(s, n, ns)

            tokens_dve(0, 0, 1)
            blocks(dve, experts_dve)
            n_over = dve.value_load(nover_i[0:1, :], min_val=0, max_val=OVER)
            with dve.Fori(0, OVER) as o:
                with dve.If(o < n_over):
                    tokens_dve(0, o + NE, 2)
                    hidden_dve(o + NE)
                    down_dve(0, o + NE, o + NE // 2)
                dve.nop()
            for i in range(TT):
                dve.wait_ge(sem("yg_loaded0") if i % 2 == 0 else sem("yg_loaded1"), 32 * (i // 2 + 1))
                for a in range(2):
                    dve.scalar_tensor_tensor(Xr[:, i, :], yg[i % 2][a], gates[:, 8 * a + i:8 * a + i + 1], Xr[:, i, :], ALU.mult, ALU.add).then_inc(sem("y_added"), 1)
                    dve.drain()
            dve.wait_ge(sem("ss_ready"), 26 + TT)
            dve.tensor_scalar(rstd[:, :], ss[:, :], 1.0 / D, EPS, ALU.mult, ALU.add).then_inc(sem("ms_ready"), 1)
            dve.wait_ge(sem("rms_ready"), 5)
            dve.reciprocal(rstd[:, :], rstd[:, :])
            dve.drain()
            dve.wait_ge(sem("wfin_loaded"), 16)
            for i in range(TT):
                if i >= 2:
                    dve.wait_ge(sem("out0") if i % 2 == 0 else sem("out1"), 16 * (i // 2))
                dve.scalar_tensor_tensor(ost[i % 2], Xr[:, i, :], rstd[:, i:i + 1], wfin, ALU.mult, ALU.mult).then_inc(sem("out_ready"), 1)


def kernel(**inputs):
    import concourse.bacc as bacc
    from concourse.bass_utils import run_bass_kernel_spmd

    nc = bacc.Bacc("TRN2", target_bir_lowering=False, num_devices=1)
    arrays, views = {}, {}
    for name, value in inputs.items():
        a = np.ascontiguousarray(value)
        arrays["in_" + name] = a
        views[name] = nc.dram_tensor("in_" + name, a.shape, mybir.dt.from_np(a.dtype), kind="ExternalInput").ap()
    out = nc.dram_tensor("out_0_dram", (1, T, D), F32, kind="ExternalOutput").ap()
    program(nc, views, out)
    result = run_bass_kernel_spmd(nc, [arrays], core_ids=[0])
    return result.results[0]["out_0_dram"]
```

```python
from contextlib import ExitStack

import concourse.bass as bass
import numpy as np
from concourse import mybir

F32 = mybir.dt.float32
I32 = mybir.dt.int32
U32 = mybir.dt.uint32
ALU = mybir.AluOpType
ACT = mybir.ActivationFunctionType
AX_X = mybir.AxisListType.X
ds = bass.ds

P = 128
D = 1024
T = 1024
KT = D // P
TT = T // P
HEADS, HD = 8, 64
J = HEADS * HD // P
CH = 64
NC = T // CH
N_SHIFT = 14
GROUPS, GC, NS = 32, 16, 64
PAIRS = GROUPS // 2
TAU = P // GC
SC = T // TAU
MEM = 256
XH = 4
NE, NG, EPG = 32, 4, 8
FE = 512
OVER = 2 * T // P - 1
SLOTS = (NE + OVER) * P
EPS = 1e-6
DECAY = float(np.exp(-0.5))
TWO_PI = 2.0 * np.pi

ROWS = {}
_at = 0
for _n, _k in (("norm_mix_w", 8), ("mu_shift", 14), ("w0", 4), ("a0", 4), ("k_k", 4), ("k_a", 4), ("r_k", 4),
               ("norm_xattn_w", 8), ("norm_mem_w", 8), ("norm_moe_w", 8), ("b_glu", 4),
               ("s5_lam_re", 16), ("s5_lam_im", 16)):
    ROWS[_n] = (_at, _k)
    _at += _k
NROWS = _at


def program(nc, I, out):
    ctx = ExitStack()
    with ctx:
        def sb(name, shape, dt=F32):
            return ctx.enter_context(nc.sbuf_tensor(name, shape, dt))

        sems = {}

        def sem(name):
            if name not in sems:
                sems[name] = ctx.enter_context(nc.semaphore(name))
            return sems[name]

        ONCE = {
            "dve_marks": ["ldrow_ready", "rkc_ready", "s5_angle", "w2_ready", "v1_ready", "trig_ready", "kk_ready", "bd_zero2", "states_done",
                          "gn_centred", "gn_var", "sprev_ready", "gn_done", "l1_ready", "dv_ready", "marks_ready", "slots_a", "slots_ready"],
            "act_marks": ["pcol_ready", "s5_dt", "s5_trig", "dwda_ready", "rks_ready", "gn_sq", "gn_std", "exp_l1", "exp_dv"],
            "pe_marks": ["pcol_ps", "dt_ps", "c_ps", "rks_ps", "logits_ps", "ranks_ps"],
            "pool_marks": ["consts_a", "consts_b", "reset_a", "reset_b", "bd_zero", "toe_zero", "router_consts"],
        }

        def once(event):
            return next((name, events.index(event) + 1) for name, events in ONCE.items() if event in events)

        def reach(event):
            return sem(once(event)[0]), 1

        def reached(event):
            return sem(once(event)[0]), once(event)[1]

        arena = sb("arena", [P, 50 * 1024])

        def unit(a, n=1):
            return arena[:, a * 1024:(a + n) * 1024]

        ident = sb("ident", [P, P])
        ones = sb("ones", [P, P])
        blockones = sb("blockones", [P, P])
        pmask = sb("pmask", [P, P])
        strictU = sb("strictU", [P, P])
        lmask = sb("lmask", [P, 6, HD])
        lmask1T = sb("lmask1T", [P, HD])
        eye = sb("eye", [P, HD])
        prow = sb("prow", [P, P])
        pcol = sb("pcol", [P, NROWS])
        omka = sb("omka", [P, J])
        rkc = sb("rkc", [P, J, 2])
        small = sb("small", [P, 64])
        banks = [ctx.enter_context(nc.psum_tensor(f"bank{i}", [P, 512], F32)) for i in range(8)]

        def col(name, k=0):
            return pcol[:, ROWS[name][0] + k:ROWS[name][0] + k + 1]

        def cols(name):
            a, n = ROWS[name]
            return pcol[:, a:a + n]

        hT = unit(0, 8).rearrange("p (k t) -> p k t", k=KT)
        PT = unit(8, 14).rearrange("p (m t) -> p m t", m=N_SHIFT)
        uT = unit(22, 4).rearrange("p (j t) -> p j t", j=4)
        AR = unit(26, 8).rearrange("p (j c x) -> p j c x", j=J, c=NC)
        BK = unit(34, 8).rearrange("p (j c x) -> p j c x", j=J, c=NC)
        X = unit(8, 8).rearrange("p (i d) -> p i d", i=TT)
        wring = [unit(42 + s).rearrange("p (k m) -> p k m", k=KT) for s in range(2)]
        zbuf = [arena[:, (44 * 1024 + s * 1088):(44 * 1024 + s * 1088) + 1025] for s in range(2)]
        shift_d = unit(47)
        xs = [unit(48 + s).rearrange("p (k t) -> p k t", k=KT) for s in range(2)]
        junk = unit(16)
        zeros = unit(17)
        KINDS = (1, 0, 2)
        SHIFTED = [12, 13] + [4 * kind + j for j in range(J) for kind in KINDS]

        ss = small[:, 0:8]
        rstd = small[:, 8:16]

        d_u = nc.dram_tensor("d_u", (4 * P, TAU, SC), F32).ap()
        d_z = nc.dram_tensor("d_z", (4 * P, TAU, SC), F32).ap()

        w_in = I["w_in"][0].rearrange("(k p) n -> p k n", p=P)

        sig, csum, gexp, ginv = (unit(22 + n) for n in range(4))
        gprev, kk = unit(48), unit(49)
        avecs = [unit(32 if j < J - 1 else 12) for j in range(J)]
        tmps = [unit(33 if j < J - 1 else 13) for j in range(J)]
        gcol = sb("gcol", [P, NC, J])
        wdi = unit(46)[:, 128:640]
        wgu = unit(42)[:, 0:512]
        resets = [unit(40 if j < J - 1 else 14) for j in range(J)]
        Vt = unit(4, 4).rearrange("p (i c) -> p i c", i=TT)
        Gt = unit(0, 4).rearrange("p (i c) -> p i c", i=TT)
        rks = sb("rks", [P, TT, HEADS])
        Yt = unit(16, 4).rearrange("p (i c) -> p i c", i=TT)
        def half(u, i):
            return unit(u + i // 2)[:, 512 * (i % 2):512 * (i % 2) + 512]

        jx = lambda v: v.rearrange("p (j x) -> p j x", j=J)
        ARc = [jx(half(42, i)) for i in range(4)]
        BKz = [unit(44 + s).rearrange("p (h x) -> p h x", h=HEADS) for s in range(2)]
        BKc = [jx(half(20, i)) for i in range(2)]
        BKT = [jx(half(46, i)) for i in range(4)]
        UV = [half(48, i).rearrange("p (h v) -> p h v", h=HEADS) for i in range(2)]
        V0 = [half(49, i).rearrange("p (h v) -> p h v", h=HEADS) for i in range(2)]
        PM = [unit(8 + i).rearrange("p (h x) -> p h x", h=HEADS) for i in range(4)]
        TTbd = [jx(half(12, i)) for i in range(4)]
        LTbd = [jx(half(15, i)) for i in range(2)]
        Xbd = [jx(half(22, i)) for i in range(2)]
        TS = [half(23, i).rearrange("p (a j x) -> p a j x", a=2, j=J) for i in range(2)]
        Xst = [jx(unit(24)[:, 256 * i:256 * i + 256]) for i in range(2)]
        Qst = jx(unit(14)[:, 512:768])
        Zbd = jx(unit(14)[:, 0:512])
        Ztmp = jx(unit(14)[:, 768:1024])
        LB = [banks[2], banks[6]]
        PIECES = {(0, 1): (0, 0), (1, 0): (0, 1), (1, 1): (0, 2), (2, 0): (0, 3),
                  (2, 1): (1, 0), (3, 1): (1, 1), (4, 1): (1, 2), (5, 0): (1, 3)}

        def pairs(eng, pair):
            pair(eng, -1, 1, True, False)
            with eng.Fori(0, 3) as i:
                pair(eng, i * 2, 0, True, True)
                pair(eng, i * 2 + 1, 1, True, True)
            pair(eng, 6, 0, True, True)
            pair(eng, 7, 1, False, True)

        gtmp = unit(12, 4)
        lnwb = unit(24)
        gstat = unit(25)[:, 0:192].rearrange("p (a g) -> p a g", a=3)
        ymixT = unit(26, 8).rearrange("p (k t) -> p k t", k=KT)
        Xg = unit(35, 4).rearrange("p (g c) -> p g c", g=GROUPS)
        Toe = unit(12, 4).rearrange("p (g x) -> p g x", g=GROUPS)
        W1 = [unit(26 + 2 * a, 2).rearrange("p (q x) -> p q x", q=PAIRS) for a in range(2)]
        W2 = [arena[:, 30 * 1024 + 2304 * a:30 * 1024 + 2304 * (a + 1)].rearrange("p (q x) -> p q x", q=PAIRS) for a in range(2)]
        w2all = arena[:, 30 * 1024:30 * 1024 + 4608]
        V1 = [unit(38 + 2 * a, 2).rearrange("p (q x) -> p q x", q=PAIRS) for a in range(2)]
        trig0 = [unit(38, 2), unit(40, 2)]
        Braw = [unit(35)[:, 256 * a:256 * a + 256].rearrange("p (q i) -> p q i", q=PAIRS) for a in range(2)]
        Bbar = [unit(35)[:, 512 + 256 * a:768 + 256 * a].rearrange("p (q i) -> p q i", q=PAIRS) for a in range(2)]
        Cst = [unit(37)[:, 256 * a:256 * a + 256].rearrange("p (q o) -> p q o", q=PAIRS) for a in range(2)]
        Craw = [unit(37)[:, 512 + 256 * a:768 + 256 * a].rearrange("p (r n) -> p r n", r=4) for a in range(2)]
        KK = unit(8, 4)[0:16, :].rearrange("p (g x) -> p g x", g=GROUPS)
        s5_tmp = unit(18, 4)
        d_w1 = nc.dram_tensor("d_w1", (P, 4096), F32).ap()
        d_w2 = nc.dram_tensor("d_w2", (P, 4608), F32).ap()
        d_trig = nc.dram_tensor("d_trig", (P, 4096), F32).ap()
        d_kk = nc.dram_tensor("d_kk", (16, 4096), F32).ap()
        r8 = sb("r8", [P, PAIRS])
        E5 = [unit(46, 2), unit(48, 2)]
        trig = [unit(42, 2), unit(44, 2)]
        Rtab = unit(39, 2)
        rot = [unit(20 + 2 * a, 2) for a in range(2)]
        zst = [unit(8 + 2 * a, 2) for a in range(2)]
        Sprev = rot
        y5 = unit(46, 4)
        zT = unit(34, 4).rearrange("p (j t) -> p j t", j=4)
        wglu = unit(39, 2).rearrange("p (k m) -> p k m", k=4)
        sglu = unit(41)
        s5d = unit(36)[0:16, 992:1024]
        ldt = unit(36)[0:16, 988:990]
        ldrow = unit(36)[0:16, 856:984]
        names5 = ["dt", "are", "th", "rho", "kr", "rr", "ra", "sn", "cs", "lr", "li", "nr", "den", "cr", "ci", "t1", "t2", "t3", "t4",
                  "pr", "pi", "pr2", "pi2"]
        a5 = {n: unit(36)[:, 16 * i:16 * i + 16] for i, n in enumerate(names5)}
        a5["r8"] = r8[:, :]
        pw = [unit(36)[:, 400 + 144 * a:544 + 144 * a].rearrange("p (k q) -> p k q", k=9) for a in range(2)]
        pwr = [unit(34)[:, 512 + 128 * a:640 + 128 * a].rearrange("p (k q) -> p k q", k=8) for a in range(2)]
        Xr = unit(0, 8).rearrange("p (i d) -> p i d", i=TT)
        wmix = unit(8, 8).rearrange("p (k n) -> p k n", k=KT)
        tokring = [unit(16 + s).rearrange("p (k t) -> p k t", k=KT) for s in range(2)]

        hB = unit(18, 8).rearrange("p (k t) -> p k t", k=KT)
        wq = unit(26, 8).rearrange("p (k n) -> p k n", k=KT)
        wvo = unit(8, 8).rearrange("p (k n) -> p k n", k=KT)
        Xm = unit(34, 2).rearrange("p (i d) -> p i d", i=2)
        hM = unit(36, 2).rearrange("p (k m) -> p k m", k=KT)
        kT = unit(38, 2).rearrange("p (k m) -> p k m", k=KT)
        vM = unit(40, 2).rearrange("p (i d) -> p i d", i=2)
        wkr = [unit(42 + s).rearrange("p (k m) -> p k m", k=KT) for s in range(2)]
        qr = [unit(44 + s).rearrange("p (k t) -> p k t", k=KT) for s in range(2)]
        oR = [unit(46 + s).rearrange("p (k t) -> p k t", k=KT) for s in range(2)]
        pr_ = unit(16).rearrange("p (h m) -> p h m", h=XH)
        pT = unit(17).rearrange("p (i h t) -> p i h t", i=2, h=XH)
        junk2 = unit(47)
        smx = [small[:, 16 + 4 * s:20 + 4 * s] for s in range(2)]
        ssum = [small[:, 24 + 4 * s:28 + 4 * s] for s in range(2)]
        wrt = unit(43)[:, 0:288].rearrange("p (k e) -> p k e", k=KT)
        brt = unit(43)[:, 288:324]
        LG = unit(16)[:, 0:288].rearrange("p (i e) -> p i e", i=TT)
        l2 = unit(16)[:, 288:544].rearrange("p (i e) -> p i e", i=TT)
        io32 = unit(16)[:, 544:576]
        io4b, io8b = unit(16)[:, 576:580], unit(16)[:, 580:588]
        io128 = unit(16)[:, 588:620]
        ioM = unit(16)[:, 620:627]
        ioO = unit(16)[:, 628:643]
        e8 = [unit(16)[:, 644 + 64 * i:708 + 64 * i].rearrange("p (i e) -> p i e", i=TT) for i in range(5)]
        O2 = [unit(17)[:, 256 * a:256 * a + 256].rearrange("p (i e) -> p i e", i=TT) for a in range(2)]
        MS = unit(17)[:, 512:768].rearrange("p (i e) -> p i e", i=TT)
        MA = unit(17)[:, 768:1024].rearrange("p (i e) -> p i e", i=TT)
        RK = unit(46)[:, 0:256].rearrange("p (i e) -> p i e", i=TT)
        RT = unit(46)[:, 256:512].rearrange("p (i e) -> p i e", i=TT)
        c32 = [unit(46)[:, 512 + 32 * i:544 + 32 * i] for i in range(5)]
        cmpb = unit(46)[:, 672:672 + 224].rearrange("p (e m) -> p e m", m=7)
        cmpo = unit(45)[:, 0:480].rearrange("p (b e) -> p b e", e=NE)
        s8 = [unit(46)[:, 896 + 8 * i:904 + 8 * i] for i in range(14)]
        gates = sb("gates", [P, 16])
        ints = sb("ints", [P, 48], I32)
        slots_i = ints[:, 0:16]
        tokid = ints[:, 16:24]
        nover_i = ints[:, 24:25]
        eid_i = ints[:, 25:40]
        idx = [ints[:, 40 + s:41 + s] for s in range(2)]
        zint = unit(44)[:, 0:47].bitcast(I32)
        d_slot = nc.dram_tensor("d_slot", (SLOTS, 1), I32).ap()
        d_xn = nc.dram_tensor("d_xn", (T, D), F32).ap()
        d_y = nc.dram_tensor("d_y", (SLOTS, D), F32).ap()
        WG = [unit(a, 4).rearrange("p (k n) -> p k n", k=KT) for a in (26, 8)]
        WU = [unit(a, 4).rearrange("p (k n) -> p k n", k=KT) for a in (30, 12)]
        WD = [unit(a, 4).rearrange("p (k n) -> p k n", k=4) for a in (34, 38)]
        xb = [unit(42 + s) for s in range(2)]
        xbT = [unit(44 + s).rearrange("p (k t) -> p k t", k=KT) for s in range(2)]
        sg = unit(46)[:, 0:512]
        hid = unit(46)[:, 512:1024]
        hidT = unit(47)[:, 0:512].rearrange("p (k t) -> p k t", k=4)
        gainp = small[:, 48:56]
        ysb = [unit(48 + s) for s in range(2)]

        def blocks(eng, block_of):
            with eng.Fori(0, NE // 2 - 1) as b:
                for s in range(2):
                    block_of(eng, s, b * 2 + s, b)
            block_of(eng, 0, NE - 2, NE // 2 - 1)
            block_of(eng, 1, NE - 1, NE // 2 - 1, last=True)

        yg = [[unit(26 + 2 * s + a) for a in range(2)] for s in range(TT)]
        wfin = unit(12)
        ost = [unit(s) for s in (8, 9, 10, 11, 13, 14, 15, 18)]

        block = ctx.enter_context(nc.Block())

        @block.gpsimd
        def _(pool):
            n = [0]

            def step(ins):
                ins.then_inc(sem("pool_chain"), 1)
                n[0] += 1
                pool.wait_ge(sem("pool_chain"), n[0])

            def keep(view, op, base, pattern, cm, fill=0.0):
                step(pool.affine_select(out=view, in_=view, compare_op=op, fill=fill, base=base,
                                        pattern=pattern, channel_multiplier=cm))

            step(pool.memset(ident[:, :], 0.0))
            keep(ident[:, :], ALU.not_equal, 0, [[-1, P]], 1, 1.0)
            step(pool.memset(ones[:, :], 1.0))
            step(pool.memset(blockones[:, :], 0.0))
            step(pool.memset(blockones[0:64, 0:64], 1.0))
            step(pool.memset(blockones[64:128, 64:128], 1.0))
            step(pool.memset(prow[:, :], 0.0))
            step(pool.memset(zeros, 0.0))
            pool.nop().then_inc(*reach("consts_a"))
            step(pool.memset(pmask[:, :], 1.0))
            step(pool.memset(strictU[:, :], 1.0))
            keep(strictU[:, :], ALU.is_ge, -1, [[1, P]], -1)
            step(pool.memset(eye[:, :], 0.0))
            step(pool.memset(lmask1T[:, :], 0.0))
            step(pool.memset(lmask[:, :, :], 0.0))
            for h in (0, 64):
                keep(eye[h:h + 64, :], ALU.not_equal, 0, [[-1, 64]], 1, 1.0)
                keep(pmask[h:h + 64, 0:64], ALU.is_ge, -1, [[1, 64]], -1)
                keep(pmask[h:h + 64, 64:128], ALU.is_ge, 0, [[1, 64]], -1)
                keep(lmask1T[h:h + 64, 1:64:2], ALU.not_equal, 0, [[-2, 32]], 1, 1.0)
                for lv in range(6):
                    m = 1 << lv
                    v = lmask[h:h + 64, lv, :].rearrange("p (b x) -> p b x", x=2 * m)
                    step(pool.memset(v[:, :, 0:m], 1.0))
                    keep(v, ALU.is_ge, -m, [[-2 * m, 32 // m], [0, 2 * m]], 1)
                    keep(v, ALU.is_ge, 2 * m - 1, [[2 * m, 32 // m], [0, 2 * m]], -1)
            pool.nop().then_inc(*reach("consts_b"))
            pool.dma_start(d_y[NE * P:SLOTS, :].rearrange("(b p) d -> p b d", p=P),
                         zeros.rearrange("p (o d) -> p o d", o=1).to_broadcast((P, OVER, D))).then_inc(sem("y_zeroed"), 16)
            pool.wait_ge(sem("w1_evac"), 8)
            pool.dma_start(d_w1, unit(26, 4)).then_inc(sem("s5_stored"), 16)
            pool.wait_ge(*reached("w2_ready"))
            pool.dma_start(d_w2, w2all).then_inc(sem("s5_stored"), 16)
            pool.wait_ge(*reached("trig_ready"))
            pool.dma_start(d_trig, unit(38, 4)).then_inc(sem("s5_stored"), 16)
            pool.wait_ge(*reached("kk_ready"))
            pool.dma_start(d_kk, unit(8, 4)[0:16, :]).then_inc(sem("s5_stored"), 16)
            pool.wait_ge(sem("z_evac"), 4 + 8)
            pool.dma_start(d_u.rearrange("(j p) a c -> p j (a c)", p=P), uT).then_inc(sem("u_stored"), 16)
            for event, unit_ in (("reset_a", resets[0]), ("reset_b", resets[J - 1])):
                if event == "reset_a":
                    pool.wait_ge(sem("s5_stored"), 64)
                else:
                    pool.wait_ge(sem("elem_done"), J - 1)
                step(pool.memset(unit_, 1.0))
                step(pool.memset(unit_.rearrange("p (c x) -> p c x", x=CH)[:, :, 0:1], 0.0))
                pool.sem_inc(*reach(event))
            pool.wait_ge(sem("pt_ready"), 2 + 14)
            step(pool.memset(unit(44, 2), 0.0))
            pool.wait_ge(sem("elem_done"), J)
            for v in (unit(14)[:, 0:512], unit(49)[0:64, :]):
                step(pool.memset(v, 0.0))
            pool.sem_inc(*reach("bd_zero"))
            pool.wait_ge(sem("Y_ready"), 2 + NC)
            pool.wait_ge(*reached("states_done"))
            pool.wait_ge(*reached("gn_var"))
            step(pool.memset(Toe, 0.0))
            pool.sem_inc(*reach("toe_zero"))
            pool.wait_ge(sem("x_attn"), 4 + 2 * TT)
            for v, pat, base in ((io32, [[1, NE]], 0), (io4b, [[1, NG]], 8), (io8b, [[1, EPG]], 16), (io128, [[P, NE]], 0),
                                 (ioM, [[P, 7]], P), (ioO, [[1, OVER]], 0)):
                step(pool.iota(v, pat, base=base, channel_multiplier=0, allow_small_or_imprecise_dtypes=True))
            step(pool.iota(tokid, [[P, TT]], base=0, channel_multiplier=1))
            step(pool.memset(zint, 0))
            pool.sem_inc(*reach("router_consts"))
            pool.dma_start(d_slot.rearrange("(p b) o -> p (b o)", p=P), zint).then_inc(sem("slot_zero"), 16)
            pool.wait_ge(sem("slot_zero"), 16)
            pool.wait_ge(*reached("slots_a"))
            for k in range(2 * TT):
                if k == TT:
                    pool.wait_ge(*reached("slots_ready"))
                pool.indirect_dma_start(d_slot, bass.IndirectOffsetOnAxis(ap=slots_i[:, k:k + 1], axis=0),
                                        tokid[:, k % TT:k % TT + 1], None).then_inc(sem("slot_written"), 16)
            pool.wait_ge(sem("slot_written"), 16 * 2 * TT)
            pool.wait_ge(sem("xn_stored0"), 16 + 64)
            pool.wait_ge(sem("xn_stored1"), 16 + 64)

            def gather_block(s, n, ns, lead):
                idx_loaded, xb_loaded = (sem("idx_loaded0"), sem("xb_loaded0")) if s == 0 else (sem("idx_loaded1"), sem("xb_loaded1"))
                pool.wait_ge(sem("xT_ps"), n * 2 + 2 * lead)
                pool.dma_start(idx[s], d_slot[ds(n * P, P), :]).then_inc(idx_loaded, 16)
                pool.wait_ge(idx_loaded, ns * 16 + 16)
                pool.sem_inc(sem("pool_waits"), 1)
                pool.indirect_dma_start(xb[s], None, d_xn, bass.IndirectOffsetOnAxis(ap=idx[s], axis=0)).then_inc(xb_loaded, 16)

            with pool.Fori(0, NE // 2) as bb:
                for s in range(2):
                    gather_block(s, bb * 2 + s, bb, 1)
            n_over = pool.value_load(nover_i[0:1, :], min_val=0, max_val=OVER)
            with pool.Fori(0, OVER) as o:
                with pool.If(o < n_over):
                    gather_block(0, o + NE, o + NE // 2, 2)
                pool.nop()
            pool.wait_ge(sem("y_stored0"), n_over * 16 + (16 + 16 * (NE // 2)))
            pool.sem_inc(sem("pool_waits"), 1)
            pool.wait_ge(sem("y_stored1"), 16 + 16 * (NE // 2))
            for i in range(TT):
                for a in range(2):
                    pool.indirect_dma_start(yg[i][a], None, d_y, bass.IndirectOffsetOnAxis(ap=slots_i[:, a * TT + i:a * TT + i + 1], axis=0)
                                            ).then_inc(sem(f"yg_loaded{i}"), 16)

        @block.sync
        def _(sp):
            for q in range(2):
                sp.dma_start(X[:, 4 * q:4 * q + 4, :], I["x"][0].rearrange("(i p) d -> p i d", p=P)[:, 4 * q:4 * q + 4, :]).then_inc(sem(f"x_loaded{q}"), 16)
            sp.wait_ge(*reached("consts_a"))
            for name, (a, k) in ROWS.items():
                src = I[name][0]
                if name == "r_k":
                    src = src.rearrange("(j h) c -> j (h c)", j=J)
                elif name.startswith("s5_lam"):
                    src = src.rearrange("(q h) c -> q (h c)", q=PAIRS)
                else:
                    src = src.rearrange("(k p) -> k p", p=P)
                sp.dma_start(prow[a:a + k, :], src).then_inc(sem("params_loaded"), 16)
            sp.dma_start(ldt, I["s5_log_dt"][0].rearrange("(q h) -> q h", q=PAIRS)).then_inc(sem("s5_loaded"), 16)
            for a, n in enumerate(("re", "im")):
                sp.dma_start(Braw[a], I["s5_b_" + n][0].rearrange("(q h) n i -> (h n) q i", h=2)).then_inc(sem("s5_loaded"), 16)
                sp.dma_start(Craw[a], I["s5_c_" + n][0].rearrange("(r g) o n -> (g o) r n", r=4)).then_inc(sem("s5_loaded"), 16)
            with nc.allow_non_contiguous_dma(reason="512 skip weights, once"):
                sp.dma_start(s5d, I["s5_d"][0].rearrange("g i -> i g")).then_inc(sem("s5_loaded"), 16)
            sp.dma_start(wdi[0:64, :], I["w_decay_up"][0]).then_inc(sem("lora_loaded"), 16)
            sp.dma_start(wdi[64:128, :], I["w_iclr_up"][0]).then_inc(sem("lora_loaded"), 16)

            def load_tile(pos, s, column):
                sp.wait_ge(sem("z_done"), pos * 2 + 2)
                sp.dma_start(wring[s], w_in[:, :, ds(column, P)]).then_inc(sem("win_loaded0") if s == 0 else sem("win_loaded1"), 16)

            with sp.Fori(0, 2) as i:
                for s in range(2):
                    load_tile(i * 2 + s, s, i * 256 + (14 + s) * P)
            for s in range(2):
                load_tile(4 + s, s, (12 + s) * P)
            for pos in range(6, 18):
                load_tile(pos, pos % 2, SHIFTED[pos - 4] * P)
            sp.wait_ge(sem("z_done"), 4 + 34)
            sp.dma_start(wgu[:, :], I["w_gate_up"][0]).then_inc(sem("wgu_loaded"), 16)
            sp.wait_ge(*reached("bd_zero"))
            sp.wait_ge(sem("tokens_evac"), 2 * TT)

            def stage(p, par):
                for h in range(2):
                    c = p * 2 + h
                    loaded = sem("ops_loaded0") if h == 0 else sem("ops_loaded1")
                    sp.wait_ge(sem("bkt_ps"), c + 1)
                    sp.wait_ge(sem("Q_ps"), c + 1)
                    for q in range(2):
                        sp.dma_start(BKz[h][64 * q:64 * q + 64, q:HEADS:2, :],
                                     BK[64 * q:64 * q + 64, :, ds(c, 1), :].rearrange("p j o x -> p j (o x)")).then_inc(loaded, 16)
                    sp.dma_start(BKc[h], BK[:, :, ds(c, 1), :].rearrange("p j o x -> p j (o x)")).then_inc(loaded, 16)
                    sp.dma_start(ARc[2 * par + h], AR[:, :, ds(c, 1), :].rearrange("p j o x -> p j (o x)")).then_inc(loaded, 16)

            def stage_values(p):
                for h in range(2):
                    loaded = sem("uv_loaded0") if h == 0 else sem("uv_loaded1")
                    sp.wait_ge(sem("y_ps"), p * 2 + (h + 3))
                    for v in (UV, V0):
                        sp.dma_start(v[h][64:128, :, :], Vt[64 * h:64 * h + 64, ds(p, 1), :].rearrange("p o (h v) -> p (o h) v", h=HEADS)
                                     ).then_inc(loaded, 16)

            def reload_s5():
                sp.wait_ge(sem("ops_loaded0"), 64 * (NC // 2))
                sp.wait_ge(sem("ops_loaded1"), 64 * (NC // 2))
                sp.wait_ge(sem("s5_stored"), 64)
                sp.wait_ge(sem("u_stored"), 16)
                sp.dma_start(unit(26, 4), d_w1).then_inc(sem("w1_loaded"), 16)
                for a in range(TAU):
                    sp.dma_start(Xg[GC * a:GC * a + GC, :, :], d_u[:, a, :].rearrange("(g i) c -> i g c", i=GC)).then_inc(sem("xg_loaded"), 16)
                sp.dma_start(w2all, d_w2).then_inc(sem("w2_loaded"), 16)

            def stage_pair(sp, p, par, prep, state):
                if prep:
                    stage(p + 1, 1 - par)
                else:
                    reload_s5()
                if state:
                    stage_values(p)

            pairs(sp, stage_pair)
            sp.wait_ge(sem("TS_ready"), 6 * NC)
            sp.dma_start(lnwb[:, 0:512], I["ln_x_w"].to_broadcast((P, 512))).then_inc(sem("ln_loaded"), 16)
            sp.dma_start(lnwb[:, 512:1024], I["ln_x_b"].to_broadcast((P, 512))).then_inc(sem("ln_loaded"), 16)
            sp.wait_ge(sem("Q_ps"), 4 + NC)
            sp.dma_start(unit(42, 4), d_trig).then_inc(sem("trig_loaded"), 16)
            sp.wait_ge(*reached("toe_zero"))
            for a in range(TAU):
                sp.dma_start(Toe[GC * a:GC * a + GC, :, GC * a:P], d_kk.rearrange("p (g x) -> p g x", g=GROUPS)[:, :, 0:P - GC * a]).then_inc(sem("toe_loaded"), 16)
            sp.wait_ge(*reached("sprev_ready"))
            sp.dma_start(wglu, I["w_glu"][0].rearrange("(k p) m -> p k m", p=P)).then_inc(sem("wglu_loaded"), 16)
            wm = I["w_mix_out"][0].rearrange("(k p) n -> p k n", p=P)
            sp.dma_start(wmix[:, 0:4, :], wm[:, 0:4, :]).then_inc(sem("wmix_loaded"), 16)
            for a in range(TAU):
                if a == 0:
                    sp.wait_ge(sem("gelu_done"), 8)
                sp.dma_start(d_z[:, a, :].rearrange("(g o) c -> o g c", o=GC),
                             y5[GC * a:GC * a + GC, :].rearrange("p (g c) -> p g c", g=GROUPS)).then_inc(sem("z_stored"), 16)
            xrows = I["x"][0].rearrange("(i p) d -> p i d", p=P)
            sp.wait_ge(sem("z_stored"), 16 * TAU)
            sp.dma_start(zT, d_z.rearrange("(j p) a c -> p j (a c)", p=P)).then_inc(sem("zT_loaded"), 16)
            sp.dma_start(wmix[:, 4:8, :], wm[:, 4:8, :]).then_inc(sem("wmix_loaded"), 16)
            sp.wait_ge(*reached("gn_done"))
            sp.dma_start(Xr, xrows).then_inc(sem("xr_loaded"), 16)
            sp.wait_ge(sem("ymix_rwkv"), TT)
            sp.wait_ge(sem("ymix_s5"), 8)
            sp.wait_ge(sem("z_stored"), 16 * TAU)
            sp.dma_start(Xm, I["mem"][0].rearrange("(i p) d -> p i d", p=P)).then_inc(sem("xm_loaded"), 16)
            for s in range(2):
                sp.dma_start(tokring[s], ymixT[:, :, 256 + s * P:384 + s * P]).then_inc(sem("tok0_loaded") if s == 0 else sem("tok1_loaded"), 16)
            with sp.Fori(0, TT // 2 - 2) as ii:
                for s in range(2):
                    sp.wait_ge(sem("mix_ps"), ii * 4 + (2 * s + 10))
                    sp.dma_start(tokring[s], ymixT[:, :, ds(ii * 256 + (512 + s * 128), P)]).then_inc(sem("tok0_loaded") if s == 0 else sem("tok1_loaded"), 16)
            wk = I["w_k"][0].rearrange("(k p) n -> p k n", p=P)
            for s in range(2):
                sp.dma_start(wkr[s], wk[:, :, s * P:(s + 1) * P]).then_inc(sem("wk_loaded0") if s == 0 else sem("wk_loaded1"), 16)
            sp.wait_ge(sem("tok0_loaded"), 8 * TT - 16)
            sp.wait_ge(sem("tok1_loaded"), 8 * TT - 16)
            sp.dma_start(wq, I["w_q"][0].rearrange("(k p) n -> p k n", p=P)).then_inc(sem("wq_loaded"), 16)
            sp.wait_ge(sem("mix_ps"), 4 + 2 * TT)
            wv = I["w_v"][0].rearrange("(k p) n -> p k n", p=P)
            sp.dma_start(wvo[:, 0:4, :], wv[:, 0:4, :]).then_inc(sem("wv_loaded"), 16)
            with sp.Fori(0, KT // 2 - 1) as mm:
                for s in range(2):
                    sp.wait_ge(sem("k_ps"), mm * 2 + (s + 3))
                    sp.dma_start(wkr[s], wk[:, :, ds(mm * 256 + (2 + s) * P, P)]).then_inc(sem("wk_loaded0") if s == 0 else sem("wk_loaded1"), 16)
            sp.dma_start(wvo[:, 4:8, :], wv[:, 4:8, :]).then_inc(sem("wv_loaded"), 16)
            sp.wait_ge(sem("v_ps"), 4)
            sp.dma_start(wvo, I["w_o"][0].rearrange("(k p) n -> p k n", p=P)).then_inc(sem("wo_loaded"), 16)
            def load_expert(s, e, n, lead):
                g, u, d = (sem("wg0"), sem("wu0"), sem("wd0")) if s == 0 else (sem("wg1"), sem("wu1"), sem("wd1"))
                if lead:
                    sp.wait_ge(sem("gate_ps"), n + (lead - 2))
                sp.dma_start(WG[s], I["w_exp_gate"][0, ds(e, 1)].rearrange("o (p k) n -> p (o k) n", p=P)).then_inc(g, 16)
                if lead:
                    sp.wait_ge(sem("up_ps"), n + lead)
                sp.dma_start(WU[s], I["w_exp_up"][0, ds(e, 1)].rearrange("o (p k) n -> p (o k) n", p=P)).then_inc(u, 16)
                if lead:
                    sp.wait_ge(sem("dn_ps"), n * 2 + 2 * lead)
                sp.dma_start(WD[s], I["w_exp_down"][0, ds(e, 1)].rearrange("o (p k) n -> p (o k) n", p=P)).then_inc(d, 16)

            sp.dma_start(wrt[:, :, 0:NG], I["w_router_group"][0].rearrange("(k p) g -> p k g", p=P)).then_inc(sem("router_loaded"), 16)
            for g in range(NG):
                sp.dma_start(wrt[:, :, NG + EPG * g:NG + EPG * g + EPG], I["w_router_expert"][0, g].rearrange("(k p) e -> p k e", p=P)).then_inc(sem("router_loaded"), 16)
            sp.dma_start(brt[:, 0:NG], I["b_router_group"].to_broadcast((P, NG))).then_inc(sem("router_loaded"), 16)
            sp.dma_start(brt[:, NG:NG + NE], I["b_router_expert"].rearrange("a g e -> a (g e)").to_broadcast((P, NE))).then_inc(sem("router_loaded"), 16)
            sp.dma_start(gainp, I["norm_moe_w"][0].rearrange("(p k) -> p k", p=P)).then_inc(sem("router_loaded"), 16)

            sp.wait_ge(sem("q_ps"), 2 * TT)
            load_expert(0, 0, 0, None)
            for i in range(TT):
                sp.wait_ge(sem("xs_ready"), 18 + i + 1)
                sp.dma_start(d_xn[i * P:(i + 1) * P, :], xs[i % 2].rearrange("p k d -> p (k d)")).then_inc(sem("xn_stored0") if i % 2 == 0 else sem("xn_stored1"), 16)
            sp.wait_ge(sem("x_attn"), 4 + 2 * TT)
            load_expert(1, 1, 1, None)
            with sp.Fori(0, NE // 2 - 1) as bb:
                for s in range(2):
                    load_expert(s, bb * 2 + (2 + s), bb * 2 + (2 + s), 1)
            sp.wait_ge(*reached("slots_ready"))
            n_over = sp.value_load(nover_i[0:1, :], min_val=0, max_val=OVER)
            with sp.Fori(0, OVER) as o:
                with sp.If(o < n_over):
                    e = sp.value_load(eid_i[0:1, ds(o, 1)], min_val=0, max_val=NE - 1)
                    load_expert(0, e, o + NE, 2)
                sp.nop()
            sp.wait_ge(sem("dn_ps"), n_over * 2 + (4 + 2 * NE))
            sp.dma_start(wfin, I["norm_final_w"].rearrange("(o d) -> o d", o=1).to_broadcast((P, D))).then_inc(sem("wfin_loaded"), 16)
            for i in range(TT):
                sp.wait_ge(sem("out_ready"), i + 1)
                sp.dma_start(out[0, i * P:(i + 1) * P, :], ost[i]).then_inc(sem("out_stored"), 16)
            sp.wait_ge(sem("out_stored"), 16 * TT)
        def norm_pe(pe, base, tiles):
            with pe.Fori(0, tiles // 2) as i:
                for s in range(2):
                    norm_tile_pe(pe, base, i * 2 + s, s)

        def norm_tile_pe(pe, base, i, s):
            pe.wait_ge(sem("xs_ready"), i + (base + 1))
            for q in range(2):
                pe.wait_ge(sem("hT_ready"), i * 2 + (2 * base + q + 1))
                for k in range(4):
                    t = pe.transpose(banks[4 + 2 * s + q][:, k * P:(k + 1) * P], xs[s][:, 4 * q + k, :], ident[:, :])
                t.then_inc(sem("xsT_ps"), 1)

        @block.tensor
        def _(pe):
            pe.sem_inc(sem("z_done"), 4)
            pe.wait_ge(*reached("consts_a"))
            pe.wait_ge(sem("params_loaded"), 16 * len(ROWS))
            pe.transpose(banks[7][:, 0:NROWS], prow[0:NROWS, :], ident[0:NROWS, 0:NROWS]).then_inc(*reach("pcol_ps"))
            pe.wait_ge(*reached("ldrow_ready"))
            pe.transpose(banks[1][:, 0:16], ldrow, ident[0:16, 0:16]).then_inc(*reach("dt_ps"))
            pe.wait_ge(sem("s5_loaded"), 96)
            for a in range(2):
                for r in range(4):
                    m = pe.transpose(banks[2 + a][0:64, r * P:(r + 1) * P], Craw[a][:, r, :], ident[:, :])
            m.then_inc(*reach("c_ps"))
            norm_pe(pe, 0, TT)
            pe.wait_ge(sem("hT_ready"), 4 + 2 * TT)

            def project(pos, halves=(0, 1)):
                s = pos % 2
                pe.wait_ge(sem("win_loaded0") if s == 0 else sem("win_loaded1"), pos // 2 * 16 + 16)
                for h in halves:
                    pe.wait_ge(sem("z_evac"), pos * 2 + h + 1)
                    for k in range(KT):
                        m = pe.matmul(banks[2 * s + h][:, :], wring[s][:, k, :], hT[:, k, 512 * h:512 * h + 512],
                                      start=(k == 0), stop=(k == KT - 1))
                    m.then_inc(sem("z_done"), 1)

            pe.wait_ge(*reached("s5_dt"))
            project(0)
            pe.wait_ge(sem("c_evac"), 16)
            for pos in range(1, 4):
                project(pos)
            pe.wait_ge(*reached("v1_ready"))
            for a in range(2):
                for q4 in range(4):
                    n = 4 * a + q4
                    if n >= 2:
                        pe.wait_ge(sem("w1_evac"), n - 1)
                    for x in range(4):
                        m = pe.transpose(banks[4 + n % 2][:, x * P:(x + 1) * P], V1[a][:, 4 * q4 + x, :], ident[:, :])
                    m.then_inc(sem("w1_ps"), 1)
            project(4)
            project(5)
            pe.wait_ge(*reached("w2_ready"))
            for q4 in range(4):
                for h in range(2):
                    n = 2 * q4 + h
                    if q4 > 0:
                        pe.wait_ge(sem("kk_evac"), n - 1)
                    for x in range(4):
                        q = 4 * q4 + x
                        o = banks[6 + h][0:16, x * P:(x + 1) * P]
                        r = slice(64 * h, 64 * h + 64)
                        pe.matmul(o, Bbar[0][r, q, :], W2[0][r, q, 0:P], start=True, stop=False)
                        m = pe.matmul(o, Bbar[1][r, q, :], W2[1][r, q, 0:P], start=False, stop=True)
                    m.then_inc(sem("kk_ps"), 1)
            pe.sem_inc(sem("bkt_ps"), 2)
            pe.sem_inc(sem("y_ps"), 4)
            pe.sem_inc(sem("Q_ps"), 4)
            pe.wait_ge(sem("lora_loaded"), 32)
            pe.wait_ge(sem("w1_evac"), 8)
            pe.wait_ge(sem("kk_evac"), 8)
            def rates_pe(j):
                if j == 0:
                    pe.wait_ge(*reached("dwda_ready"))
                else:
                    pe.wait_ge(sem("kk_norm"), 2 * j)
                for h in range(2):
                    pe.matmul(banks[4 + h][:, :], wdi[0:64, j * P:(j + 1) * P], PT[0:64, 12, 512 * h:512 * h + 512],
                              start=True, stop=True)
                    m = pe.matmul(banks[6 + h][:, :], wdi[64:128, j * P:(j + 1) * P],
                                  PT[64:128, 12, 512 * h:512 * h + 512], start=True, stop=True)
                m.then_inc(sem("rates_ps"), 1)

            def norms_pe(j):
                pe.wait_ge(sem("kk_sq"), j + 1)
                pe.wait_ge(sem("rates_ready"), 4 * j + 4)
                for h in range(2):
                    m = pe.matmul(banks[4 + h][:, :], blockones[:, :], tmps[j][:, 512 * h:512 * h + 512], start=True, stop=True)
                m.then_inc(sem("kk_sum"), 1)

            for j in range(J):
                project(6 + 3 * j)
                if j > 0:
                    rates_pe(j)
                if j > 0:
                    project(7 + 3 * j, (0,))
                    norms_pe(j)
                    project(7 + 3 * j, (1,))
                else:
                    project(7)
                    rates_pe(j)
                project(8 + 3 * j)
                if j == 0:
                    norms_pe(j)
            pe.wait_ge(sem("wgu_loaded"), 16)
            pe.wait_ge(sem("z_evac"), 4 + 36)
            pe.wait_ge(sem("pt_ready"), 2 + 14)
            for i in range(TT):
                b = 2 * (i % 2)
                if i >= 2:
                    pe.wait_ge(sem("tokens_evac"), 2 * (i - 1))
                for j in range(J):
                    pe.transpose(banks[b][:, j * P:(j + 1) * P], PT[:, 8 + j, i * P:(i + 1) * P], ident[:, :])
                pe.matmul(banks[b + 1][:, :], PT[:, 13, i * P:(i + 1) * P], wgu[:, :], start=True, stop=True).then_inc(sem("tok_ps"), 1)
            pe.wait_ge(*reached("rkc_ready"))
            pe.wait_ge(sem("kk_norm"), 2 * J)
            for j in range(J):
                pe.wait_ge(sem("elem_done"), j + 1)
                for i in range(TT):
                    m = pe.matmul(banks[4][:, 8 * i + 2 * j:8 * i + 2 * j + 2], PT[:, j, i * P:(i + 1) * P], rkc[:, j, :], start=True, stop=True)
            m.then_inc(*reach("rks_ps"))
            pe.wait_ge(sem("tokens_evac"), 2 * TT)
            pe.wait_ge(*reached("rks_ready"))
            pe.wait_ge(*reached("consts_b"))
            pe.wait_ge(*reached("bd_zero"))
            pe.wait_ge(*reached("bd_zero2"))

            def state_pe(p, par, h, piece):
                c, q = p * 2 + h, 2 * par + h
                if piece == 0:
                    pe.wait_ge(sem("Z_ready"), c + 1)
                    pe.wait_ge(sem("uv_loaded0") if h == 0 else sem("uv_loaded1"), p * 32 + 32)
                    pe.wait_ge(sem("Y_ready"), c + 2)
                    for j in range(J):
                        pe.matmul(banks[7][:, j * P:(j + 1) * P], ARc[q][:, j, :], Zbd[:, j, :], start=(j == 0), stop=False, skip_group_check=True)
                    for x in range(HEADS):
                        m = pe.matmul(banks[7][0:64, x * 64:x * 64 + 64], PM[q][:, x, 0:64], V0[h][:, x, :], start=False, stop=(x == HEADS - 1),
                                      skip_group_check=True)
                    m.then_inc(sem("Q_ps"), 1)
                elif piece == 1:
                    pe.wait_ge(sem("Q_ready"), c + 1)
                    pe.wait_ge(sem("TS_ready"), p * 12 + (11 + h))
                    for j in range(J):
                        m = pe.matmul(banks[5][:, j * 64:j * 64 + 64], TTbd[q][:, j, :], Qst[:, j, :], start=True, stop=True)
                    m.then_inc(sem("U_ps"), 1)
                elif piece == 2:
                    pe.wait_ge(sem("U_ready"), c * 2 + 2)
                    for j in range(J):
                        m = pe.matmul(banks[5][:, j * P:(j + 1) * P], BKT[q][:, j, :], UV[h][:, 2 * j:2 * j + 2, :].rearrange("p h v -> p (h v)"),
                                      start=True, stop=True)
                    m.then_inc(sem("M_ps"), 1)
                else:
                    for x in range(HEADS):
                        m = pe.matmul(banks[7][64:128, x * 64:x * 64 + 64], PM[q][:, x, 64:128], UV[h][:, x, :],
                                      start=False, stop=(x == HEADS - 1), skip_group_check=True)
                    m.then_inc(sem("y_ps"), 1)

            def prepare_pe(n, par, h, first):
                c, q = n * 2 + h, 2 * par + h
                pe.wait_ge(sem("ops_loaded0") if h == 0 else sem("ops_loaded1"), n * 64 + 64)
                for x in range(HEADS):
                    if x % 4 == 0:
                        pe.wait_ge(sem("PM_ready"), c * 2 + (x // 4 + 1))
                    m = pe.matmul(banks[x // 4][:, (x % 4) * P:(x % 4 + 1) * P], BKz[h][:, x, :], ARc[q][:, x // 2, :], start=True, stop=True)
                    if x % 4 == 3:
                        m.then_inc(sem("pm_ps"), 1)
                for j in range(J):
                    m = pe.matmul(LB[h][0:64, j * P:(j + 1) * P].rearrange("p (x s) -> p x s", x=2), ARc[q][:, j, 0:64],
                                  BKz[h][:, 2 * j:2 * j + 2, 0:64], start=True, stop=True)
                m.then_inc(sem("L_ps"), 1)
                if not first:
                    pe.wait_ge(sem("TS_ready"), n * 12 + (h - 1))
                for j in range(J):
                    m = pe.transpose(banks[3 + h][:, j * P:(j + 1) * P], BKc[h][:, j, :], ident[:, :])
                m.then_inc(sem("bkt_ps"), 1)

            def pair_pe(pe, p, par, prep, state):
                n, np_ = p + 1, 1 - par
                if prep:
                    for h in range(2):
                        prepare_pe(n, np_, h, not state)
                for lv in range(6):
                    for gap in range(2):
                        for h in range(2 if prep and lv else 0):
                            if gap == 0:
                                if lv == 1:
                                    pe.wait_ge(sem("LTbd_ready"), n * 2 + (h + 1))
                                pe.wait_ge(sem("TS_new"), n * 12 + (2 * lv - 1 + h))
                                for j in range(J):
                                    m = pe.matmul(LB[h][:, j * 64:j * 64 + 64], LTbd[h][:, j, :], TS[h][:, 0, j, :], start=True, stop=True)
                                m.then_inc(sem("X_ps"), 1)
                            else:
                                pe.wait_ge(sem("Xst_ready"), n * 10 + (2 * lv - 1 + h))
                                pe.wait_ge(sem("TS_ready"), n * 12 + (2 * lv - 1 + h))
                                for j in range(J if lv < 5 else 0):
                                    pe.matmul(banks[3 + h][:, j * 64:j * 64 + 64], TTbd[2 * np_ + h][:, j, :], Xst[h][:, j, :], start=True, stop=True)
                                pe.wait_ge(sem("Xbd_ready"), n * 10 + (2 * lv - 1 + h))
                                for j in range(J):
                                    m = pe.matmul(banks[3 + h][:, 256 + j * 64:256 + j * 64 + 64], Xbd[h][:, j, :], TS[h][:, 1, j, :], start=True, stop=True)
                                m.then_inc(sem("D_ps"), 1)
                        if state and (lv, gap) in PIECES:
                            state_pe(p, par, *PIECES[lv, gap])

            pairs(pe, pair_pe)
            pe.wait_ge(sem("xg_loaded"), 16 * TAU)
            pe.wait_ge(sem("w1_loaded"), 16)
            for q4 in range(4):
                for a in range(2):
                    n = 2 * q4 + a
                    if n >= 4:
                        pe.wait_ge(sem("e_evac"), n - 3)
                    for x in range(4):
                        for h in range(2):
                            q = 4 * q4 + x
                            m = pe.matmul(banks[n % 4][64 * h:64 * h + 64, x * P:(x + 1) * P], W1[a][:, q, 64 * h:64 * h + 64],
                                          Xg[:, 2 * q + h, :], start=True, stop=True)
                    m.then_inc(sem("e_ps"), 1)
            pe.wait_ge(sem("toe_loaded"), 16 * TAU)
            pe.wait_ge(sem("e_evac"), 8)
            pe.wait_ge(sem("Y_ready"), 2 + NC)
            pe.wait_ge(*reached("states_done"))
            for n in range(8):
                for x in range(4):
                    g = 8 * (n // 2) + 2 * x + n % 2
                    pe.matmul(banks[n][:, x * P:(x + 1) * P], Toe[:, g, :], Xg[:, g, :], start=(x == 0), stop=False, skip_group_check=True)
            pe.wait_ge(sem("w2_loaded"), 16)
            pe.wait_ge(*reached("sprev_ready"))
            for n in range(8):
                r = slice(64 * (n % 2), 64 * (n % 2) + 64)
                for x in range(4):
                    q = 4 * (n // 2) + x
                    for a in range(2):
                        m = pe.matmul(banks[n][:, x * P:(x + 1) * P], W2[a][r, q, GC:GC + P],
                                      Sprev[a].rearrange("p (q c) -> p q c", q=PAIRS)[r, q, :], start=False, stop=(x == 3 and a == 1),
                                      skip_group_check=True)
                m.then_inc(sem("y5_ps"), 1)
            pe.wait_ge(sem("gelu_done"), 8)
            pe.wait_ge(*reached("gn_done"))
            for i in range(TT):
                if i >= 2:
                    pe.wait_ge(sem("ymix_rwkv"), i - 1)
                for j in range(J):
                    m = pe.transpose(banks[4 + i % 2][:, j * P:(j + 1) * P], Yt[:, i, j * P:(j + 1) * P], ident[:, :])
                m.then_inc(sem("ymixT_ps"), 1)
            pe.wait_ge(sem("wglu_loaded"), 16)
            pe.wait_ge(sem("zT_loaded"), 16)
            pe.wait_ge(sem("gelu_done"), 8)
            for m4 in range(4):
                for h in range(2):
                    n = 2 * m4 + h
                    if n >= 4:
                        pe.wait_ge(sem("glu_evac"), n - 3)
                    for k in range(4):
                        m = pe.matmul(banks[n % 4][:, :], wglu[:, k, m4 * P:(m4 + 1) * P], zT[:, k, 512 * h:512 * h + 512],
                                      start=(k == 0), stop=(k == 3))
                    m.then_inc(sem("glu_ps"), 1)
            pe.sem_inc(sem("mix_ps"), 4)
            pe.wait_ge(sem("wmix_loaded"), 32)
            pe.wait_ge(sem("glu_evac"), 8)
            pe.wait_ge(sem("ymix_rwkv"), TT)
            pe.wait_ge(sem("ymix_s5"), 8)

            def mix_pe(ii, first=False):
                for s in range(2):
                    if not first:
                        pe.wait_ge(sem("tok0_loaded") if s == 0 else sem("tok1_loaded"), ii * 16)
                    pe.wait_ge(sem("mix_added"), ii * 4 + (2 * s + 2))
                    rows = ymixT[:, :, s * P:(s + 1) * P] if first else tokring[s]
                    for h in range(2):
                        for k in range(KT):
                            m = pe.matmul(banks[2 * s + h][:, :], rows[:, k, :], wmix[:, k, 512 * h:512 * h + 512],
                                          start=(k == 0), stop=(k == KT - 1))
                        m.then_inc(sem("mix_ps"), 1)

            mix_pe(0, first=True)
            norm_pe(pe, 8, 2)
            with pe.Fori(0, TT // 2 - 1) as ii:
                mix_pe(ii + 1)
            pe.sem_inc(sem("k_ps"), 2)
            pe.wait_ge(sem("hT_ready"), 4 + 2 * 10)
            pe.wait_ge(sem("mix_added"), 4 + 2 * TT)
            with pe.Fori(0, KT // 2) as mm:
                for s in range(2):
                    pe.wait_ge(sem("wk_loaded0") if s == 0 else sem("wk_loaded1"), mm * 16 + 16)
                    pe.wait_ge(sem("kT_ready"), mm * 2 + (s + 1))
                    for k in range(KT):
                        m = pe.matmul(banks[s][:, 0:MEM], wkr[s][:, k, :], hM[:, k, :], start=(k == 0), stop=(k == KT - 1))
                    m.then_inc(sem("k_ps"), 1)
                    norm_tile_pe(pe, 10, mm * 2 + s, s)
            pe.wait_ge(sem("wv_loaded"), 32)
            pe.wait_ge(sem("kT_ready"), 2 + KT)
            for i in range(2):
                for h in range(2):
                    for k in range(KT):
                        m = pe.matmul(banks[2 * i + h][:, :], hM[:, k, i * P:(i + 1) * P], wvo[:, k, 512 * h:512 * h + 512],
                                      start=(k == 0), stop=(k == KT - 1))
                    m.then_inc(sem("v_ps"), 1)
            pe.wait_ge(sem("hT_ready"), 4 + 2 * 18)
            pe.wait_ge(sem("wq_loaded"), 16)
            pe.wait_ge(sem("kT_ready"), 2 + KT)
            pe.wait_ge(sem("vM_ready"), 4)

            def queries(t, tiles):
                for m in tiles:
                    if m % 4 == 0:
                        pe.wait_ge(sem("qr_ready"), t * 2 + (m // 4 + 1))
                    for k in range(KT):
                        mm = pe.matmul(banks[m // 4][:, (m % 4) * P:(m % 4 + 1) * P], wq[:, k, m * P:(m + 1) * P], hB[:, k, ds(t * P, P)],
                                       start=(k == 0), stop=(k == KT - 1))
                    if m % 4 == 3:
                        mm.then_inc(sem("q_ps"), 1)

            def attend(t, s, last):
                pe.wait_ge(sem("qr_ready"), t * 2 + 4)
                pe.wait_ge(sem("p_ready"), t + 1)
                for h in range(XH):
                    for kk_ in range(2):
                        m = pe.matmul(banks[2 + h // 2][:, (h % 2) * MEM:(h % 2 + 1) * MEM], qr[s][:, 2 * h + kk_, :], kT[:, 2 * h + kk_, :],
                                      start=(kk_ == 0), stop=(kk_ == 1))
                m.then_inc(sem("s_ps"), 1)
                if not last:
                    queries(t + 1, range(0, 4))
                pe.wait_ge(sem("p_ready"), t + 2)
                pe.wait_ge(sem("x_attn"), t * 2 + 4)
                for i in range(2):
                    for h in range(XH):
                        m = pe.transpose(banks[4 + i][:, h * P:(h + 1) * P], pr_[:, h, i * P:(i + 1) * P], ident[:, :])
                m.then_inc(sem("pT_ps"), 1)
                if not last:
                    queries(t + 1, range(4, 6))
                pe.wait_ge(sem("pT_ready"), t * 2 + 2)
                pe.wait_ge(sem("o_ready"), t * 2 + 2)
                for h in range(XH):
                    for dd in range(2):
                        c = 2 * h + dd
                        for i in range(2):
                            m = pe.matmul(banks[6 + c // 4][:, (c % 4) * P:(c % 4 + 1) * P], vM[:, i, c * P:(c + 1) * P], pT[:, i, h, :],
                                          start=(i == 0), stop=(i == 1))
                m.then_inc(sem("o_ps"), 1)
                if not last:
                    queries(t + 1, range(6, 8))
                pe.wait_ge(sem("o_ready"), t * 2 + 4)
                for h in range(2):
                    for k in range(KT):
                        m = pe.matmul(banks[4 + h][:, :], oR[s][:, k, :], wvo[:, k, 512 * h:512 * h + 512], start=(k == 0), stop=(k == KT - 1))
                    m.then_inc(sem("oproj_ps"), 1)

            queries(0, range(KT))
            pe.wait_ge(sem("wo_loaded"), 16)
            with pe.Fori(0, TT // 2 - 1) as ii:
                for s in range(2):
                    attend(ii * 2 + s, s, False)
            attend(TT - 2, 0, False)
            attend(TT - 1, 1, True)
            pe.wait_ge(sem("router_loaded"), 128)
            for i in range(TT + 1):
                if i < TT:
                    norm_tile_pe(pe, 18, i, i % 2)
                if i > 0:
                    pe.wait_ge(sem("hT_ready"), 4 + 2 * (18 + i))
                    for k in range(KT):
                        m = pe.matmul(banks[0][:, (i - 1) * 36:i * 36], hB[:, k, (i - 1) * P:i * P], wrt[:, k, :], start=(k == 0), stop=(k == KT - 1))
            m.then_inc(*reach("logits_ps"))
            pe.wait_ge(*reached("marks_ready"))
            pe.wait_ge(*reached("consts_b"))
            pe.matmul(banks[1][:, 0:256], strictU[:, :], MS.rearrange("p i e -> p (i e)"), start=True, stop=False)
            pe.matmul(banks[1][:, 0:256], ones[:, :], MA.rearrange("p i e -> p (i e)"), start=False, stop=True)
            pe.matmul(banks[1][:, 256:288], ones[:, :], c32[0], start=True, stop=True).then_inc(*reach("ranks_ps"))
            pe.sem_inc(sem("xT_ps"), 4)
            pe.sem_inc(sem("up_ps"), 2)
            pe.sem_inc(sem("dn_ps"), 4)
            pe.sem_inc(sem("hidT_ps"), 1)

            def tokens_pe(s, n, ns):
                pe.wait_ge(sem("xb_loaded0") if s == 0 else sem("xb_loaded1"), ns * 16 + 16)
                for q in range(2):
                    pe.wait_ge(sem("xbT_ready"), n * 2 + (q + 1))
                    for k in range(4):
                        m = pe.transpose(banks[q][:, k * P:(k + 1) * P], xb[s][:, 4 * q + k:D:KT], ident[:, :])
                    m.then_inc(sem("xT_ps"), 1)

            def gate_pe(s, n, ns):
                pe.wait_ge(sem("xbT_ready"), n * 2 + 4)
                pe.wait_ge(sem("wg0") if s == 0 else sem("wg1"), ns * 16 + 16)
                pe.wait_ge(sem("sg_ready"), n + 1)
                for k in range(KT):
                    m = pe.matmul(banks[2][:, :], xbT[s][:, k, :], WG[s][:, k, :], start=(k == 0), stop=(k == KT - 1))
                m.then_inc(sem("gate_ps"), 1)

            def up_pe(s, n, ns):
                pe.wait_ge(sem("wu0") if s == 0 else sem("wu1"), ns * 16 + 16)
                pe.wait_ge(sem("hid_ready"), n + 1)
                for k in range(KT):
                    m = pe.matmul(banks[3][:, :], xbT[s][:, k, :], WU[s][:, k, :], start=(k == 0), stop=(k == KT - 1))
                m.then_inc(sem("up_ps"), 1)

            def hidden_pe(n):
                pe.wait_ge(sem("hid_ready"), n + 2)
                pe.wait_ge(sem("hidT_ready"), n + 1)
                for k in range(4):
                    m = pe.transpose(banks[4][:, k * P:(k + 1) * P], hid[:, k:FE:4], ident[:, :])
                m.then_inc(sem("hidT_ps"), 1)

            def down_pe(s, n, ns):
                pe.wait_ge(sem("hidT_ready"), n + 2)
                pe.wait_ge(sem("wd0") if s == 0 else sem("wd1"), ns * 16 + 16)
                for h in range(2):
                    pe.wait_ge(sem("y_evac0") if h == 0 else sem("y_evac1"), n + 1)
                    for k in range(4):
                        m = pe.matmul(banks[5 + h][:, :], hidT[:, k, :], WD[s][:, k, 512 * h:512 * h + 512], start=(k == 0), stop=(k == 3))
                    m.then_inc(sem("dn_ps"), 1)

            def experts_pe(pe, s, n, ns, last=False):
                up_pe(s, n, ns)
                if not last:
                    tokens_pe(1 - s, n + 1, ns + s)
                hidden_pe(n)
                if not last:
                    gate_pe(1 - s, n + 1, ns + s)
                down_pe(s, n, ns)

            tokens_pe(0, 0, 0)
            gate_pe(0, 0, 0)
            blocks(pe, experts_pe)
            pe.wait_ge(*reached("slots_ready"))
            n_over = pe.value_load(nover_i[0:1, :], min_val=0, max_val=OVER)
            with pe.Fori(0, OVER) as o:
                with pe.If(o < n_over):
                    n, ns = o + NE, o + NE // 2
                    tokens_pe(0, n, ns)
                    gate_pe(0, n, ns)
                    up_pe(0, n, ns)
                    hidden_pe(n)
                    down_pe(0, n, ns)
                pe.nop()

        def norm_act(act, src, junk, base, tiles, use, stored=False, halves=None, loads=None, with_tile=None):
            parts = 2 if loads is not None else 1
            for part in range(parts):
                if loads is not None:
                    act.wait_ge(loads[part], 16)
                with act.Fori(part * tiles // parts, (part + 1) * tiles // parts) as i:
                    if halves is not None:
                        act.wait_ge(halves, i * 2 + 6)
                    act.activation(junk, src[:, ds(i, 1), :].rearrange("p o d -> p (o d)"), ACT.Square, accum_out=ss[:, ds(i, 1)]).then_inc(sem("ss_ready"), 1)
                    act.drain()
            act.wait_ge(sem("ms_ready"), use)
            act.activation(rstd[:, 0:tiles], rstd[:, 0:tiles], ACT.Sqrt).then_inc(sem("rms_ready"), 1)
            act.wait_ge(sem("rstd_ready"), use)
            with act.Fori(0, tiles // 2) as i:
                for s in range(2):
                    if stored:
                        act.wait_ge(sem("xn_stored0") if s == 0 else sem("xn_stored1"), i * 16 + 16)
                    scale_act(act, src, base, i * 2 + s, s)
                    if with_tile is not None:
                        with_tile(i * 2 + s, s)

        def scale_act(act, src, base, i, s):
            act.wait_ge(sem("xs_free"), i + (base + 1))
            act.activation(xs[s], src[:, ds(i, 1), :].rearrange("p o (k d) -> p (o k) d", k=KT),
                           ACT.Copy, scale=rstd[:, ds(i, 1)]).then_inc(sem("xs_ready"), 1)

        @block.scalar
        def _(act):
            act.wait_ge(*reached("pcol_ps"))
            act.activation(pcol[:, :], banks[7][:, 0:NROWS], ACT.Copy).then_inc(*reach("pcol_ready"))
            norm_act(act, X, junk, 0, TT, 1, loads=[sem("x_loaded0"), sem("x_loaded1")])
            act.wait_ge(*reached("dt_ps"))
            act.activation(a5["dt"], banks[1][:, 0:16], ACT.Exp).then_inc(*reach("s5_dt"))
            act.wait_ge(*reached("c_ps"))
            act.wait_ge(sem("s5_loaded"), 96)
            for a in range(2):
                for h in range(2):
                    for r in range(4):
                        act.activation(Cst[a][64 * h:64 * h + 64, 4 * r:4 * r + 4, :],
                                       banks[2 + a][0:64, r * P:(r + 1) * P].rearrange("n (q h o) -> n h q o", h=2, o=GC)[:, h, :, :],
                                       ACT.Copy).then_inc(sem("c_evac"), 1)
            act.wait_ge(*reached("s5_angle"))
            act.activation(a5["rho"], a5["are"], ACT.Exp)
            act.activation(a5["r8"], a5["are"], ACT.Exp, scale=float(TAU))
            act.activation(a5["sn"], a5["rr"], ACT.Sin)
            act.activation(a5["cs"], a5["ra"], ACT.Sin).then_inc(*reach("s5_trig"))
            act.sem_inc(sem("z_evac"), 4)

            def u_act(j):
                for h in range(2):
                    act.wait_ge(sem("z_done"), 4 + 2 * j + h + 1)
                    act.activation(uT[:, j, :].rearrange("p (a c) -> p a c", a=TAU)[:, :, 64 * h:64 * h + 64],
                                   banks[2 * (j % 2) + h][:, :].rearrange("p (c a) -> p a c", a=TAU), ACT.Copy).then_inc(sem("z_evac"), 1)

            def tile_act(pos):
                s = pos % 2
                act.wait_ge(sem("pt_ready"), pos - 4 + 1)
                for h in range(2):
                    act.wait_ge(sem("z_done"), 4 + 2 * pos + h + 1)
                    act.activation(zbuf[s][:, 1 + 512 * h:513 + 512 * h], banks[2 * s + h][:, :], ACT.Copy).then_inc(sem("z_evac"), 1)

            for j in range(4):
                u_act(j)
            for n in range(8):
                act.wait_ge(sem("w1_ps"), n + 1)
                act.activation(W1[n // 4][:, 4 * (n % 4):4 * (n % 4) + 4, :].rearrange("p q x -> p (q x)"), banks[4 + n % 2][:, :], ACT.Copy).then_inc(sem("w1_evac"), 1)
            tile_act(4)
            tile_act(5)
            for n in range(8):
                act.wait_ge(sem("kk_ps"), n + 1)
                q4, h = n // 2, n % 2
                act.activation(KK[:, 8 * q4 + h:8 * q4 + 8:2, :], banks[6 + h][0:16, :].rearrange("p (q x) -> p q x", q=4), ACT.Copy).then_inc(sem("kk_evac"), 1)
            tile_act(6)
            act.wait_ge(sem("pt_ready"), 2 + 2)
            act.activation(PT[0:64, 12, :], PT[0:64, 12, :], ACT.Tanh)
            act.activation(PT[:, 13, :], PT[:, 13, :], ACT.Sigmoid)
            act.drain()
            act.activation(small[:, 63:64], small[:, 8:9], ACT.Copy).then_inc(*reach("dwda_ready"))
            for j in range(J):
                avec, tmp = avecs[j], tmps[j]
                if j > 0:
                    tile_act(6 + 3 * j)
                else:
                    tile_act(7)
                act.wait_ge(sem("rates_ps"), j + 1)
                if j > 0:
                    act.wait_ge(sem("elem_done"), j)
                else:
                    act.wait_ge(sem("u_stored"), 16)
                    act.wait_ge(sem("s5_stored"), 64)
                for h in range(2):
                    act.activation(sig[:, 512 * h:512 * h + 512], banks[4 + h][:, :], ACT.Sigmoid, bias=col("w0", j)).then_inc(sem("rates_ready"), 1)
                    act.activation(avec[:, 512 * h:512 * h + 512], banks[6 + h][:, :], ACT.Sigmoid, bias=col("a0", j)).then_inc(sem("rates_ready"), 1)
                act.wait_ge(sem("kk0_ready"), j + 1)
                act.activation(tmp, kk, ACT.Square).then_inc(sem("kk_sq"), 1)
                act.wait_ge(sem("csum_ready"), j + 1)
                act.activation(gexp, csum, ACT.Exp, scale=-DECAY).then_inc(sem("gexp_ready"), 1)
                act.activation(ginv, csum, ACT.Exp, scale=DECAY).then_inc(sem("gexp_ready"), 1)
                act.wait_ge(sem("cprev_ready"), j + 1)
                act.activation(gprev, gprev, ACT.Exp, scale=-DECAY).then_inc(sem("gexp_ready"), 1)
                if j == 0:
                    tile_act(8)
                act.wait_ge(sem("kk_sum"), j + 1)
                act.wait_ge(sem("kk_sq"), j + 1)
                for h in range(2):
                    act.activation(tmp[:, 512 * h:512 * h + 512], banks[4 + h][:, :], ACT.Sqrt).then_inc(sem("kk_norm"), 1)
                if j > 0:
                    tile_act(7 + 3 * j)
                    tile_act(8 + 3 * j)
            for i in range(TT):
                b = 2 * (i % 2)
                act.wait_ge(sem("tok_ps"), i + 1)
                act.activation(Vt[:, i, :], banks[b][:, :], ACT.Copy).then_inc(sem("tokens_evac"), 1)
                act.activation(Gt[:, i, :], banks[b + 1][:, :], ACT.Copy).then_inc(sem("tokens_evac"), 1)
            act.wait_ge(*reached("rks_ps"))
            act.activation(rks.rearrange("p i h -> p (i h)"), banks[4][:, 0:64], ACT.Copy).then_inc(*reach("rks_ready"))
            act.sem_inc(sem("Y_ready"), 2)
            act.wait_ge(*reached("bd_zero"))
            act.wait_ge(*reached("bd_zero2"))

            def diag(dst, src, event=None):
                for q in range(2):
                    a = act.activation(dst[64 * q:64 * q + 64, :, 64 * q:64 * q + 64], src(q), ACT.Copy)
                a.then_inc(event, 1)

            def pair_act(act, p, par, prep, state):
                n, np_ = p + 1, 1 - par
                for h in range(2 if prep else 0):
                    q, c = 2 * np_ + h, n * 2 + h
                    act.wait_ge(sem("PM_ready"), c * 2 + 4)
                    diag(LTbd[h], lambda a: PM[q][0:64, a:HEADS:2, 0:64], sem("LTbd_ready"))
                    act.wait_ge(sem("bkt_ps"), c + 3)
                    act.activation(BKT[q].rearrange("p j x -> p (j x)"), banks[3 + h][:, :], ACT.Copy)
                    act.wait_ge(sem("TS_new"), n * 12 + (h + 1))
                    diag(TTbd[q], lambda a: TS[h][64 * a:64 * a + 64, 1, :, :], sem("TS_ready"))
                for lv in range(6):
                    for gap in range(2):
                        for h in range(2 if prep and lv else 0):
                            if gap == 0:
                                act.wait_ge(sem("Xst_ready"), n * 10 + (2 * lv - 1 + h))
                                diag(Xbd[h], lambda a: Xst[h][64 * a:64 * a + 64, :, :], sem("Xbd_ready"))
                            else:
                                act.wait_ge(sem("TS_new"), n * 12 + (2 * lv + 1 + h))
                                diag(TTbd[2 * np_ + h], lambda a: TS[h][64 * a:64 * a + 64, 1, :, :], sem("TS_ready"))
                        if state and (lv, gap) in PIECES:
                            h, piece = PIECES[lv, gap]
                            c = p * 2 + h
                            if piece == 1:
                                act.wait_ge(sem("U_ps"), c + 1)
                                for q in range(2):
                                    act.activation(UV[h][0:64, q:HEADS:2, :], jx(banks[5][64 * q:64 * q + 64, 0:256]), ACT.Copy).then_inc(sem("U_ready"), 1)
                            elif piece == 3:
                                act.wait_ge(sem("y_ps"), c + 5)
                                act.activation(Yt[64 * h:64 * h + 64, ds(p, 1), :].rearrange("p o c -> p (o c)"),
                                               banks[7][64:128, :], ACT.Copy).then_inc(sem("Y_ready"), 1)

            pairs(act, pair_act)
            for n in range(8):
                act.wait_ge(sem("e_ps"), n + 1)
                act.activation(E5[n % 2][:, 512 * (n // 2):512 * (n // 2) + 512], banks[n % 4][:, :], ACT.Copy).then_inc(sem("e_evac"), 1)
            act.wait_ge(*reached("gn_centred"))
            act.activation(gtmp, unit(16, 4), ACT.Square).then_inc(*reach("gn_sq"))
            act.wait_ge(*reached("gn_var"))
            act.activation(gstat[:, 1, :], gstat[:, 1, :], ACT.Sqrt).then_inc(*reach("gn_std"))
            for n in range(8):
                act.wait_ge(sem("y5_ps"), n + 1)
                q4, h = n // 2, n % 2
                act.activation(y5.rearrange("p (g c) -> p g c", g=GROUPS)[:, 8 * q4 + h:8 * q4 + 8:2, :],
                               banks[n][:, :].rearrange("p (q c) -> p q c", q=4), ACT.Gelu_apprx_tanh).then_inc(sem("gelu_done"), 1)
            for i in range(TT):
                act.wait_ge(sem("ymixT_ps"), i + 1)
                act.activation(ymixT[:, 0:4, i * P:(i + 1) * P], banks[4 + i % 2][:, :].rearrange("p (k t) -> p k t", k=4), ACT.Copy).then_inc(sem("ymix_rwkv"), 1)
            for n in range(8):
                act.wait_ge(sem("glu_ps"), n + 1)
                if n >= 2:
                    act.wait_ge(sem("ymix_s5"), n - 1)
                act.activation(sglu[:, 512 * (n % 2):512 * (n % 2) + 512], banks[n % 4][:, :], ACT.Sigmoid, bias=col("b_glu", n // 2)).then_inc(sem("glu_evac"), 1)
            act.sem_inc(sem("kT_ready"), 2)
            act.sem_inc(sem("qr_ready"), 2)
            act.wait_ge(sem("xm_loaded"), 16)
            norm_act(act, Xm, junk2, 8, 2, 2)

            def keys_act(i, s):
                act.wait_ge(sem("k_ps"), i + 3)
                act.activation(kT[:, ds(i, 1), :].rearrange("p o m -> p (o m)"), banks[s][:, 0:MEM], ACT.Copy).then_inc(sem("kT_ready"), 1)

            norm_act(act, Xr, junk2, 10, TT, 3, halves=sem("mix_added"), with_tile=keys_act)

            def queries_act(t, s, halves=(0, 1)):
                for h in halves:
                    act.wait_ge(sem("q_ps"), t * 2 + (h + 1))
                    act.activation(qr[s][:, 4 * h:4 * h + 4, :].rearrange("p k t -> p (k t)"), banks[h][:, :], ACT.Copy).then_inc(sem("qr_ready"), 1)

            def attend_act(t, s, last):
                act.wait_ge(sem("smx_ready"), t + 1)
                for h in range(XH):
                    act.activation(pr_[:, h, :], banks[2 + h // 2][:, (h % 2) * MEM:(h % 2 + 1) * MEM], ACT.Exp, bias=smx[s][:, h:h + 1],
                                   scale=1.0 / 16.0, accum_out=ssum[s][:, h:h + 1]).then_inc(sem("exp_done"), 1)
                if not last:
                    queries_act(t + 1, 1 - s, (0,))
                act.wait_ge(sem("pT_ps"), t + 1)
                for i in range(2):
                    act.activation(pT[:, i, :, :].rearrange("p h t -> p (h t)"), banks[4 + i][:, :], ACT.Copy).then_inc(sem("pT_ready"), 1)
                act.wait_ge(sem("o_ps"), t + 1)
                for h in range(2):
                    act.activation(oR[s][:, 4 * h:4 * h + 4, :].rearrange("p k t -> p (k t)"), banks[6 + h][:, :], ACT.Copy).then_inc(sem("o_ready"), 1)
                if not last:
                    queries_act(t + 1, 1 - s, (1,))

            act.sem_inc(sem("o_ready"), 2)
            queries_act(0, 0)
            with act.Fori(0, TT // 2 - 1) as ii:
                for s in range(2):
                    attend_act(ii * 2 + s, s, False)
            attend_act(TT - 2, 0, False)
            attend_act(TT - 1, 1, True)
            norm_act(act, Xr, unit(17), 18, TT, 4, stored=True, halves=sem("x_attn"))
            act.wait_ge(*reached("l1_ready"))
            act.activation(e8[0][:, :, 0:NG], e8[0][:, :, 0:NG], ACT.Exp).then_inc(*reach("exp_l1"))
            act.wait_ge(*reached("dv_ready"))
            act.activation(s8[6], s8[6], ACT.Exp).then_inc(*reach("exp_dv"))
            act.wait_ge(*reached("slots_ready"))
            act.sem_inc(sem("sg_ready"), 1)
            act.sem_inc(sem("hidT_ready"), 1)
            act.sem_inc(sem("y_evac0"), 1)
            act.sem_inc(sem("y_stored0"), 16)
            act.sem_inc(sem("y_stored1"), 16)

            def gate_act(n):
                act.wait_ge(sem("gate_ps"), n + 1)
                act.wait_ge(sem("hid_ready"), n + 1)
                act.activation(sg, banks[2][:, :], ACT.Silu).then_inc(sem("sg_ready"), 1)

            def hidden_act(n):
                act.wait_ge(sem("hidT_ps"), n + 2)
                act.wait_ge(sem("dn_ps"), n * 2 + 4)
                act.activation(hidT.rearrange("p k t -> p (k t)"), banks[4][:, :], ACT.Copy).then_inc(sem("hidT_ready"), 1)

            def down_act(s, n, ns):
                stored = sem("y_stored0") if s == 0 else sem("y_stored1")
                act.wait_ge(sem("dn_ps"), n * 2 + 5)
                act.wait_ge(stored, ns * 16 + 16)
                act.activation(ysb[s][:, 0:512], banks[5][:, :], ACT.Copy).then_inc(sem("y_evac0"), 1)
                act.wait_ge(sem("y_evac0"), n + 2)
                act.wait_ge(sem("y_evac1"), n + 2)
                act.dma_start(d_y[ds(n * P, P), :], ysb[s]).then_inc(stored, 16)

            def experts_act(act, s, n, ns, last=False):
                hidden_act(n)
                if not last:
                    gate_act(n + 1)
                down_act(s, n, ns)

            gate_act(0)
            blocks(act, experts_act)
            n_over = act.value_load(nover_i[0:1, :], min_val=0, max_val=OVER)
            with act.Fori(0, OVER) as o:
                with act.If(o < n_over):
                    gate_act(o + NE)
                    hidden_act(o + NE)
                    down_act(0, o + NE, o + NE // 2)
                act.nop()
            for half in range(2):
                with act.Fori(4 * half, 4 * half + 4) as i:
                    act.wait_ge(sem("y_added"), i * 2 + 2)
                    act.activation(unit(16), Xr[:, ds(i, 1), :].rearrange("p o d -> p (o d)"), ACT.Square, accum_out=ss[:, ds(i, 1)]).then_inc(sem("ss_ready"), 1)
                    act.drain()
                act.wait_ge(sem("ms_ready"), 5 + half)
                act.activation(rstd[:, 4 * half:4 * half + 4], rstd[:, 4 * half:4 * half + 4], ACT.Sqrt).then_inc(sem("rms_ready"), 1)

        def norm_dve(dve, wname, dst, base, tiles, use):
            dve.wait_ge(sem("ss_ready"), base + tiles)
            dve.tensor_scalar(rstd[:, 0:tiles], ss[:, 0:tiles], 1.0 / D, EPS, ALU.mult, ALU.add).then_inc(sem("ms_ready"), 1)
            dve.wait_ge(sem("rms_ready"), use)
            dve.reciprocal(rstd[:, 0:tiles], rstd[:, 0:tiles]).then_inc(sem("rstd_ready"), 1)
            gain = cols(wname).rearrange("p (k o) -> p k o", o=1)
            with dve.Fori(0, tiles // 2) as i:
                for s in range(2):
                    for q in range(2):
                        dve.wait_ge(sem("xsT_ps"), i * 4 + (2 * base + 2 * s + q + 1))
                        if q == 1:
                            dve.sem_inc(sem("xs_free"), 1)
                        dve.tensor_tensor(dst[:, 4 * q:4 * q + 4, ds(i * 256 + s * 128, P)],
                                          banks[4 + 2 * s + q][:, :].rearrange("p (k t) -> p k t", k=4),
                                          gain[:, 4 * q:4 * q + 4, :].to_broadcast((P, 4, P)), ALU.mult).then_inc(sem("hT_ready"), 1)

        @block.vector
        def _(dve):
            dve.sem_inc(sem("hT_ready"), 4)
            dve.sem_inc(sem("xs_free"), 2)
            dve.sem_inc(sem("pt_ready"), 2)
            for z in zbuf:
                dve.memset(z[:, 0:1], 0.0)
            dve.wait_ge(*reached("pcol_ready"))

            def tt(o, a, b, op):
                dve.tensor_tensor(o, a, b, op)
                dve.drain()

            def tsc(o, a, s1, s2, o1, o2=None):
                if o2 is None:
                    dve.tensor_scalar(o, a, s1, None, o1)
                else:
                    dve.tensor_scalar(o, a, s1, s2, o1, o2)
                dve.drain()

            dve.wait_ge(sem("s5_loaded"), 96)
            dve.tensor_copy(ldrow.rearrange("p (h n) -> p h n", h=2), ldt.rearrange("p (h o) -> p h o", o=1).to_broadcast((16, 2, NS))).then_inc(*reach("ldrow_ready"))
            norm_dve(dve, "norm_mix_w", hT, 0, TT, 1)
            dve.tensor_scalar(omka[:, :], cols("k_a"), -1.0, 1.0, ALU.mult, ALU.add)
            dve.memset(rkc[:, :, :], 0.0)
            dve.drain()
            for p in range(2):
                m = dve.tensor_copy(rkc[64 * p:64 * p + 64, :, p:p + 1],
                                cols("r_k")[64 * p:64 * p + 64, :].rearrange("p (j o) -> p j o", o=1))
            m.then_inc(*reach("rkc_ready"))
            lre, lim = cols("s5_lam_re"), cols("s5_lam_im")
            A = a5
            dve.wait_ge(*reached("s5_dt"))
            tt(A["are"], lre, A["dt"], ALU.mult)
            tt(A["th"], lim, A["dt"], ALU.mult)
            tsc(A["kr"], A["th"], 1.0 / TWO_PI, None, ALU.mult)
            tsc(A["kr"], A["kr"], 12582912.0, None, ALU.add)
            tsc(A["kr"], A["kr"], -12582912.0, None, ALU.add)
            c1 = 6.28125
            c2 = float(np.float32(np.round((TWO_PI - c1) * 2 ** 20) / 2 ** 20))
            c3 = float(np.float32(TWO_PI - c1 - c2))
            dve.scalar_tensor_tensor(A["rr"], A["kr"], -c1, A["th"], ALU.mult, ALU.add)
            dve.drain()
            for c in (c2, c3):
                dve.scalar_tensor_tensor(A["rr"], A["kr"], -c, A["rr"], ALU.mult, ALU.add)
                dve.drain()
            tsc(A["rr"], A["rr"], 3.1415925, -3.1415925, ALU.min, ALU.max)
            dve.scalar_tensor_tensor(A["ra"], A["rr"], -1.0, A["rr"], ALU.mult, ALU.min)
            dve.drain()
            dve.tensor_scalar(A["ra"], A["ra"], float(np.pi / 2), None, ALU.add).then_inc(*reach("s5_angle"))
            dve.wait_ge(*reached("s5_trig"))
            tt(A["lr"], A["rho"], A["cs"], ALU.mult)
            tt(A["li"], A["rho"], A["sn"], ALU.mult)

            def cmul(o, a, b, t, conj=False):
                dve.tensor_tensor(t[0], a[0], b[0], ALU.mult)
                dve.tensor_tensor(t[1], a[1], b[1], ALU.mult)
                dve.tensor_tensor(t[2], a[0], b[1], ALU.mult)
                dve.tensor_tensor(t[3], a[1], b[0], ALU.mult)
                dve.drain()
                dve.tensor_tensor(o[0], t[0], t[1], ALU.add if conj else ALU.subtract)
                dve.tensor_tensor(o[1], t[2], t[3], ALU.subtract if conj else ALU.add)
                dve.drain()

            T4 = [A["t1"], A["t2"], A["t3"], A["t4"]]
            tsc(A["nr"], A["lr"], -1.0, None, ALU.add)
            tt(A["t1"], lre, lre, ALU.mult)
            tt(A["t2"], lim, lim, ALU.mult)
            tt(A["den"], A["t1"], A["t2"], ALU.add)
            dve.reciprocal(A["den"], A["den"])
            dve.drain()
            cmul((A["cr"], A["ci"]), (lre, lim), (A["nr"], A["li"]), T4, conj=True)
            tt(A["cr"], A["cr"], A["den"], ALU.mult)
            tt(A["ci"], A["ci"], A["den"], ALU.mult)
            q_ = lambda v, n: v.rearrange("p (q o) -> p q o", o=1).to_broadcast((P, PAIRS, n))
            tmp4 = [s5_tmp[:, 256 * i:256 * i + 256].rearrange("p (q i) -> p q i", q=PAIRS) for i in range(4)]
            cmul(Bbar, (q_(A["cr"], GC), q_(A["ci"], GC)), Braw, tmp4)
            dve.memset(pw[0][:, 0, :], 1.0)
            dve.memset(pw[1][:, 0, :], 0.0)
            dve.tensor_copy(pw[0][:, 1, :], A["lr"])
            dve.tensor_copy(pw[1][:, 1, :], A["li"])
            dve.drain()
            for n in range(2, TAU + 1):
                cmul((pw[0][:, n, :], pw[1][:, n, :]), (pw[0][:, n - 1, :], pw[1][:, n - 1, :]), (A["lr"], A["li"]), T4)
            dve.wait_ge(sem("c_evac"), 16)
            def kq(v, k0, n, rev=False):
                return v[:, k0:k0 + n, :].rearrange("p k (q o) -> p q k o", o=1).to_broadcast((P, PAIRS, n, GC))
            def qx(v, n):
                return v.rearrange("p q (o x) -> p q o x", o=1).to_broadcast((P, PAIRS, n, GC))
            w4 = lambda v: v.rearrange("p q (k x) -> p q k x", x=GC)
            sc = s5_tmp[:, 0:2304].rearrange("p (q k x) -> p q k x", q=PAIRS, k=9)
            for a in range(2):
                dve.tensor_tensor(w4(W2[a]), kq(pw[0], 0, 9), qx(Cst[a], 9), ALU.mult)
                dve.tensor_tensor(sc, kq(pw[1], 0, 9), qx(Cst[1 - a], 9), ALU.mult)
                dve.drain()
                if a == 0:
                    tt(w4(W2[0]), w4(W2[0]), sc, ALU.subtract)
                else:
                    dve.scalar_tensor_tensor(W2[1].rearrange("p q x -> p (q x)"), W2[1].rearrange("p q x -> p (q x)"), -1.0,
                                             sc.rearrange("p q k x -> p (q k x)"), ALU.mult, ALU.subtract).then_inc(*reach("w2_ready"))
                    dve.drain()
            for a in range(2):
                for k in range(TAU):
                    dve.tensor_copy(pwr[a][:, k, :], pw[a][:, TAU - 1 - k, :])
            dve.drain()
            sv = s5_tmp[:, 0:2048].rearrange("p (q k x) -> p q k x", q=PAIRS, k=TAU)
            for a in range(2):
                dve.tensor_tensor(w4(V1[a]), kq(pwr[0], 0, 8), qx(Bbar[a], 8), ALU.mult)
                dve.tensor_tensor(sv, kq(pwr[1], 0, 8), qx(Bbar[1 - a], 8), ALU.mult)
                dve.drain()
                m = dve.tensor_tensor(w4(V1[a]), w4(V1[a]), sv, ALU.subtract if a == 0 else ALU.add)
                dve.drain()
            m.then_inc(*reach("v1_ready"))
            p1, p2 = ("pr", "pi"), ("pr2", "pi2")
            cmul((A["pr"], A["pi"]), (A["cs"], A["sn"]), (A["cs"], A["sn"]), T4)
            cmul((A["pr2"], A["pi2"]), (A["pr"], A["pi"]), (A["pr"], A["pi"]), T4)
            cmul((A["pr"], A["pi"]), (A["pr2"], A["pi2"]), (A["pr2"], A["pi2"]), T4)
            dve.wait_ge(sem("w1_evac"), 8)
            tg = [v.rearrange("p (q c) -> p q c", q=PAIRS) for v in trig0]
            dve.memset(tg[0][:, :, 0:1], 1.0)
            dve.memset(tg[1][:, :, 0:1], 0.0)
            dve.drain()
            n = 1
            while n < SC:
                b = [v.rearrange("p (q o) -> p q o", o=1).to_broadcast((P, PAIRS, n)) for v in (A[p1[0]], A[p1[1]])]
                t = [s5_tmp[:, 1024 * i:1024 * i + 16 * n].rearrange("p (q c) -> p q c", q=PAIRS) for i in range(4)]
                cmul([v[:, :, n:2 * n] for v in tg], [v[:, :, 0:n] for v in tg], b, t)
                cmul([A[x] for x in p2], [A[x] for x in p1], [A[x] for x in p1], T4)
                p1, p2 = p2, p1
                n *= 2
            dve.sem_inc(*reach("trig_ready"))
            dve.wait_ge(sem("kk_evac"), 8)
            d3 = s5_tmp[0:16, 0:512].rearrange("p (g x) -> p g x", g=GROUPS)
            tt(d3, ident[0:16, 0:16].rearrange("p (o x) -> p o x", o=1).to_broadcast((16, GROUPS, GC)),
               s5d.rearrange("p (g o) -> p g o", o=1).to_broadcast((16, GROUPS, GC)), ALU.mult)
            dve.tensor_tensor(KK[:, :, 0:GC], KK[:, :, 0:GC], d3, ALU.add).then_inc(*reach("kk_ready"))
            dve.drain()

            def shift_tile(pos):
                s, m = pos % 2, SHIFTED[pos - 4]
                dve.wait_ge(sem("z_evac"), 4 + 2 * pos + 2)
                dve.tensor_tensor(shift_d, zbuf[s][:, 0:1024], zbuf[s][:, 1:1025], ALU.subtract)
                dve.drain()
                dve.scalar_tensor_tensor(PT[:, m, :], shift_d, col("mu_shift", m), zbuf[s][:, 1:1025], ALU.mult, ALU.add).then_inc(sem("pt_ready"), 1)
                dve.drain()

            dve.wait_ge(*reached("consts_b"))
            shift_tile(4)
            shift_tile(5)
            dve.wait_ge(sem("y_zeroed"), 16)
            dve.wait_ge(sem("s5_stored"), 64)
            dve.wait_ge(sem("u_stored"), 16)
            for j in range(J):
                avec, tmp = avecs[j], tmps[j]
                shift_tile(6 + 3 * j)
                if j == 0:
                    shift_tile(7)
                ch = lambda v: v.rearrange("p (c x) -> p c x", x=CH)
                r, k = PT[:, j, :], PT[:, 4 + j, :]
                dve.tensor_scalar(kk, k, col("k_k", j), None, ALU.mult).then_inc(sem("kk0_ready"), 1)
                dve.wait_ge(sem("rates_ready"), 4 * j + 4)
                dve.wait_ge(*reached("reset_a" if j < J - 1 else "reset_b"))
                dve.tensor_tensor_scan(csum, resets[j], sig, 0.0, ALU.mult, ALU.add).then_inc(sem("csum_ready"), 1)
                dve.wait_ge(sem("csum_ready"), j + 1)
                dve.tensor_tensor(gprev, csum, sig, ALU.subtract).then_inc(sem("cprev_ready"), 1)
                dve.wait_ge(sem("cprev_ready"), j + 1)
                dve.tensor_scalar(sig, avec, col("k_a", j), omka[:, j:j + 1], ALU.mult, ALU.add)
                dve.drain()
                dve.tensor_tensor(k, k, sig, ALU.mult)
                if j == 0:
                    shift_tile(8)
                dve.wait_ge(sem("kk_norm"), 2 * j + 2)
                dve.tensor_scalar(tmp, tmp, 1e-12, None, ALU.max)
                dve.drain()
                dve.reciprocal(tmp, tmp)
                dve.drain()
                dve.tensor_tensor(kk, kk, tmp, ALU.mult)
                dve.wait_ge(sem("gexp_ready"), 3 * j + 3)
                dve.drain()
                dve.scalar_tensor_tensor(AR[:, j, :, 0:64], ch(kk), -1.0, ch(gprev), ALU.mult, ALU.mult)
                dve.tensor_tensor(avec, avec, kk, ALU.mult)
                dve.tensor_tensor(BK[:, j, :, 64:128], ch(k), ch(ginv), ALU.mult)
                dve.drain()
                dve.tensor_tensor(BK[:, j, :, 0:64], ch(avec), ch(ginv), ALU.mult)
                if j > 0:
                    shift_tile(7 + 3 * j)
                dve.tensor_tensor(AR[:, j, :, 64:128], ch(r), ch(gexp), ALU.mult)
                dve.tensor_tensor(r, r, k, ALU.mult)
                dve.tensor_copy(gcol[:, :, j:j + 1], ch(gexp)[:, :, 63:64]).then_inc(sem("elem_done"), 1)
                dve.drain()
                if j > 0:
                    shift_tile(8 + 3 * j)
            for v in (unit(12, 2), unit(15), unit(22)):
                m = dve.memset(v, 0.0)
            m.then_inc(*reach("bd_zero2"))
            dve.wait_ge(*reached("bd_zero"))
            dve.drain()
            dve.sem_inc(sem("Z_ready"), 1)
            heads = lambda m, n: m.rearrange("p (o x) -> p o x", o=1).to_broadcast((m.shape[0], n, m.shape[1]))
            dve.sem_inc(sem("PM_ready"), 2)

            def prepare_dve(n, par, h, first):
                c, q = n * 2 + h, 2 * par + h
                dve.wait_ge(sem("y_ps"), c + 1)
                for x in range(2):
                    dve.wait_ge(sem("pm_ps"), c * 2 + (x + 1))
                    dve.tensor_tensor(PM[q][:, 4 * x:4 * x + 4, :], banks[x][:, :].rearrange("p (h x) -> p h x", h=4),
                                      heads(pmask[:, :], 4), ALU.mult).then_inc(sem("PM_ready"), 1)
                if not first:
                    dve.wait_ge(sem("TS_ready"), n * 12 + (h - 1))
                dve.wait_ge(sem("L_ps"), c + 1)
                for x in range(2):
                    dve.tensor_tensor(TS[h][64 * x:64 * x + 64, 0, :, :], jx(LB[h][0:64, :])[:, :, 64 * x:64 * x + 64], heads(lmask[0:64, 0, :], J), ALU.mult)
                dve.drain()
                for x in range(2):
                    dve.tensor_tensor(TS[h][64 * x:64 * x + 64, 1, :, :], PM[q][0:64, x:HEADS:2, 0:64], heads(lmask1T[0:64, :], J), ALU.mult)
                dve.drain()
                v = TS[h].rearrange("p a j x -> p (a j) x")
                dve.tensor_tensor(v, v, heads(eye[:, :], 2 * J), ALU.add).then_inc(sem("TS_new"), 1)

            def pair_dve(dve, p, par, prep, state):
                n, np_ = p + 1, 1 - par
                if prep:
                    for h in range(2):
                        prepare_dve(n, np_, h, not state)
                for lv in range(6):
                    for gap in range(2):
                        if gap == 1:
                            dve.drain()
                        for h in range(2 if prep and lv else 0):
                            if gap == 0:
                                dve.wait_ge(sem("X_ps"), n * 10 + (2 * lv - 1 + h))
                                dve.tensor_tensor(Xst[h], jx(LB[h][:, 0:256]), heads(lmask[:, lv, :], J), ALU.mult).then_inc(sem("Xst_ready"), 1)
                            else:
                                dve.wait_ge(sem("D_ps"), n * 10 + (2 * lv - 1 + h))
                                a = 0 if lv < 5 else 256
                                v = TS[h].rearrange("p a j x -> p (a j x)")[:, a:512]
                                dve.tensor_tensor(v, v, banks[3 + h][:, a:512], ALU.add).then_inc(sem("TS_new"), 1)
                        if state and (lv, gap) in PIECES:
                            h, piece = PIECES[lv, gap]
                            c = p * 2 + h
                            if piece == 0:
                                dve.wait_ge(sem("Q_ps"), c + 5)
                                for x in range(2):
                                    m = dve.tensor_copy(Qst[64 * x:64 * x + 64, :, :], jx(banks[7][0:64, :])[:, :, 64 * x:64 * x + 64])
                                m.then_inc(sem("Q_ready"), 1)
                            elif piece == 2:
                                dve.drain()
                                dve.wait_ge(sem("M_ps"), c + 1)
                                diagonal = [(slice(64 * x, 64 * x + 64), slice(64 * x, 64 * x + 64)) for x in range(2)]
                                for r, x in diagonal:
                                    dve.tensor_tensor(Ztmp[r, :, :], Zbd[r, :, x], jx(banks[5][r, :])[:, :, x], ALU.add)
                                dve.drain()
                                for r, x in diagonal:
                                    g = gcol[r, ds(c, 1), :].rearrange("p o j -> p (o j)").rearrange("p (j o) -> p j o", o=1)
                                    m = dve.tensor_tensor(Zbd[r, :, x], Ztmp[r, :, :], g.to_broadcast((64, J, 64)), ALU.mult)
                                m.then_inc(sem("Z_ready"), 1)
                dve.drain()

            pairs(dve, pair_dve)
            dve.sem_inc(*reach("states_done"))
            act_y = unit(16, 4)
            Y3 = act_y.rearrange("p (g x) -> p g x", x=HD)
            bc = lambda v: v.rearrange("p (g o) -> p g o", o=1).to_broadcast((P, TT * HEADS, HD))

            dve.wait_ge(sem("Y_ready"), 2 + NC)
            dve.tensor_reduce(gstat[:, 0, :], Y3, AX_X, ALU.add)
            dve.drain()
            tsc(gstat[:, 0, :], gstat[:, 0, :], 1.0 / HD, None, ALU.mult)
            dve.tensor_tensor(Y3, Y3, bc(gstat[:, 0, :]), ALU.subtract).then_inc(*reach("gn_centred"))
            dve.wait_ge(sem("xg_loaded"), 16 * TAU)
            dve.tensor_copy(Rtab.rearrange("p (q c) -> p q c", q=PAIRS), q_(A["r8"], SC))
            dve.drain()
            dve.memset(Rtab.rearrange("p (q c) -> p q c", q=PAIRS)[:, :, 0:1], 0.0)
            dve.wait_ge(sem("e_evac"), 8)
            dve.wait_ge(sem("trig_loaded"), 16)
            z4 = [zst[0], zst[1], rot[0], rot[1]]
            cmul((E5[0], E5[1]), (trig[0], trig[1]), (E5[0], E5[1]), z4, conj=True)
            dve.wait_ge(*reached("gn_sq"))
            dve.tensor_reduce(gstat[:, 1, :], gtmp.rearrange("p (g x) -> p g x", x=HD), AX_X, ALU.add)
            dve.drain()
            dve.tensor_scalar(gstat[:, 1, :], gstat[:, 1, :], 1.0 / HD, 64e-5, ALU.mult, ALU.add).then_inc(*reach("gn_var"))
            for a in range(2):
                dve.tensor_tensor_scan(zst[a], Rtab, E5[a], 0.0, ALU.mult, ALU.add)
            dve.drain()
            tg1 = [v.rearrange("p (q c) -> p q c", q=PAIRS)[:, :, 0:SC - 1] for v in (*trig, *zst, *Sprev, *E5)]
            sh = [v.rearrange("p (q c) -> p q c", q=PAIRS) for v in Sprev]
            for o, c in enumerate((ALU.subtract, ALU.add)):
                dve.tensor_tensor(tg1[6], tg1[0], tg1[2 + o], ALU.mult)
                dve.tensor_tensor(tg1[7], tg1[1], tg1[3 - o], ALU.mult)
                dve.memset(sh[o][:, :, 0:1], 0.0)
                dve.drain()
                m = dve.tensor_tensor(sh[o][:, :, 1:SC], tg1[6], tg1[7], c)
                if o == 1:
                    m.then_inc(*reach("sprev_ready"))
                dve.drain()
            dve.wait_ge(*reached("rks_ready"))
            Vg = unit(4, 4).rearrange("p (g x) -> p g x", x=HD)
            tt(Vg, Vg, bc(rks.rearrange("p i h -> p (i h)")), ALU.mult)
            ln = lambda a: lnwb[:, 512 * a:512 * a + 512].rearrange("p (o c) -> p o c", o=1).to_broadcast((P, TT, 512))
            dve.wait_ge(sem("ln_loaded"), 32)
            tt(Vt, Vt, ln(1), ALU.add)
            dve.wait_ge(*reached("gn_std"))
            dve.reciprocal(gstat[:, 2, :], gstat[:, 1, :])
            dve.drain()
            tt(Y3, Y3, bc(gstat[:, 2, :]), ALU.mult)
            tt(Yt, Yt, ln(0), ALU.mult)
            tt(Yt, Yt, Vt, ALU.add)
            dve.tensor_tensor(Yt, Yt, Gt, ALU.mult).then_inc(*reach("gn_done"))
            dve.drain()
            for n in range(8):
                m4, h = n // 2, n % 2
                dve.wait_ge(sem("glu_evac"), n + 1)
                if n == 0:
                    dve.wait_ge(sem("zT_loaded"), 16)
                o = ymixT[:, 4 + m4, :].rearrange("p (c a) -> p a c", a=TAU)[:, 4 * h:4 * h + 4, :]
                dve.tensor_tensor(o, sglu[:, 512 * (n % 2):512 * (n % 2) + 512].rearrange("p (a c) -> p a c", a=4),
                                  zT[:, m4, 512 * h:512 * h + 512].rearrange("p (a c) -> p a c", a=4), ALU.mult).then_inc(sem("ymix_s5"), 1)
            dve.sem_inc(sem("mix_added"), 4)
            dve.wait_ge(sem("xr_loaded"), 16)

            def mix_dve(ii):
                for s in range(2):
                    for h in range(2):
                        dve.wait_ge(sem("mix_ps"), ii * 4 + (4 + 2 * s + h + 1))
                        v = Xr[:, ds(ii * 2 + s, 1), 512 * h:512 * h + 512].rearrange("p o d -> p (o d)")
                        dve.tensor_tensor(v, v, banks[2 * s + h][:, :], ALU.add).then_inc(sem("mix_added"), 1)

            mix_dve(0)
            norm_dve(dve, "norm_mem_w", hM, 8, 2, 2)
            with dve.Fori(0, TT // 2 - 1) as ii:
                mix_dve(ii + 1)
            norm_dve(dve, "norm_xattn_w", hB, 10, TT, 3)
            for i in range(2):
                for h in range(2):
                    dve.wait_ge(sem("v_ps"), 2 * i + h + 1)
                    dve.tensor_copy(vM[:, i, 512 * h:512 * h + 512], banks[2 * i + h][:, :]).then_inc(sem("vM_ready"), 1)
            dve.sem_inc(sem("p_ready"), 1)
            dve.sem_inc(sem("x_attn"), 4)

            def attend_dve(t, s):
                dve.wait_ge(sem("s_ps"), t + 1)
                for h in range(2):
                    dve.tensor_reduce(smx[s][:, 2 * h:2 * h + 2], banks[2 + h][:, :].rearrange("p (h m) -> p h m", h=2), AX_X, ALU.max)
                dve.drain()
                dve.tensor_scalar(smx[s], smx[s], -1.0 / 16.0, None, ALU.mult).then_inc(sem("smx_ready"), 1)
                dve.wait_ge(sem("exp_done"), t * 4 + 4)
                dve.reciprocal(ssum[s], ssum[s])
                dve.drain()
                dve.tensor_tensor(pr_, pr_, ssum[s].rearrange("p (h o) -> p h o", o=1).to_broadcast((P, XH, MEM)), ALU.mult).then_inc(sem("p_ready"), 1)
                for h in range(2):
                    dve.wait_ge(sem("oproj_ps"), t * 2 + (h + 1))
                    v = Xr[:, ds(t, 1), 512 * h:512 * h + 512].rearrange("p o d -> p (o d)")
                    dve.tensor_tensor(v, v, banks[4 + h][:, :], ALU.add).then_inc(sem("x_attn"), 1)

            with dve.Fori(0, TT // 2) as ii:
                for s in range(2):
                    attend_dve(ii * 2 + s, s)
            dve.sem_inc(sem("xn_stored0"), 16)
            dve.sem_inc(sem("xn_stored1"), 16)
            norm_dve(dve, "norm_moe_w", hB, 18, TT, 4)
            dve.wait_ge(*reached("logits_ps"))
            dve.wait_ge(*reached("router_consts"))
            b3 = lambda v, n: v.rearrange("p (o e) -> p o e", o=1).to_broadcast((P, TT, n))
            c3 = lambda v, n: v.rearrange("p (i o) -> p i o", o=1).to_broadcast((P, TT, n))
            tt(LG, banks[0][:, 0:288].rearrange("p (i e) -> p i e", i=TT), b3(brt, 36), ALU.add)
            l1 = LG[:, :, 0:NG]

            def red(o, a, op):
                dve.tensor_reduce(o, a, AX_X, op)
                dve.drain()

            def first_of_max(o, best, a, n, iob, t):
                red(best, a, ALU.max)
                tt(t, a, c3(best, n), ALU.is_equal)
                tsc(t, t, -2.0 * EPG, None, ALU.mult)
                tt(t, t, b3(iob, n), ALU.add)
                red(o, t, ALU.min)

            grp, m1, s1, i0, v0, i1, v1 = s8[0], s8[1], s8[2], s8[3], s8[4], s8[5], s8[7]
            first_of_max(grp, m1, l1, NG, io4b, e8[1][:, :, 0:NG])
            tsc(grp, grp, float(EPG), None, ALU.add)
            dve.tensor_tensor(e8[0][:, :, 0:NG], l1, c3(m1, NG), ALU.subtract).then_inc(*reach("l1_ready"))
            tt(e8[1][:, :, 0:NG], b3(io32[:, 0:NG], NG), c3(grp, NG), ALU.is_equal)
            tt(l2.rearrange("p i (g e) -> p i g e", g=NG), LG[:, :, NG:36].rearrange("p i (g e) -> p i g e", g=NG),
               e8[1][:, :, 0:NG].rearrange("p i (g o) -> p i g o", o=1).to_broadcast((P, TT, NG, EPG)), ALU.mult)
            red(e8[2], l2.rearrange("p i (g e) -> p i e g", g=NG), ALU.add)
            first_of_max(i0, v0, e8[2], EPG, io8b, e8[3])
            tt(e8[3], b3(io32[:, 0:EPG], EPG), c3(i0, EPG), ALU.is_equal)
            tsc(e8[3], e8[3], -3.0e38, None, ALU.mult)
            tt(e8[2], e8[2], e8[3], ALU.add)
            first_of_max(i1, v1, e8[2], EPG, io8b, e8[3])
            dve.tensor_tensor(s8[6], v1, v0, ALU.subtract).then_inc(*reach("dv_ready"))
            dve.drain()
            dve.wait_ge(*reached("exp_dv"))
            red(s1, e8[0][:, :, 0:NG], ALU.add)
            tsc(s8[8], s8[6], 1.0, None, ALU.add)
            tt(s8[8], s8[8], s1, ALU.mult)
            dve.reciprocal(gates[:, 0:8], s8[8])
            dve.drain()
            tt(gates[:, 8:16], gates[:, 0:8], s8[6], ALU.mult)
            tsc(grp, grp, float(EPG), None, ALU.mult)
            for a, i in enumerate((i0, i1)):
                tt(i, i, grp, ALU.add)
                tt(O2[a], b3(io32, NE), c3(i, NE), ALU.is_equal)
            tt(MS, O2[0], O2[1], ALU.add)
            dve.memset(MA[:, 0, :], 0.0)
            dve.drain()
            for i in range(1, TT):
                tt(MA[:, i, :], MA[:, i - 1, :], MS[:, i - 1, :], ALU.add)
            dve.tensor_tensor(c32[0], MA[:, TT - 1, :], MS[:, TT - 1, :], ALU.add).then_inc(*reach("marks_ready"))
            dve.wait_ge(*reached("ranks_ps"))
            tt(cmpb, banks[1][:, 256:288].rearrange("p (e o) -> p e o", o=1).to_broadcast((P, NE, 7)),
               ioM.rearrange("p (o m) -> p o m", o=1).to_broadcast((P, NE, 7)), ALU.is_gt)
            red(c32[1], cmpb, ALU.add)
            dve.tensor_tensor_scan(c32[2], ones[:, 0:NE], c32[1], 0.0, ALU.mult, ALU.add)
            dve.drain()
            tt(c32[3], c32[2], c32[1], ALU.subtract)
            dve.scalar_tensor_tensor(c32[4], c32[3], float(P), io128, ALU.mult, ALU.subtract)
            dve.drain()
            tsc(c32[4], c32[4], float(NE * P - P), None, ALU.add)
            tt(RK, banks[1][:, 0:256].rearrange("p (i e) -> p i e", i=TT), b3(io128, NE), ALU.add)
            tsc(RT, banks[1][:, 0:256].rearrange("p (i e) -> p i e", i=TT), float(P), None, ALU.is_ge)
            tt(RT, RT, b3(c32[4], NE), ALU.mult)
            tt(RK, RK, RT, ALU.add)
            for a in range(2):
                tt(RT, RK, O2[a], ALU.mult)
                red(s8[9 + a], RT, ALU.add)
                m = dve.tensor_copy(slots_i[:, 8 * a:8 * a + 8], s8[9 + a])
                if a == 0:
                    m.then_inc(*reach("slots_a"))
            tt(cmpo, c32[2].rearrange("p (o e) -> p o e", o=1).to_broadcast((P, OVER, NE)),
               ioO.rearrange("p (b o) -> p b o", o=1).to_broadcast((P, OVER, NE)), ALU.is_le)
            red(e8[4].rearrange("p i e -> p (i e)")[:, 0:OVER], cmpo, ALU.add)
            tsc(e8[4].rearrange("p i e -> p (i e)")[:, 0:OVER], e8[4].rearrange("p i e -> p (i e)")[:, 0:OVER], float(NE - 1), None, ALU.min)
            dve.tensor_copy(eid_i, e8[4].rearrange("p i e -> p (i e)")[:, 0:OVER])
            dve.tensor_copy(nover_i, c32[2][:, NE - 1:NE])
            dve.drain()
            dve.tensor_copy(eid_i[:, 0:1], eid_i[:, 0:1]).then_inc(*reach("slots_ready"))
            dve.drain()
            dve.sem_inc(sem("xbT_ready"), 2)
            dve.sem_inc(sem("hid_ready"), 1)
            dve.sem_inc(sem("y_evac1"), 1)
            gp = gainp.rearrange("p (k o) -> p k o", o=1)

            def tokens_dve(s, n, lead):
                dve.wait_ge(sem("up_ps"), n + lead)
                for q in range(2):
                    dve.wait_ge(sem("xT_ps"), n * 2 + (4 + q + 1))
                    dve.tensor_tensor(xbT[s][:, 4 * q:4 * q + 4, :], banks[q][:, :].rearrange("p (k t) -> p k t", k=4),
                                      gp[:, 4 * q:4 * q + 4, :].to_broadcast((P, 4, P)), ALU.mult).then_inc(sem("xbT_ready"), 1)

            def hidden_dve(n):
                dve.wait_ge(sem("sg_ready"), n + 2)
                dve.wait_ge(sem("up_ps"), n + 3)
                dve.wait_ge(sem("hidT_ps"), n + 1)
                dve.tensor_tensor(hid, sg, banks[3][:, :], ALU.mult).then_inc(sem("hid_ready"), 1)

            def down_dve(s, n, ns):
                dve.wait_ge(sem("dn_ps"), n * 2 + 6)
                dve.wait_ge(sem("y_stored0") if s == 0 else sem("y_stored1"), ns * 16 + 16)
                dve.tensor_copy(ysb[s][:, 512:1024], banks[6][:, :]).then_inc(sem("y_evac1"), 1)

            def experts_dve(dve, s, n, ns, last=False):
                hidden_dve(n)
                if not last:
                    tokens_dve(1 - s, n + 1, 1)
                down_dve(s, n, ns)

            tokens_dve(0, 0, 1)
            blocks(dve, experts_dve)
            n_over = dve.value_load(nover_i[0:1, :], min_val=0, max_val=OVER)
            with dve.Fori(0, OVER) as o:
                with dve.If(o < n_over):
                    tokens_dve(0, o + NE, 2)
                    hidden_dve(o + NE)
                    down_dve(0, o + NE, o + NE // 2)
                dve.nop()
            def add_rows(i):
                dve.wait_ge(sem(f"yg_loaded{i}"), 32)
                for a in range(2):
                    dve.scalar_tensor_tensor(Xr[:, i, :], yg[i][a], gates[:, 8 * a + i:8 * a + i + 1], Xr[:, i, :], ALU.mult, ALU.add).then_inc(sem("y_added"), 1)
                    dve.drain()

            def final_scale(half):
                r = slice(4 * half, 4 * half + 4)
                dve.wait_ge(sem("ss_ready"), 26 + 4 * half + 4)
                dve.tensor_scalar(rstd[:, r], ss[:, r], 1.0 / D, EPS, ALU.mult, ALU.add).then_inc(sem("ms_ready"), 1)
                if half == 0:
                    add_rows(5)
                dve.wait_ge(sem("rms_ready"), 5 + half)
                dve.reciprocal(rstd[:, r], rstd[:, r])
                dve.drain()
                for i in range(4 * half, 4 * half + 4):
                    dve.scalar_tensor_tensor(ost[i], Xr[:, i, :], rstd[:, i:i + 1], wfin, ALU.mult, ALU.mult).then_inc(sem("out_ready"), 1)

            for i in range(5):
                add_rows(i)
            dve.wait_ge(sem("wfin_loaded"), 16)
            final_scale(0)
            add_rows(6)
            add_rows(7)
            final_scale(1)


def kernel(**inputs):
    import concourse.bacc as bacc
    from concourse.bass_utils import run_bass_kernel_spmd

    nc = bacc.Bacc("TRN2", target_bir_lowering=False, num_devices=1)
    arrays, views = {}, {}
    for name, value in inputs.items():
        a = np.ascontiguousarray(value)
        arrays["in_" + name] = a
        views[name] = nc.dram_tensor("in_" + name, a.shape, mybir.dt.from_np(a.dtype), kind="ExternalInput").ap()
    out = nc.dram_tensor("out_0_dram", (1, T, D), F32, kind="ExternalOutput").ap()
    program(nc, views, out)
    result = run_bass_kernel_spmd(nc, [arrays], core_ids=[0])
    return result.results[0]["out_0_dram"]
```
